# Optimizing a Trainium2 kernel written in Bass

```python
import math
import jax, jax.numpy as jnp
from jax import lax
import numpy as np

D_MODEL = 2048
BATCH = 1
SEQ = 512
DEPTH = 1
DEC_BATCH = 8
DEC_SEQ = 1
PAST_LEN = 4096
PAGE_SIZE = 128

D_MIX = D_MODEL
LRU_WIDTH = D_MIX // 2
LRU_HEADS = 8
LRU_BLOCK = LRU_WIDTH // LRU_HEADS
LRU_C = 8.0
CONV_W = 4
GDN_HEADS = 8
GDN_DK = 128
GDN_DV = (D_MIX - LRU_WIDTH) // GDN_HEADS
GDN_QK_WIDTH = GDN_HEADS * GDN_DK
GDN_V_WIDTH = GDN_HEADS * GDN_DV
GDN_CONV_DIM = 2 * GDN_QK_WIDTH + GDN_V_WIDTH
GDN_CHUNK = 64
IN_COLS = 2 * LRU_WIDTH + GDN_CONV_DIM + GDN_V_WIDTH + 2 * GDN_HEADS
N_MEM = 256
XA_HEADS = 4
XA_HEAD_DIM = D_MODEL // XA_HEADS
XA_WIDTH = XA_HEADS * XA_HEAD_DIM
D_FF = -(-8 * D_MODEL // (3 * 256)) * 256
EPS = 1e-6

kernel_name = 'hymba_rglru_gdn_memxattn_decoder_step'

F32 = jnp.float32

def rmsnorm(x, w):
    x32 = x.astype(F32)
    y = x32 * lax.rsqrt(jnp.mean(x32 * x32, axis=-1, keepdims=True) + EPS)
    return (y * w.astype(F32)).astype(x.dtype)

def l2norm(x):
    return x * lax.rsqrt(jnp.sum(x * x, axis=-1, keepdims=True) + EPS)

def causal_conv(x, buf, w):
    L = x.shape[1]
    xp = jnp.concatenate([buf.astype(x.dtype), x], axis=1)
    y = xp[:, 0:L] * w[0]
    for j in range(1, CONV_W):
        y = y + xp[:, j:j + L] * w[j]
    return y, xp[:, L:]

def _lin_combine(c1, c2):
    a1, b1 = c1
    a2, b2 = c2
    return a1 * a2, a2 * b1 + b2

def rg_lru(x, h0, gx_w, gx_b, ga_w, ga_b, lam):
    B, L, W = x.shape
    x32 = x.astype(F32)
    xb = x32.reshape(B, L, LRU_HEADS, LRU_BLOCK)
    gate_x = jax.nn.sigmoid(jnp.einsum('blhi,hij->blhj', xb, gx_w.astype(F32)).reshape(B, L, W) + gx_b.astype(F32))
    gate_a = jax.nn.sigmoid(jnp.einsum('blhi,hij->blhj', xb, ga_w.astype(F32)).reshape(B, L, W) + ga_b.astype(F32))
    log_a = -LRU_C * gate_a * jax.nn.softplus(-lam.astype(F32))
    a = jnp.exp(log_a)
    b = x32 * gate_x * jnp.sqrt(-jnp.expm1(2.0 * log_a))
    b = b.at[:, 0].add(a[:, 0] * h0.astype(F32))
    _, h = lax.associative_scan(_lin_combine, (a, b), axis=1)
    return h.astype(x.dtype), h[:, -1].astype(x.dtype)

def _to_chunks(t, n, C, pad):
    t = jnp.pad(t, [(0, 0), (0, pad)] + [(0, 0)] * (t.ndim - 2))
    t = t.reshape((t.shape[0], n, C) + t.shape[2:])
    perm = (1, 0, 3, 2) + tuple(range(4, t.ndim))
    return t.transpose(perm)

def gated_delta_rule(q, k, v, g, beta, S0):
    B, L, H, _ = q.shape
    DV = v.shape[-1]
    C = GDN_CHUNK if L >= GDN_CHUNK else L
    n = -(-L // C)
    pad = n * C - L
    q, k, v, g, beta = [_to_chunks(t.astype(F32), n, C, pad) for t in (q, k, v, g, beta)]
    gc = jnp.cumsum(g, axis=-1)
    idx = jnp.arange(C)
    incl = idx[:, None] >= idx[None, :]
    strict = idx[:, None] > idx[None, :]
    decay = jnp.exp(jnp.where(incl, gc[..., :, None] - gc[..., None, :], -jnp.inf))
    kb = k * beta[..., None]
    A = jnp.where(strict, jnp.einsum('nbhid,nbhjd->nbhij', kb, k) * decay, 0.0)
    T = A + jnp.eye(C, dtype=F32)
    rhs = jnp.concatenate([v * beta[..., None], kb * jnp.exp(gc)[..., None]], axis=-1)
    sol = lax.linalg.triangular_solve(T, rhs, left_side=True, lower=True, unit_diagonal=True)
    u, w = sol[..., :DV], sol[..., DV:]
    qk = jnp.where(incl, jnp.einsum('nbhid,nbhjd->nbhij', q, k) * decay, 0.0)

    def step(S, inp):
        q_c, k_c, u_c, w_c, g_c, qk_c = inp
        v_new = u_c - jnp.einsum('bhck,bhkv->bhcv', w_c, S)
        o = jnp.einsum('bhck,bhkv->bhcv', q_c * jnp.exp(g_c)[..., None], S) + jnp.einsum('bhij,bhjv->bhiv', qk_c, v_new)
        g_last = g_c[..., -1:]
        S = S * jnp.exp(g_last)[..., None] + jnp.einsum('bhck,bhcv->bhkv', k_c * jnp.exp(g_last - g_c)[..., None], v_new)
        return S, o

    S, o = lax.scan(step, S0.astype(F32), (q, k, u, w, gc, qk))
    o = o.transpose(1, 0, 3, 2, 4).reshape(B, n * C, H, DV)[:, :L]
    return o, S

def mixer(xn, lru_conv, lru_h, gdn_conv, gdn_S, p):
    B, L, _ = xn.shape
    proj = xn @ p['w_in']
    o1 = LRU_WIDTH
    o2 = 2 * LRU_WIDTH
    o3 = o2 + GDN_CONV_DIM
    o4 = o3 + GDN_V_WIDTH
    o5 = o4 + GDN_HEADS
    lru_x, lru_y, qkv = proj[..., :o1], proj[..., o1:o2], proj[..., o2:o3]
    z, b_raw, a_raw = proj[..., o3:o4], proj[..., o4:o5], proj[..., o5:]
    lx, lru_conv = causal_conv(lru_x, lru_conv, p['lru_conv_w'])
    lx = lx + p['lru_conv_b']
    lh, lru_h = rg_lru(lx, lru_h, p['lru_gate_x_w'], p['lru_gate_x_b'], p['lru_gate_a_w'], p['lru_gate_a_b'], p['lru_lambda'])
    lru_out = lh * jax.nn.gelu(lru_y)
    qkv, gdn_conv = causal_conv(qkv, gdn_conv, p['gdn_conv_w'])
    qkv = jax.nn.silu(qkv).astype(F32)
    q = l2norm(qkv[..., :GDN_QK_WIDTH].reshape(B, L, GDN_HEADS, GDN_DK)) * (GDN_DK ** -0.5)
    k = l2norm(qkv[..., GDN_QK_WIDTH:2 * GDN_QK_WIDTH].reshape(B, L, GDN_HEADS, GDN_DK))
    v = qkv[..., 2 * GDN_QK_WIDTH:].reshape(B, L, GDN_HEADS, GDN_DV)
    beta = jax.nn.sigmoid(b_raw.astype(F32))
    g = -jnp.exp(p['gdn_A_log'].astype(F32)) * jax.nn.softplus(a_raw.astype(F32) + p['gdn_dt_bias'].astype(F32))
    o, S = gated_delta_rule(q, k, v, g, beta, gdn_S)
    o = o * lax.rsqrt(jnp.mean(o * o, axis=-1, keepdims=True) + EPS) * p['gdn_norm_w'].astype(F32)
    o = o * jax.nn.silu(z.astype(F32)).reshape(B, L, GDN_HEADS, GDN_DV)
    mixed = jnp.concatenate([lru_out, o.reshape(B, L, GDN_V_WIDTH).astype(xn.dtype)], axis=-1)
    return mixed @ p['w_out'], lru_conv, lru_h, gdn_conv, S.astype(xn.dtype)

def memory_kv(mem, p):
    B, M, _ = mem.shape
    mn = rmsnorm(mem, p['norm_mem'])
    k = (mn @ p['xa_wk']).reshape(B, M, XA_HEADS, XA_HEAD_DIM)
    v = (mn @ p['xa_wv']).reshape(B, M, XA_HEADS, XA_HEAD_DIM)
    return k, v

def cross_attn(xn, mk, mv, p):
    B, L, _ = xn.shape
    q = (xn @ p['xa_wq']).reshape(B, L, XA_HEADS, XA_HEAD_DIM)
    s = jnp.einsum('blhd,bmhd->bhlm', q.astype(F32), mk.astype(F32)) * (XA_HEAD_DIM ** -0.5)
    pr = jax.nn.softmax(s, axis=-1)
    o = jnp.einsum('bhlm,bmhd->blhd', pr.astype(mv.dtype), mv).reshape(B, L, XA_WIDTH)
    return o @ p['xa_wo']

def swiglu(xn, p):
    return (jax.nn.silu(xn @ p['ffn_w_gate']) * (xn @ p['ffn_w_up'])) @ p['ffn_w_down']

def decoder_layer(x, lru_conv, lru_h, gdn_conv, gdn_S, mk, mv, p):
    m, lru_conv, lru_h, gdn_conv, gdn_S = mixer(rmsnorm(x, p['norm_mix_pre']), lru_conv, lru_h, gdn_conv, gdn_S, p)
    x = x + rmsnorm(m, p['norm_mix_post'])
    c = cross_attn(rmsnorm(x, p['norm_xa_pre']), mk, mv, p)
    x = x + rmsnorm(c, p['norm_xa_post'])
    f = swiglu(rmsnorm(x, p['norm_ffn_pre']), p)
    x = x + rmsnorm(f, p['norm_ffn_post'])
    return x, lru_conv, lru_h, gdn_conv, gdn_S

def setup_inputs(seed: int = 0) -> dict:
    key = jax.random.key(seed)
    ks = iter(jax.random.split(key, 48))

    def nrm(shape, scale):
        return scale * jax.random.normal(next(ks), shape, F32)

    def gain(shape):
        return 1.0 + 0.05 * jax.random.normal(next(ks), shape, F32)

    Ld = DEPTH
    a_c = jax.random.uniform(next(ks), (Ld, LRU_WIDTH), F32, minval=0.9, maxval=0.999)
    s = a_c ** (1.0 / LRU_C)
    lru_lambda = jnp.log(s) - jnp.log1p(-s)
    gdn_A_log = jnp.log(jax.random.uniform(next(ks), (Ld, GDN_HEADS), F32, minval=1.0, maxval=16.0))
    dt = jnp.exp(jax.random.uniform(next(ks), (Ld, GDN_HEADS), F32, minval=math.log(1e-3), maxval=math.log(1e-1)))
    gdn_dt_bias = dt + jnp.log(-jnp.expm1(-dt))
    return {
        'x_prompt': nrm((BATCH, SEQ, D_MODEL), 1.0),
        'x_sample': nrm((DEC_BATCH, DEC_SEQ, D_MODEL), 1.0),
        'mem_prompt': nrm((BATCH, N_MEM, D_MODEL), 1.0),
        'state_lru_conv': nrm((Ld, DEC_BATCH, CONV_W - 1, LRU_WIDTH), 1.0),
        'state_lru_h': nrm((Ld, DEC_BATCH, LRU_WIDTH), 1.0),
        'state_gdn_conv': nrm((Ld, DEC_BATCH, CONV_W - 1, GDN_CONV_DIM), 1.0),
        'state_gdn_S': nrm((Ld, DEC_BATCH, GDN_HEADS, GDN_DK, GDN_DV), 0.1),
        'cache_mem_k': nrm((Ld, DEC_BATCH, N_MEM, XA_HEADS, XA_HEAD_DIM), 1.0),
        'cache_mem_v': nrm((Ld, DEC_BATCH, N_MEM, XA_HEADS, XA_HEAD_DIM), 1.0),
        'norm_mix_pre': gain((Ld, D_MODEL)),
        'norm_mix_post': gain((Ld, D_MODEL)),
        'w_in': nrm((Ld, D_MODEL, IN_COLS), D_MODEL ** -0.5),
        'lru_conv_w': nrm((Ld, CONV_W, LRU_WIDTH), CONV_W ** -0.5),
        'lru_conv_b': nrm((Ld, LRU_WIDTH), 0.01),
        'lru_gate_x_w': nrm((Ld, LRU_HEADS, LRU_BLOCK, LRU_BLOCK), LRU_BLOCK ** -0.5),
        'lru_gate_x_b': nrm((Ld, LRU_WIDTH), 0.01),
        'lru_gate_a_w': nrm((Ld, LRU_HEADS, LRU_BLOCK, LRU_BLOCK), LRU_BLOCK ** -0.5),
        'lru_gate_a_b': nrm((Ld, LRU_WIDTH), 0.01),
        'lru_lambda': lru_lambda,
        'gdn_conv_w': nrm((Ld, CONV_W, GDN_CONV_DIM), CONV_W ** -0.5),
        'gdn_A_log': gdn_A_log,
        'gdn_dt_bias': gdn_dt_bias,
        'gdn_norm_w': gain((Ld, GDN_DV)),
        'w_out': nrm((Ld, D_MIX, D_MODEL), D_MIX ** -0.5),
        'norm_xa_pre': gain((Ld, D_MODEL)),
        'norm_xa_post': gain((Ld, D_MODEL)),
        'norm_mem': gain((Ld, D_MODEL)),
        'xa_wq': nrm((Ld, D_MODEL, XA_WIDTH), D_MODEL ** -0.5),
        'xa_wk': nrm((Ld, D_MODEL, XA_WIDTH), D_MODEL ** -0.5),
        'xa_wv': nrm((Ld, D_MODEL, XA_WIDTH), D_MODEL ** -0.5),
        'xa_wo': nrm((Ld, XA_WIDTH, D_MODEL), XA_WIDTH ** -0.5),
        'norm_ffn_pre': gain((Ld, D_MODEL)),
        'norm_ffn_post': gain((Ld, D_MODEL)),
        'ffn_w_gate': nrm((Ld, D_MODEL, D_FF), D_MODEL ** -0.5),
        'ffn_w_up': nrm((Ld, D_MODEL, D_FF), D_MODEL ** -0.5),
        'ffn_w_down': nrm((Ld, D_FF, D_MODEL), D_FF ** -0.5),
    }

def reference(x_prompt, x_sample, mem_prompt, state_lru_conv, state_lru_h, state_gdn_conv, state_gdn_S,
              cache_mem_k, cache_mem_v, norm_mix_pre, norm_mix_post, w_in, lru_conv_w, lru_conv_b,
              lru_gate_x_w, lru_gate_x_b, lru_gate_a_w, lru_gate_a_b, lru_lambda, gdn_conv_w, gdn_A_log,
              gdn_dt_bias, gdn_norm_w, w_out, norm_xa_pre, norm_xa_post, norm_mem, xa_wq, xa_wk, xa_wv,
              xa_wo, norm_ffn_pre, norm_ffn_post, ffn_w_gate, ffn_w_up, ffn_w_down):
    weights = {
        'norm_mix_pre': norm_mix_pre, 'norm_mix_post': norm_mix_post, 'w_in': w_in,
        'lru_conv_w': lru_conv_w, 'lru_conv_b': lru_conv_b,
        'lru_gate_x_w': lru_gate_x_w, 'lru_gate_x_b': lru_gate_x_b,
        'lru_gate_a_w': lru_gate_a_w, 'lru_gate_a_b': lru_gate_a_b, 'lru_lambda': lru_lambda,
        'gdn_conv_w': gdn_conv_w, 'gdn_A_log': gdn_A_log, 'gdn_dt_bias': gdn_dt_bias,
        'gdn_norm_w': gdn_norm_w, 'w_out': w_out,
        'norm_xa_pre': norm_xa_pre, 'norm_xa_post': norm_xa_post, 'norm_mem': norm_mem,
        'xa_wq': xa_wq, 'xa_wk': xa_wk, 'xa_wv': xa_wv, 'xa_wo': xa_wo,
        'norm_ffn_pre': norm_ffn_pre, 'norm_ffn_post': norm_ffn_post,
        'ffn_w_gate': ffn_w_gate, 'ffn_w_up': ffn_w_up, 'ffn_w_down': ffn_w_down,
    }
    dt = x_prompt.dtype
    bp = x_prompt.shape[0]
    zero_lc = jnp.zeros((bp, CONV_W - 1, LRU_WIDTH), dt)
    zero_lh = jnp.zeros((bp, LRU_WIDTH), dt)
    zero_gc = jnp.zeros((bp, CONV_W - 1, GDN_CONV_DIM), dt)
    zero_gs = jnp.zeros((bp, GDN_HEADS, GDN_DK, GDN_DV), dt)
    xp = x_prompt
    xs = x_sample
    p_lc, p_lh, p_gc, p_gs, p_mk, p_mv = [], [], [], [], [], []
    s_lc, s_lh, s_gc, s_gs = [], [], [], []
    for l in range(DEPTH):
        p = {name: w[l] for name, w in weights.items()}
        mk, mv = memory_kv(mem_prompt, p)
        xp, lc, lh, gc, gs = decoder_layer(xp, zero_lc, zero_lh, zero_gc, zero_gs, mk, mv, p)
        p_lc.append(lc); p_lh.append(lh); p_gc.append(gc); p_gs.append(gs); p_mk.append(mk); p_mv.append(mv)
        xs, lc, lh, gc, gs = decoder_layer(xs, state_lru_conv[l], state_lru_h[l], state_gdn_conv[l], state_gdn_S[l],
                                           cache_mem_k[l], cache_mem_v[l], p)
        s_lc.append(lc); s_lh.append(lh); s_gc.append(gc); s_gs.append(gs)
    return (xp, xs,
            jnp.stack(p_lc), jnp.stack(p_lh), jnp.stack(p_gc), jnp.stack(p_gs), jnp.stack(p_mk), jnp.stack(p_mv),
            jnp.stack(s_lc), jnp.stack(s_lh), jnp.stack(s_gc), jnp.stack(s_gs))


_drawn_inputs = setup_inputs


def setup_inputs(seed=0):
    import zlib

    import numpy as np

    out = dict(_drawn_inputs(seed))
    spreads = {}
    factors = {'lru_gate_x_b': 8.0, 'lru_gate_a_b': 24.925}
    for name, (base, spread) in spreads.items():
        noise = np.random.default_rng([zlib.crc32(name.encode()), seed]).standard_normal(out[name].shape)
        drawn = base * np.exp(spread * noise) if base else spread * noise
        out[name] = __import__('jax').numpy.asarray(drawn.astype(out[name].dtype))
    for name, factor in factors.items():
        out[name] = (out[name] * factor).astype(out[name].dtype)
    return out
```

```python
from contextlib import ExitStack

import concourse.bass as bass
from concourse import mybir
from concourse.alu_op_type import AluOpType as ALU

ACT = mybir.ActivationFunctionType
AX_X = mybir.AxisListType.X
F32 = mybir.dt.float32
F32R = mybir.dt.float32r
P = 128
EPS = 1e-6
KS = 4
COLS = 256
RAW = 4
SPLIT = 2


class Gemm:

    def __init__(self, name, sources, iters, blocks, slabs, chunks, high, low, memory=False):
        self.name, self.sources, self.iters, self.blocks, self.slabs = name, sources, iters, blocks, slabs
        self.chunks, self.high, self.low, self.memory = chunks, high, low, memory

    def slab(self, it, jj):
        return it * (self.blocks * self.slabs) + (self.slab0 + jj)

    def block(self, it, j):
        return it * self.blocks + (self.block0 + j)

    def loads(self, it, jj):
        return it * (self.blocks * self.slabs // RAW) + ((self.slab0 + jj) // RAW + 1)

    def acc(self, j):
        return (self.block0 + j) % 2


def loop(engine, first, end, body):
    if end - first == 1:
        body(first)
    elif end > first:
        with engine.Fori(first, end) as i:
            body(i)


def build(nc, i, o):
    D = i["w_out"].shape[2]
    SEQ = i["x_prompt"].shape[1]
    B = i["x_sample"].shape[0]
    T = SEQ + B
    HALF = T // 2
    NC = D // P
    W = i["lru_lambda"].shape[1]
    LC = W // P
    H = i["gdn_A_log"].shape[1]
    QKV = i["gdn_conv_w"].shape[2]
    GC = QKV // P
    CC = LC + GC
    M = i["mem_prompt"].shape[1]
    MT = M // P
    TT = SEQ // P
    FF = i["ffn_w_up"].shape[2] // P
    TAPS = i["lru_conv_w"].shape[1]
    PADDED = TAPS - 1 + SEQ + TAPS * B
    CONVED = PADDED - TAPS + 1
    S0 = TAPS - 1 + SEQ
    EDGE = TAPS - 1 + B
    assert D % 1024 == 0 and T % 4 == 0 and HALF <= 512 and M == COLS and H == LC == TT * 2

    norm_names = ["norm_mix_pre", "norm_mix_post", "norm_xa_pre", "norm_xa_post", "norm_mem", "norm_ffn_pre", "norm_ffn_post"]
    NORM = {n: k * NC for k, n in enumerate(norm_names)}
    CONV0 = len(norm_names) * NC
    MISC0 = CONV0 + TAPS * CC
    misc_names = ["lru_conv_b", "lru_gate_x_b", "lru_gate_a_b", "lru_lambda"]
    MISC = {n: MISC0 + k * LC for k, n in enumerate(misc_names)}
    MISC["gdn_norm_w"] = MISC0 + len(misc_names) * LC
    NPAR = MISC["gdn_norm_w"] + 1

    with ExitStack() as ctx:
        def sb(name, shape, dt=F32):
            return ctx.enter_context(nc.sbuf_tensor(name, shape, dt))

        sems = {}

        NB = B * H // 4
        XT = SEQ // P * 4 + 1
        SEQUENCES = {
            "scalar": [("sp_exp", 2), ("beta", 1), ("gates", LC), ("lru_tanh", 1), ("lru_sqrt", 1), ("gc_exps", 3),
                       ("o_squares", 1), ("s_bg_wide", 1), ("o_root", 1), ("s_root", 1), ("mixed_high", 4), ("x_turns_taken", XT),
                       ("k_t", NC // 2), ("qs_rows", 4), ("s_exp", 1), ("os_rows", 1), ("s_o_high", 1), ("y_copied", XT + 3)],
            "vector": [("edge_copied", CC // 4), ("sp_abs", 1), ("lru_rate", 1), ("gdn_gate", 1), ("log_a", 1), ("lru_scanned", 1),
                       ("normed", 2 * H), ("gc_ready", 1), ("gdn_small", 1), ("S_clear", 1), ("s_cols", 4), ("s_wide", 1),
                       ("o_ms", 1), ("s_products", 1), ("o_normed", H), ("o_done", H), ("s_new", 1), ("s_o_squares", 1),
                       ("s_rows", 1), ("s_var", 1), ("s_o_done", 1), ("h_rows", 2), ("mixed_low", 4), ("s_max", 1),
                       ("s_probs", 1), ("s_spread", 1), ("s_o_low", 1)],
            "tensor": [("small_turned", 4), ("edge_turned", CC // 4), ("bg_turned", 1), ("gates_ready", LC), ("l2_summed", 2 * H),
                       ("gc_summed", 1), ("s_wide_ready", 1), ("s_qk_ready", 1), ("o_turned", H), ("s_wS", 1), ("s_rows_ready", 1),
                       ("s_o_summed", 1), ("s_outer", NB), ("h_turned", 2), ("x_turned", XT), ("k_t_turned", NC // 2),
                       ("qs_turned", 4), ("s_turned", 1), ("s_probs_turned", 1), ("s_valued", B * MT), ("os_turned", 1),
                       ("y_turned", XT + 3)],
            "pool": [("gated_x", 1), ("lru_out", 1), ("s_decayed", 1), ("eye_b", 2)],
        }
        IN_SEQUENCE = {n: (f"{e}_steps", sum(c for _, c in steps[:k]))
                       for e, steps in SEQUENCES.items() for k, (n, _) in enumerate(steps)}

        def after(name, count):
            return sem(name), IN_SEQUENCE[name][1] + count

        def sem(name):
            name = IN_SEQUENCE.get(name, (name, 0))[0]
            if name not in sems:
                sems[name] = ctx.enter_context(nc.semaphore(name))
            return sems[name]

        ident = sb("ident", [P, P])
        ones = sb("ones", [P, P])
        par = sb("par", [P, NPAR])
        small = sb("small", [P, 4, 8])
        eps_col = sb("eps_col", [P, 1])
        ssq, ms, root, rstd_rows = (small[:, k] for k in range(4))
        row_groups = [(0, MT), (MT, MT + TT), (MT + TT, MT + TT + 1)]
        CH = NC * T * 4
        CONV = (nc.sbuf_base + 31) // 32 * 32
        CONVED0 = CONV + (2 * PADDED * 4 + 31) // 32 * 32
        STATE0 = CONVED0 + (CONVED * 4 + 31) // 32 * 32
        HZERO0 = (STATE0 + 4 * CC * B * (TAPS - 1) + 31) // 32 * 32
        EDGE0 = (HZERO0 + 4 * LC * B + 31) // 32 * 32
        arena0 = (EDGE0 + 4 * CC * EDGE + 31) // 32 * 32
        XH, XL, H0, H1, M0, W0 = (arena0 + k * CH for k in range(6))
        SLAB = KS * COLS * 4

        def at(name, shape, dt, offset):
            return nc.alloc_sbuf_tensor_at(name, shape, dt, offset=offset)

        xpad = at("xpad", [P, 2, PADDED], F32, CONV)
        conved = at("conved", [P, CONVED], F32, CONVED0)
        conv_state = at("conv_state", [P, CC, B * (TAPS - 1)], F32, STATE0)
        h0 = at("h0", [P, LC, B], F32, HZERO0)
        edge = at("edge", [P, CC, EDGE], F32, EDGE0)
        w_raw = at("w_raw", [P, RAW, KS, COLS], F32, W0)
        w_high = at("w_high", [P, SPLIT, KS, COLS], F32R, W0 + RAW * SLAB)
        w_low = at("w_low", [P, SPLIT, KS, COLS], F32R, W0 + (RAW + SPLIT) * SLAB)
        x_high = at("x_high", [P, NC, T], F32R, XH)
        x_low = at("x_low", [P, NC, T], F32R, XL)
        mem_high = at("mem_high", [P, NC, M], F32R, H0)
        mem_low = at("mem_low", [P, NC, M], F32R, H0 + NC * M * 4)
        x_rows = at("x_rows", [P, TT, D], F32, H1)
        mem_rows = at("mem_rows", [P, MT, D], F32, M0)
        xs_rows = at("xs_rows", [P, D], F32, M0)
        kv_out = at("kv_out", [P, 2, MT, COLS], F32, M0 + D * 4)
        norm_mem_row = at("norm_mem_row", [P, D], F32, M0 + 2 * D * 4)
        norm_x_row = at("norm_x_row", [P, D], F32, M0 + 3 * D * 4)
        state_rows = at("state_rows", [P, CC * P], F32, XL)
        h0_rows = at("h0_rows", [P, W], F32, XL + CC * P * 4)
        par_rows = at("par_rows", [P, 3, P], F32, XL + CC * P * 4 + W * 4)
        lx = at("lx", [P, LC * T], F32, M0)
        gy = at("gy", [P, LC * T], F32, M0 + CH // 2)
        qkv = at("qkv", [P, GC * T], F32, H0)
        z = at("z", [P, H * T], F32, H0 + GC * T * 4)
        edge_rows = at("edge_rows", [P, CC * P], F32, XH)
        HT = H * T * 4
        lru_a = at("lru_a", [P, LC, T], F32, XH + CC * P * 4)
        lru_w = at("lru_w", [P, 2, LC, P], F32, XH + CC * P * 4)
        gate_a = at("gate_a", [P, LC, T], F32, XL)
        gate_x = at("gate_x", [P, LC, T], F32, XL + HT)
        HG = H // 2
        GT = HG * P * 4
        top = [XH]

        def more(name, shape, dt=F32):
            t = at(name, shape, dt, top[0])
            size = 4
            for n in shape[1:]:
                size *= n
            top[0] += (size + 31) // 32 * 32
            return t

        keys = [more(f"keys{g}", [P, HG, P]) for g in range(2)]
        values = [more(f"values{g}", [P, HG, P]) for g in range(2)]
        grow = [more(f"grow{g}", [P, HG, P]) for g in range(2)]
        inner = [more(f"inner{g}", [P, HG, P]) for g in range(2)]
        qk = [more(f"qk{g}", [P, HG, P]) for g in range(2)]
        kbg = [more(f"kbg{g}", [P, HG, P]) for g in range(2)]
        kdec = [more(f"kdec{g}", [P, HG, P]) for g in range(2)]
        vb = [more(f"vb{g}", [P, HG, P]) for g in range(2)]
        inv = [more(f"inv{g}", [P, HG, P]) for g in range(2)]
        inv_t = [more(f"inv_t{g}", [P, HG, P]) for g in range(2)]
        half_t = [more(f"half_t{g}", [P, HG, P]) for g in range(2)]
        S = [more(f"S{g}", [P, HG, P]) for g in range(2)]
        LEVELS = 7
        blocks_mask = more("blocks_mask", [P, LEVELS, P])
        upper = more("upper", [P, P])
        lower = more("lower", [P, P])
        squares = more("squares", [P, 2, T])
        l2_root = more("l2_root", [P, 2, T])
        assert top[0] <= XL + CH
        top[0] = CONV
        bg_rows = more("bg_rows", [P, T])
        bg = more("bg", [P, TT + 1, 40])
        SPW = LC + (TT + 1) * H
        sp = [more(f"softplus{k}", [P, SPW]) for k in range(6)]
        row_par = more("row_par", [P, 2, H])
        beta = more("beta", [P, (TT + 1) * H])
        gate = more("gate", [P, (TT + 1) * H])
        gc = more("gc", [P, TT * H])
        egc = more("egc", [P, TT * H])
        begc = more("begc", [P, TT * H])
        dgc = more("dgc", [P, TT * H])
        glast = more("glast", [P, TT * H])
        assert top[0] <= HZERO0
        BH = B * H
        s_S = at("s_S", [P, BH, P], F32, H0)
        top[0] = XH
        s_q, s_k, s_v, s_z = (more(n, [P, BH]) for n in ("s_q", "s_k", "s_v", "s_z"))
        s_bg = more("s_bg", [P, 2, BH])
        s_wide = more("s_wide", [P, 2, BH])
        s_wq = more("s_wq", [P, BH, 2])
        s_qk = more("s_qk", [P, BH])
        s_new = more("s_new", [P, BH])
        s_o = more("s_o", [P, BH])
        s_t = more("s_t", [P, BH])
        s_rows = more("s_rows", [P, 2, P])
        SD = 16
        s_diag = [more(f"s_diag{k}", [P, SD, P]) for k in range(2)]
        o_squares = more("o_squares", [P, TT * H, P])
        o_ms = more("o_ms", [P, TT * H])
        o_root = more("o_root", [P, TT * H])
        h_rows = more("h_rows", [P, LC * P])
        assert top[0] <= XL + CH
        branch = at("branch", [P, NC, T], F32, M0)
        top[0] = CONV
        ssum = more("ssum", [P, T])
        sq = more("sq", [P, 2, T])
        xw = more("xw", [P, 2, T])
        assert top[0] <= arena0
        xt = at("xt", [P, NC, T], F32, H0)
        x_rows2 = at("x_rows2", [P, TT, D], F32, H1)
        xs_rows2 = at("xs_rows2", [P, D], F32, XL)
        y_rows = [at(f"y_rows{k}", [P, D], F32, H1 + k * D * 4) for k in range(2)]
        XH_ = i["cache_mem_k"].shape[3]
        DC = D // XH_ // P
        SCALE = float(D // XH_) ** -0.5
        q_t = at("q_t", [P, NC, T], F32, M0)
        k_t = at("k_t", [P, NC, M], F32, H1)
        kv_rows = at("kv_rows", [P, MT, D], F32, H1 + NC * M * 4)
        top[0] = H0
        cache = more("cache", [P, 3, D])
        probs_t = more("probs_t", [P, MT, SEQ])
        probs = more("probs", [P, TT, M])
        s_scores = more("s_scores", [P, MT, B * XH_])
        eye_b = more("eye_b", [P, B, B])
        assert top[0] <= H1
        top[0] = CONV
        q_wide0 = more("q_wide0", [P, D])
        spread = more("spread", [P, MT, B, XH_, B])
        stats = more("stats", [P, 3, TT * XH_])
        s_stats = more("s_stats", [P, 4])
        assert top[0] <= arena0
        q_wide = [q_wide0[:], cache[:, 2, :]]
        s_probs = at("s_probs", [P, M], F32, CONV)
        qs_rows = at("qs_rows", [P, D], F32, CONV)
        os_rows = at("os_rows", [P, D], F32, H0)
        h_high = at("h_high", [P, NC, T], F32R, H0)
        h_low = at("h_low", [P, NC, T], F32R, H1)
        x_mid = nc.dram_tensor("x_mid", (P, NC * T), F32, kind="Internal").ap()
        q_mid = nc.dram_tensor("q_mid", (B, D), F32, kind="Internal").ap()

        ps = ctx.enter_context(nc.psum_tensor("ps", [P, 8, 512], F32))

        def cols(w, it, j, blocks, col0, k0, kn, width=COLS):
            rows = w[0].rearrange("(k p) n -> p k n", p=P)
            return rows[:, k0:k0 + kn, bass.ds(it * (blocks * COLS) + (col0 + j * COLS), width)]

        def plain(w, blocks, col0):
            def sources(it, j, s):
                return [(slice(0, COLS), cols(w, it, j, blocks, col0, s * KS, KS))]
            return sources

        def beta_g(it, j, s):
            c = IN_COLS - 2 * H
            rows = i["w_in"][0].rearrange("(k p) n -> p k n", p=P)[:, s * KS:(s + 1) * KS]
            return [(slice(0, H), rows[:, :, c:c + H]), (slice(32, 32 + H), rows[:, :, c + H:c + 2 * H])]

        IN_COLS = i["w_in"].shape[2]
        SL = NC // KS
        g_wk = Gemm("wk", plain(i["xa_wk"], 2, 0), D // COLS // 2, 2, SL, NC, mem_high, mem_low, memory=True)
        g_wv = Gemm("wv", plain(i["xa_wv"], 2, 0), D // COLS // 2, 2, SL, NC, mem_high, mem_low, memory=True)
        g_lx = Gemm("lx", plain(i["w_in"], 2, 0), W // COLS // 2, 2, SL, NC, x_high, x_low)
        g_ly = Gemm("ly", plain(i["w_in"], 2, W), W // COLS // 2, 2, SL, NC, x_high, x_low)
        g_qkv = Gemm("qkv", plain(i["w_in"], 2, 2 * W), QKV // COLS // 2, 2, SL, NC, x_high, x_low)
        g_z = Gemm("z", plain(i["w_in"], 2, 2 * W + QKV), W // COLS // 2, 2, SL, NC, x_high, x_low)
        g_bg = Gemm("bg", beta_g, 1, 1, SL, NC, x_high, x_low)
        DB = D // COLS
        g_out = Gemm("out", plain(i["w_out"], 2, 0), DB // 2, 2, SL, NC, x_high, x_low)
        g_q = Gemm("q", plain(i["xa_wq"], 2, 0), DB // 2, 2, SL, NC, x_high, x_low)
        g_o = Gemm("o", plain(i["xa_wo"], 2, 0), DB // 2, 2, SL, NC, x_high, x_low)

        def gate_up(c0):
            def sources(it, j, s):
                out = []
                for k, n in enumerate(("ffn_w_gate", "ffn_w_up")):
                    rows = i[n][0].rearrange("(k p) n -> p k n", p=P)[:, s * KS:(s + 1) * KS]
                    out.append((slice(k * P, (k + 1) * P), rows[:, :, bass.ds(it * (2 * P) + (c0 + j) * P, P)]))
                return out
            return sources

        def down(c0, chunks, blocks):
            def sources(it, j, s):
                kn = min(KS, chunks - s * KS)
                return [(slice(0, COLS), cols(i["ffn_w_down"], it, j, blocks, 0, c0 + s * KS, kn))]
            return sources

        ffn = []
        for c0 in range(0, FF, NC):
            n = min(NC, FF - c0)
            slabs = -(-n // KS)
            blocks = 4 if slabs % 2 else 2
            ffn.append((c0, n, Gemm(f"up{c0}", gate_up(c0), n // 2, 2, SL, NC, x_high, x_low),
                        Gemm(f"down{c0}", down(c0, n, blocks), DB // blocks, blocks, slabs, n, h_high, h_low)))
        gemms = [g_wk, g_wv, g_lx, g_ly, g_qkv, g_z, g_bg, g_out, g_q, g_o] + [g for f in ffn for g in f[2:]]
        slab = block = 0
        for g in gemms:
            g.slab0, g.block0 = slab, block
            slab += g.iters * g.blocks * g.slabs
            block += g.iters * g.blocks
            assert g.slab0 % RAW == 0 and (g.blocks * g.slabs % RAW == 0) and (g.iters == 1 or g.blocks % 2 == 0)
        first_gemm, last_gemm = gemms[0], gemms[-1]

        params = ([(0, NORM[n], NC, i[n][0]) for n in norm_names]
                  + [(1, 0, TAPS * LC, i["lru_conv_w"][0]), (1, TAPS * LC, TAPS * GC, i["gdn_conv_w"][0])]
                  + [(2, MISC[n] - MISC0, LC, i[n][0]) for n in misc_names]
                  + [(2, MISC["gdn_norm_w"] - MISC0, 1, i["gdn_norm_w"][0])])
        PAR_ROWS = [len(norm_names) * NC, TAPS * CC, NPAR - MISC0]
        PAR_COLS = [0, CONV0, MISC0]
        row_tiles = ([(mem_rows[:, t, :], P, norm_mem_row) for t in range(MT)]
                     + [(x_rows[:, t, :], P, norm_x_row) for t in range(TT)] + [(xs_rows[:], B, norm_x_row)])
        turns = []
        for t, (rows, n, _) in enumerate(row_tiles):
            per = 4 if n == P else NC
            for c in range(0, NC, per):
                if t < MT:
                    to = [m[:, c:c + per, t * P:t * P + n] for m in (mem_high, mem_low)]
                else:
                    to = [m[:, c:c + per, (t - MT) * P:(t - MT) * P + n] for m in (x_high, x_low)]
                turns.append((t, c, per, n, to))
        TURN_BANKS = 4

        levels = range(LEVELS)
        STEPS = {
            "tensor": ["grow_ready", "k_turned", "kk_ready", "qk_ready", "v_turned"]
            + [f"{n}{l}" for l in levels for n in ("half_ready", "inv_t_ready", "inv_ready") if (n, l) != ("inv_ready", LEVELS - 1)]
            + ["wt_ready", "v_new_ready", "o_ready", "S_ready"],
            "vector": ["differ", "differences", "k_rows", "v_rows", "inner", "qk"]
            + [f"{n}{l}" for l in levels for n in ("half", "inv_t", "inv") if (n, l) != ("inv", LEVELS - 1)] + ["S_done"],
            "scalar": ["grow", "decays", "wt", "v_new", "o_taken"],
            "pool": ["gate_wide", "keys", "values", "inner_low", "inner_beta", "qk_mask", "q_scaled"],
        }
        ENGINE_OF = {n: e for e, names in STEPS.items() for n in names}

        def chunk_sem(name, g):
            return sem(f"chunk_{ENGINE_OF[name]}{g}")

        def step(name, g, n):
            names = STEPS[ENGINE_OF[name]]
            return chunk_sem(name, g), n * len(names) + (names.index(name) + 1)

        block_ = ctx.enter_context(nc.Block())

        @block_.gpsimd
        def _(pool):
            pool.memset(ones[:], 1.0).then_inc(sem("consts"), 1)
            pool.memset(ident[:], 0.0).then_inc(sem("consts"), 1)
            pool.memset(xpad[:, :, 0:TAPS - 1], 0.0).then_inc(sem("consts"), 1)
            pool.wait_ge(sem("consts"), 2)
            pool.affine_select(out=ident[:], in_=ident[:], compare_op=ALU.not_equal, fill=1.0, base=0,
                               pattern=[[-1, P]], channel_multiplier=1).then_inc(sem("consts"), 1)
            for src, dst in (("state_lru_conv", "s_lru_conv"), ("state_gdn_conv", "s_gdn_conv")):
                pool.dma_start(o[dst][0, :, 0:TAPS - 2, :], i[src][0, :, 1:TAPS - 1, :]).then_inc(sem("stored"), 16)
            for g, name in ((g_wk, "p_mem_k"), (g_wv, "p_mem_v")):
                out = o[name][0, 0].rearrange("(t p) h d -> p t (h d)", p=P)

                def store(it):
                    for j in range(g.blocks):
                        pool.wait_ge(sem("acc_taken"), g.block(it, j) + 1)
                        pool.dma_start(out[:, :, bass.ds((it * g.blocks + j) * COLS, COLS)],
                                       kv_out[:, g.acc(j)]).then_inc(sem(f"kv_stored{g.acc(j)}"), 16)
                loop(pool, 0, g.iters, store)
            pool.wait_ge(*after("edge_copied", CC // 4))
            e = edge_rows
            for c0, cn, p_out, s_out in ((0, W, "p_lru_conv", "s_lru_conv"), (W, QKV, "p_gdn_conv", "s_gdn_conv")):
                pool.dma_start(o[p_out][0, 0], e[0:TAPS - 1, c0:c0 + cn]).then_inc(sem("stored"), 16)
                pool.dma_start(o[s_out][0, :, TAPS - 2, :], e[TAPS - 1:EDGE, c0:c0 + cn]).then_inc(sem("stored"), 16)
            pool.wait_ge(sem("slab_used"), g_bg.slab0 + g_bg.slabs)
            for k, n in enumerate(("lru_gate_a_w", "lru_gate_x_w")):
                pool.dma_start(lru_w[:, k], i[n][0].rearrange("h i j -> i h j")).then_inc(sem("lru_w_loaded"), 16)
            for k, n in enumerate(("gdn_A_log", "gdn_dt_bias")):
                pool.dma_start(row_par[:, k, :], i[n].to_broadcast([P, H])).then_inc(sem("row_par_loaded"), 16)
            pool.wait_ge(*after("gates", LC))
            pool.tensor_tensor(gate_x[:], gate_x[:], lx[:].rearrange("p (c t) -> p c t", t=T), ALU.mult).then_inc(sem("gated_x"), 1)
            pool.wait_ge(*after("lru_scanned", 1))
            pool.wait_ge(sem("stored"), 16 * 6)
            pool.memset(upper[:], 1.0).then_inc(sem("masks0"), 1)
            pool.memset(lower[:], 1.0).then_inc(sem("masks0"), 1)
            pool.memset(blocks_mask[:], 0.0).then_inc(sem("masks0"), 1)
            pool.wait_ge(sem("masks0"), 3)
            pool.affine_select(out=upper[:], in_=upper[:], compare_op=ALU.is_ge, fill=0.0, base=0,
                               pattern=[[1, P]], channel_multiplier=-1).then_inc(sem("masks"), 1)
            pool.affine_select(out=lower[:], in_=lower[:], compare_op=ALU.is_ge, fill=0.0, base=-1,
                               pattern=[[-1, P]], channel_multiplier=1).then_inc(sem("masks"), 1)
            for l in range(LEVELS):
                r = 1 << l
                odd = blocks_mask[:, l].rearrange("p (q o r) -> p q o r", o=2, r=r)[:, :, 1, :]
                n = P // (2 * r)
                pool.memset(odd, -1.0).then_inc(sem("masks0"), 1)
                pool.wait_ge(sem("masks0"), 4 + 2 * l)
                pool.affine_select(out=odd, in_=odd, compare_op=ALU.is_ge, fill=0.0, base=0,
                                   pattern=[[-2 * r, n], [0, r]], channel_multiplier=1).then_inc(sem("masks0"), 1)
                pool.wait_ge(sem("masks0"), 5 + 2 * l)
                pool.affine_select(out=odd, in_=odd, compare_op=ALU.is_ge, fill=0.0, base=r - 1,
                                   pattern=[[2 * r, n], [0, r]], channel_multiplier=-1).then_inc(sem("masks"), 1)
            pool.tensor_tensor(gy[:], gy[:], lx[:], ALU.mult).then_inc(sem("lru_out"), 1)

            pool.wait_ge(sem("masks"), 2 + LEVELS)
            pool.wait_ge(*after("gdn_small", 1))
            pool.wait_ge(*after("normed", 2 * H))

            def chunk(n):
                if not type(n) is int:
                    for g in range(2):
                        pool.wait_ge(*step("S_done", g, n - 1))
                for g in range(2):
                    heads = bass.ds(n * H + g * HG, HG)
                    gw = gate[:, heads].rearrange("p (h a) -> p h a", a=1).to_broadcast([P, HG, P])
                    up = upper[:].rearrange("p (a j) -> p a j", a=1).to_broadcast([P, HG, P])
                    pool.tensor_tensor(inv[g][:], gw, up, ALU.mult).then_inc(chunk_sem("gate_wide", g), 1)
                    for dst, c0, name in ((keys, H, "keys"), (values, 2 * H, "values")):
                        src = qkv[:].rearrange("p (c t) -> p c t", t=T)[:, c0 + g * HG:c0 + (g + 1) * HG, bass.ds(n * P, P)]
                        pool.tensor_copy(dst[g][:], src).then_inc(chunk_sem(name, g), 1)
                for g in range(2):
                    heads = bass.ds(n * H + g * HG, HG)
                    low = lower[:].rearrange("p (a j) -> p a j", a=1).to_broadcast([P, HG, P])
                    up = upper[:].rearrange("p (a j) -> p a j", a=1).to_broadcast([P, HG, P])
                    bw = beta[:, heads].rearrange("p (h a) -> p h a", a=1).to_broadcast([P, HG, P])
                    pool.wait_ge(*step("decays", g, n))
                    pool.tensor_tensor(inner[g][:], inner[g][:], low, ALU.mult).then_inc(chunk_sem("inner_low", g), 1)
                    pool.wait_ge(*step("inner_low", g, n))
                    pool.tensor_tensor(inner[g][:], inner[g][:], bw, ALU.mult).then_inc(chunk_sem("inner_beta", g), 1)
                    pool.tensor_tensor(qk[g][:], qk[g][:], up, ALU.mult).then_inc(chunk_sem("qk_mask", g), 1)
                    q = qkv[:].rearrange("p (c t) -> p c t", t=T)[:, g * HG:(g + 1) * HG, bass.ds(n * P, P)]
                    pool.tensor_tensor(grow[g][:], grow[g][:], q, ALU.mult).then_inc(chunk_sem("q_scaled", g), 1)
            chunk(0)
            loop(pool, 1, TT, chunk)
            for g in range(2):
                pool.wait_ge(*step("S_done", g, TT - 1))
                pool.dma_start(o["p_gdn_S"][0, 0, g * HG:(g + 1) * HG].rearrange("h k v -> k h v"), S[g][:]).then_inc(sem("stored"), 16)
            pool.wait_ge(*after("s_cols", 4))
            for b in range(B):
                pool.dma_start(s_S[:, b * H:(b + 1) * H, :], i["state_gdn_S"][0, b].rearrange("h k v -> k h v")).then_inc(sem("s_S_loaded"), 16)
            pool.wait_ge(*after("s_bg_wide", 1))
            pool.wait_ge(sem("s_S_loaded"), 16 * B)
            pool.tensor_tensor(s_S[:], s_S[:], s_bg[:, 1].rearrange("p (m a) -> p m a", a=1).to_broadcast([P, BH, P]),
                               ALU.mult).then_inc(sem("s_decayed"), 1)
            pool.wait_ge(sem("s_S_new"), BH // 4)
            for b in range(B):
                pool.dma_start(o["s_gdn_S"][0, b].rearrange("h k v -> k h v"), s_S[:, b * H:(b + 1) * H, :]).then_inc(sem("stored"), 16)
            pool.wait_ge(*after("h_rows", 2))
            pool.dma_start(o["p_lru_h"][0], h_rows[0:1, :]).then_inc(sem("stored"), 16)
            pool.dma_start(o["s_lru_h"][0], h_rows[1:1 + B, :]).then_inc(sem("stored"), 16)
            pool.wait_ge(*after("mixed_low", 4))
            pool.dma_start(x_rows2[:], i["x_prompt"][0].rearrange("(t p) d -> p t d", p=P)).then_inc(sem("x_rows"), 16)

            def sum_squares(g, c0):
                def block(it, first=False):
                    for j in range(g.blocks):
                        b = g.block(it, j)
                        v = branch[:].rearrange("p c t -> p (c t)")[:, bass.ds((it * g.blocks + j) * 2 * T, 2 * T)]
                        n = b - c0
                        pool.wait_ge(sem("acc_taken"), b + 1)
                        pool.tensor_tensor(sq[:].rearrange("p a t -> p (a t)"), v, v, ALU.mult).then_inc(sem("sq"), 1)
                        pool.wait_ge(sem("sq"), n * 3 + 1)
                        if first and j == 0:
                            pool.tensor_copy(ssum[:], sq[:, 0]).then_inc(sem("sq"), 1)
                        else:
                            pool.tensor_tensor(ssum[:], ssum[:], sq[:, 0], ALU.add).then_inc(sem("sq"), 1)
                        pool.wait_ge(sem("sq"), n * 3 + 2)
                        pool.tensor_tensor(ssum[:], ssum[:], sq[:, 1], ALU.add).then_inc(sem("sq"), 1)
                        pool.wait_ge(sem("sq"), n * 3 + 3)
                block(0, True)
                loop(pool, 1, g.iters, block)

            sum_squares(g_out, g_out.block0)
            pool.wait_ge(sem("slab_used"), g_q.slab0)
            pool.dma_start(xs_rows2[0:B, :], i["x_sample"][:, 0, :]).then_inc(sem("x_rows"), 16)
            pool.wait_ge(*after("x_turned", TT * 4 + 1))
            pool.dma_start(kv_rows[:], o["p_mem_k"][0, 0].rearrange("(t p) h d -> p t (h d)", p=P)).then_inc(sem("kv_rows"), 16)
            pool.wait_ge(*after("k_t_turned", NC // 2))
            pool.dma_start(kv_rows[:], o["p_mem_v"][0, 0].rearrange("(t p) h d -> p t (h d)", p=P)).then_inc(sem("kv_rows"), 16)
            pool.wait_ge(sem("x_new"), NC)
            pool.dma_start(x_mid, xt[:].rearrange("p c t -> p (c t)")).then_inc(sem("x_mid"), 16)

            pool.wait_ge(sem("x_mid"), 16)
            pool.wait_ge(sem("norm_low"), NC)
            pool.memset(eye_b[:], 0.0).then_inc(sem("eye_b"), 1)
            pool.wait_ge(*after("eye_b", 1))
            pool.affine_select(out=eye_b[:], in_=eye_b[:], compare_op=ALU.not_equal, fill=1.0, base=0,
                               pattern=[[1, B], [-1, B]], channel_multiplier=0).then_inc(sem("eye_b"), 1)
            pool.wait_ge(*after("eye_b", 2))
            for c in range(2):
                pool.dma_start(cache[:, c, :], i["cache_mem_k"][0, 0, c * P:(c + 1) * P].rearrange("m h d -> m (h d)")).then_inc(sem(f"cache{c}"), 16)
            pool.wait_ge(*after("qs_rows", XH_))
            pool.dma_start(q_mid, qs_rows[0:B, :]).then_inc(sem("q_mid"), 16)
            pool.wait_ge(sem("q_mid"), 16)
            for b in range(B):
                if b >= 2:
                    pool.wait_ge(sem("s_scored"), (b - 1) * MT)
                pool.dma_start(q_wide[b % 2], q_mid[b:b + 1, :].to_broadcast([P, D])).then_inc(sem(f"q_wide{b % 2}"), 16)
                for c in range(MT):
                    if b:
                        pool.wait_ge(sem("s_scored"), (b - 1) * MT + c + 1)
                        pool.dma_start(cache[:, c, :], i["cache_mem_k"][0, b, c * P:(c + 1) * P].rearrange("m h d -> m (h d)")).then_inc(sem(f"cache{c}"), 16)
            for k in range(B * MT):
                if k < 3:
                    pool.wait_ge(sem("s_scored"), B * MT)
                else:
                    pool.wait_ge(*after("s_valued", k - 2))
                pool.dma_start(cache[:, k % 3, :],
                               i["cache_mem_v"][0, k // MT, k % MT * P:(k % MT + 1) * P].rearrange("m h d -> m (h d)")).then_inc(sem(f"values_in{k % 3}"), 16)
            sum_squares(g_o, g_o.block0 - DB)
            pool.wait_ge(*after("s_o_low", 1))
            pool.wait_ge(sem("slab_used"), g_o.slab0 + 1)
            pool.dma_start(xt[:].rearrange("p c t -> p (c t)"), x_mid).then_inc(sem("x_back"), 16)
            pool.wait_ge(sem("x_new"), 2 * NC)
            pool.dma_start(x_mid, xt[:].rearrange("p c t -> p (c t)")).then_inc(sem("x_mid"), 16)
            g_last = ffn[-1][3]
            sum_squares(g_last, g_last.block0 - 2 * DB)
            pool.wait_ge(sem("slab_used"), g_last.slab0 + g_last.iters * g_last.blocks * g_last.slabs)
            pool.dma_start(xt[:].rearrange("p c t -> p (c t)"), x_mid).then_inc(sem("x_back"), 16)
            for t in range(TT + 1):
                pool.wait_ge(*after("y_copied", (t + 1) * 4 if t < TT else TT * 4 + 4))
                if t < TT:
                    pool.dma_start(o["y_prompt"][0, t * P:(t + 1) * P, :], y_rows[t % 2][:]).then_inc(sem(f"y_stored{t % 2}"), 16)
                else:
                    pool.dma_start(o["y_sample"][:, 0, :], y_rows[0][0:B, :]).then_inc(sem("y_stored0"), 16)
            pool.wait_ge(sem("y_stored0"), 16 * (TT // 2 + 1))
            pool.wait_ge(sem("y_stored1"), 16 * (TT // 2))
            pool.wait_ge(sem("stored"), 16 * (6 + 2 + B + 2))

        @block_.sync
        def _(sp):
            for t in range(MT):
                sp.dma_start(mem_rows[:, t, :], i["mem_prompt"][0, t * P:(t + 1) * P, :]).then_inc(sem(f"rows{t}"), 16)
            sp.dma_start(norm_mem_row[:], i["norm_mem"].to_broadcast([P, D])).then_inc(sem("norm_rows"), 16)
            for tile, r, n, v in params:
                v = v.rearrange("(r p) -> r p", p=P) if len(v.shape) == 1 else v.rearrange("j (c p) -> j c p", p=P)
                if len(v.shape) == 3:
                    for j in range(TAPS):
                        m = n // TAPS
                        sp.dma_start(par_rows[r + j * m:r + (j + 1) * m, tile, :], v[j]).then_inc(sem("par_loaded"), 16)
                else:
                    sp.dma_start(par_rows[r:r + n, tile, :], v).then_inc(sem("par_loaded"), 16)
            for c0, cn, src in ((0, W, "state_lru_conv"), (W, QKV, "state_gdn_conv")):
                sp.dma_start(state_rows[0:B * (TAPS - 1), c0:c0 + cn],
                             i[src][0].rearrange("b j n -> (b j) n")).then_inc(sem("par_loaded"), 16)
            sp.dma_start(h0_rows[0:B, :], i["state_lru_h"][0]).then_inc(sem("par_loaded"), 16)
            sp.dma_start(norm_x_row[:], i["norm_mix_pre"].to_broadcast([P, D])).then_inc(sem("norm_rows"), 16)
            for t in range(TT):
                sp.dma_start(x_rows[:, t, :], i["x_prompt"][0, t * P:(t + 1) * P, :]).then_inc(sem(f"rows{MT + t}"), 16)
            sp.wait_ge(sem("turned"), NC // 4)
            sp.dma_start(xs_rows[0:B, :], i["x_sample"][:, 0, :]).then_inc(sem(f"rows{MT + TT}"), 16)

            def load(g, it, jj):
                if g.name != first_gemm.name or type(it) is not int or it * g.blocks * g.slabs + jj >= RAW:
                    sp.wait_ge(sem("w_low_ready"), g.slab(it, jj) - (RAW - 1))
                parts = g.sources(it, jj // g.slabs, jj % g.slabs)
                kn = min(KS, g.chunks - jj % g.slabs * KS)
                for where, source in parts:
                    sp.dma_start(w_raw[:, (g.slab0 + jj) % RAW, 0:kn, where],
                                 source).then_inc(sem(f"w_loaded{(g.slab0 + jj) % RAW}"), 32 // len(parts))

            for g in gemms:
                def loads(it, g=g):
                    for jj in range(g.blocks * g.slabs):
                        load(g, it, jj)
                if g.name == first_gemm.name:
                    loads(0)
                loop(sp, 1 if g.name == first_gemm.name else 0, g.iters, loads)

        @block_.scalar
        def _(act):
            def row_squares(tiles):
                for t in tiles:
                    rows, n, _ = row_tiles[t]
                    act.wait_ge(sem(f"rows{t}"), 16)
                    if t:
                        act.wait_ge(sem("row_squares"), t)
                    act.activation(ps[0:n, 4:4 + D // 512, :], rows[0:n].rearrange("p (b c) -> p b c", c=512),
                                   ACT.Square, accum_out=ssq[0:n, t:t + 1]).then_inc(sem("row_squares"), 1)

            def row_root(k):
                act.wait_ge(sem("row_means"), k + 1)
                a, b = row_groups[k]
                act.activation(root[:, a:b], ms[:, a:b], ACT.Sqrt).then_inc(sem("row_roots"), 1)

            act.wait_ge(sem("ssq_clear"), 1)
            row_squares(range(0, MT))
            row_root(0)
            row_squares(range(MT, MT + TT))
            row_root(1)

            def split_high(g, it, jj):
                slot = (g.slab0 + jj) % SPLIT
                act.wait_ge(sem(f"w_loaded{(g.slab0 + jj) % RAW}"), g.loads(it, jj) * 32)
                if not (g.name == first_gemm.name and type(it) is int and it * g.blocks * g.slabs + jj < SPLIT):
                    act.wait_ge(sem("slab_used"), g.slab(it, jj) - (SPLIT - 1))
                act.activation(w_high[:, slot], w_raw[:, (g.slab0 + jj) % RAW], ACT.Copy).then_inc(sem("w_high_ready"), 1)

            def turn_high(n):
                for k in n:
                    t, c, per, rows, to = turns[k]
                    act.wait_ge(sem("turned"), k + 1)
                    act.activation(to[0], ps[:, k % TURN_BANKS, 0:per * rows].rearrange("p (c t) -> p c t", c=per),
                                   ACT.Copy).then_inc(sem("turn_high"), 1)

            mem_turns = MT * NC // 4
            turn_high(range(0, mem_turns))
            row_squares([MT + TT])
            row_root(2)
            turn_high(range(mem_turns, len(turns)))
            split_high(first_gemm, 0, 0)
            split_high(first_gemm, 0, 1)

            def gemm(g, evacuate, peel=0):
                last = g.name == last_gemm.name

                def body(it, end=False):
                    for j in range(g.blocks):
                        for s in range(SPLIT, g.slabs + SPLIT):
                            if s == g.slabs and end and j == g.blocks - 1:
                                break
                            split_high(g, it, j * g.slabs + s)
                        evacuate(it, j)
                if peel:
                    body(0)
                loop(act, peel, g.iters - last, body)
                if last:
                    body(g.iters - 1, True)

            def acc_ready(g, it, j):
                act.wait_ge(sem("slab_used"), g.slab(it, (j + 1) * g.slabs - 1) + 1)
                return g.acc(j) * 4

            def take_kv(g):
                def evacuate(it, j):
                    b = acc_ready(g, it, j)
                    if not (g.name == first_gemm.name and type(it) is int and it == 0):
                        act.wait_ge(sem(f"kv_stored{g.acc(j)}"), (it + g.block0 // 2) * 16)
                    act.activation(kv_out[:, g.acc(j)], ps[:, b:b + 4:2, 0:COLS], ACT.Copy).then_inc(sem("acc_taken"), 1)
                return evacuate

            def gemm_kv(g):
                def body(it):
                    for j in range(g.blocks):
                        for s in range(SPLIT, g.slabs + SPLIT):
                            split_high(g, it, j * g.slabs + s)
                        take_kv(g)(it, j)
                if g.name == first_gemm.name:
                    body(0)
                loop(act, 1 if g.name == first_gemm.name else 0, g.iters, body)

            gemm_kv(g_wk)
            gemm_kv(g_wv)

            for p in range(2):
                act.wait_ge(sem(f"kv_stored{p}"), 16 * (g_wk.iters + g_wv.iters))

            def take_convolved(g, func, out, c0):
                def evacuate(it, j):
                    b = acc_ready(g, it, j)
                    for m in range(2):
                        chunk = it * (2 * g.blocks) + (2 * j + m)
                        done = chunk + c0
                        first = type(it) is int and c0 == 0 and it == 0 and j == 0
                        if not first:
                            act.wait_ge(sem("convolved"), done - 1)
                        acc = ps[:, b + 2 * m:b + 2 * m + 2, 0:HALF]
                        x = xpad[:, m]
                        windows = x[:, S0:PADDED].rearrange("p (b j) -> p b j", j=TAPS)
                        act.activation(x[:, TAPS - 1:TAPS - 1 + HALF], acc[:, 0], ACT.Copy)
                        act.activation(x[:, TAPS - 1 + HALF:S0], acc[:, 1, 0:SEQ - HALF], ACT.Copy)
                        act.activation(windows[:, :, TAPS - 1], acc[:, 1, SEQ - HALF:HALF], ACT.Copy)
                        act.activation(windows[:, :, 0:TAPS - 1],
                                       conv_state[:, bass.ds(done, 1), :].rearrange("p a (b j) -> p (a b) j", b=B), ACT.Copy)
                        ins = act.activation(edge[:, bass.ds(done, 1), :].rearrange("p a e -> p (a e)"),
                                             acc[:, 1, HALF - EDGE:HALF], ACT.Copy)
                        ins.then_inc(sem("acc_taken" if m else "padded"), 1)
                    for m in range(2):
                        chunk = it * (2 * g.blocks) + (2 * j + m)
                        done = chunk + c0
                        act.wait_ge(sem("convolved"), done + 1)
                        act.activation(out[:, bass.ds(chunk * T, SEQ)], conved[:, 0:SEQ], func)
                        act.activation(out[:, bass.ds(chunk * T + SEQ, B)], conved[:, S0:CONVED:TAPS],
                                       func).then_inc(sem("conv_taken"), 1)
                return evacuate

            def take(g, func, out):
                def evacuate(it, j):
                    b = acc_ready(g, it, j)
                    for m in range(2):
                        chunk = it * (2 * g.blocks) + (2 * j + m)
                        ins = act.activation(out[:, bass.ds(chunk * T, T)].rearrange("p (h t) -> p h t", h=2),
                                             ps[:, b + 2 * m:b + 2 * m + 2, 0:HALF], func)
                    ins.then_inc(sem("acc_taken"), 1)
                return evacuate

            gemm(g_lx, take_convolved(g_lx, ACT.Identity, lx, 0), peel=1)
            gemm(g_ly, take(g_ly, ACT.Gelu_apprx_tanh, gy))
            gemm(g_qkv, take_convolved(g_qkv, ACT.Silu, qkv, LC))
            gemm(g_z, take(g_z, ACT.Silu, z))

            def nothing(it, j):
                pass

            gemm(g_bg, nothing)

            act.wait_ge(*after("sp_abs", 1))
            act.activation(sp[1][:], sp[1][:], ACT.Exp, scale=-1.0).then_inc(sem("sp_exp"), 1)
            act.wait_ge(sem("row_par_loaded"), 32)
            act.activation(row_par[:, 0], row_par[:, 0], ACT.Exp).then_inc(sem("sp_exp"), 1)
            act.activation(beta[:].rearrange("p (n h) -> p n h", h=H), bg[:, :, 0:H], ACT.Sigmoid).then_inc(sem("beta"), 1)
            for c in range(LC):
                act.wait_ge(*after("gates_ready", c + 1))
                b = c % 2 * 4
                for k, (dst, name) in enumerate(((gate_a, "lru_gate_a_b"), (gate_x, "lru_gate_x_b"))):
                    ins = act.activation(dst[:, c].rearrange("p (h t) -> p h t", h=2), ps[:, b + 2 * k:b + 2 * k + 2, 0:HALF],
                                         ACT.Sigmoid, bias=par[:, MISC[name] + c:MISC[name] + c + 1])
                ins.then_inc(sem("gates"), 1)
            act.wait_ge(*after("log_a", 1))
            act.activation(lru_a[:], gate_a[:], ACT.Exp)
            act.activation(gate_a[:], gate_a[:], ACT.Tanh, scale=-0.5).then_inc(sem("lru_tanh"), 1)
            act.wait_ge(*after("lru_tanh", 1))
            act.activation(gate_a[:], gate_a[:], ACT.Sqrt).then_inc(sem("lru_sqrt"), 1)

            act.wait_ge(*after("lru_scanned", 1))
            act.wait_ge(sem("stored"), 16 * 6)
            for c in range(2 * H + 1):
                if c < 2 * H:
                    if c >= 2:
                        act.wait_ge(*after("l2_summed", c - 1))
                    act.activation(squares[:, c % 2], qkv[:, c * T:(c + 1) * T], ACT.Square).then_inc(sem("l2_squares"), 1)
                if c >= 1:
                    m = c - 1
                    act.wait_ge(*after("l2_summed", m + 1))
                    if m >= 2:
                        act.wait_ge(*after("normed", m - 1))
                    act.activation(l2_root[:, m % 2].rearrange("p (h t) -> p h t", h=2), ps[:, m % 2 * 2:m % 2 * 2 + 2, 0:HALF],
                                   ACT.Sqrt, bias=eps_col[:]).then_inc(sem("l2_roots"), 1)
            act.wait_ge(*after("gc_ready", 1))
            act.activation(egc[:], gc[:], ACT.Exp).then_inc(sem("gc_exps"), 1)
            act.activation(glast[:], glast[:], ACT.Exp).then_inc(sem("gc_exps"), 1)
            act.activation(dgc[:], dgc[:], ACT.Exp).then_inc(sem("gc_exps"), 1)

            def chunk(n):
                for g in range(2):
                    act.wait_ge(*step("grow_ready", g, n))
                    act.activation(grow[g][:], ps[:, 4 * g, :].rearrange("p (h j) -> p h j", h=HG), ACT.Exp).then_inc(chunk_sem("grow", g), 1)
                    act.wait_ge(*step("differences", g, n))
                    act.activation(inner[g][:], inner[g][:], ACT.Exp, scale=-1.0)
                    act.activation(qk[g][:], qk[g][:], ACT.Exp).then_inc(chunk_sem("decays", g), 1)
                for g in range(2):
                    act.wait_ge(*step("wt_ready", g, n))
                    act.activation(kbg[g][:], ps[:, 4 * g + 3, :].rearrange("p (h j) -> p h j", h=HG), ACT.Copy, scale=-1.0).then_inc(chunk_sem("wt", g), 1)
                for g in range(2):
                    act.wait_ge(*step("v_new_ready", g, n))
                    act.activation(vb[g][:], ps[:, 4 * g, :].rearrange("p (h j) -> p h j", h=HG), ACT.Copy).then_inc(chunk_sem("v_new", g), 1)
                for g in range(2):
                    act.wait_ge(*step("o_ready", g, n))
                    dst = qkv[:].rearrange("p (c t) -> p c t", t=T)[:, 2 * H + g * HG:2 * H + (g + 1) * HG, bass.ds(n * P, P)]
                    act.activation(dst, ps[:, 4 * g + 1, :].rearrange("p (h j) -> p h j", h=HG), ACT.Copy).then_inc(chunk_sem("o_taken", g), 1)
            loop(act, 0, TT, chunk)
            for g in range(2):
                act.wait_ge(*step("o_taken", g, TT - 1))
                act.wait_ge(*step("S_done", g, TT - 1))
            o_rows = qkv[:].rearrange("p (c t) -> p c t", t=T)[:, 2 * H:3 * H, 0:SEQ]
            act.activation(o_squares[:].rearrange("p (h n) v -> p h (n v)", h=H), o_rows, ACT.Square).then_inc(sem("o_squares"), 1)
            act.wait_ge(*after("s_wide_ready", 1))
            act.activation(s_bg[:, 0], ps[:, 0, 0:BH], ACT.Copy)
            act.activation(s_bg[:, 1], ps[:, 0, BH:2 * BH], ACT.Exp).then_inc(sem("s_bg_wide"), 1)
            act.wait_ge(*after("o_ms", 1))
            act.activation(o_root[:], o_ms[:], ACT.Sqrt).then_inc(sem("o_root"), 1)
            act.wait_ge(*after("s_var", 1))
            act.activation(s_t[:], s_t[:], ACT.Sqrt).then_inc(sem("s_root"), 1)

            act.wait_ge(*after("lru_out", 1))
            act.wait_ge(*after("s_o_done", 1))
            act.wait_ge(*after("h_rows", 2))
            act.wait_ge(sem("stored"), 16 * (6 + 2 + B + 2))
            halves = [(gy, 0), (gy, 1), (z, 0), (z, 1)]
            for k, (src, part) in enumerate(halves):
                act.activation(x_high[:, 4 * k:4 * k + 4], src[:, part * 4 * T:(part + 1) * 4 * T].rearrange("p (c t) -> p c t", t=T),
                               ACT.Copy).then_inc(sem("mixed_high"), 1)
            act.wait_ge(*after("mixed_low", 4))

            def flat(t):
                return t[:].rearrange("p c t -> p (c t)")

            def root_of_mean(r):
                act.wait_ge(sem("mean"), r + 1)
                act.activation(ssum[:], ssum[:], ACT.Sqrt).then_inc(sem("rooted"), 1)

            def residual(r, last=False):
                root_of_mean(2 * r)
                if last:
                    return
                for c in range(NC):
                    act.wait_ge(sem("x_new"), r * NC + c + 1)
                    if c >= 2:
                        act.wait_ge(sem("x_summed"), r * (NC - 1) + c - 1)
                    act.activation(sq[:, c % 2], xt[:, c], ACT.Square).then_inc(sem("x_squares"), 1)
                root_of_mean(2 * r + 1)
                for c in range(NC):
                    act.wait_ge(sem("x_weighed"), r * NC + c + 1)
                    act.activation(x_high[:, c], xw[:, c % 2], ACT.Copy).then_inc(sem("norm_high"), 1)

            gemm(g_out, take(g_out, ACT.Copy, flat(branch)))
            for t in range(TT + 1):
                for b in range(4 if t < TT else 1):
                    k = t * 4 + b
                    act.wait_ge(*after("x_turned", k + 1))
                    if t < TT:
                        act.activation(xt[:, 4 * b:4 * b + 4, t * P:(t + 1) * P],
                                       ps[:, 4 + k % 4, :].rearrange("p (c t) -> p c t", c=4), ACT.Copy).then_inc(sem("x_turns_taken"), 1)
                    else:
                        act.activation(xt[:, :, SEQ:T], ps[:, 4 + k % 4, 0:NC * B].rearrange("p (c t) -> p c t", c=NC),
                                       ACT.Copy).then_inc(sem("x_turns_taken"), 1)
            for k in range(NC // 2):
                act.wait_ge(*after("k_t_turned", k + 1))
                act.activation(k_t[:, 2 * k:2 * k + 2, :], ps[:, 4 + k % 4, :].rearrange("p (c m) -> p c m", c=2), ACT.Copy).then_inc(sem("k_t"), 1)
            residual(0)
            gemm(g_q, take(g_q, ACT.Copy, flat(q_t)))

            for k in range(XH_):
                act.wait_ge(*after("qs_turned", k + 1))
                act.activation(qs_rows[0:B, k * 512:(k + 1) * 512], ps[0:B, 4 + k, :], ACT.Copy).then_inc(sem("qs_rows"), 1)

            def exponentials(h, t):
                n = h * TT + t
                act.wait_ge(sem("row_max"), n // 2 + 1)
                if h:
                    act.wait_ge(sem("probs_turned"), h)
                act.activation(probs[:, t], ps[:, h % 2 * 2 + t // 2, t % 2 * M:(t % 2 + 1) * M], ACT.Exp, bias=stats[:, 0, n:n + 1],
                               scale=SCALE, accum_out=stats[:, 1, n:n + 1]).then_inc(sem("exponentials"), 1)

            act.wait_ge(sem("x_mid"), 16)
            for t in range(TT):
                exponentials(0, t)
            for h in range(XH_):
                act.wait_ge(sem("probs_turned"), h + 1)
                if h:
                    act.wait_ge(sem("pv_ready"), h * DC)
                for k in range(2):
                    ins = act.activation(probs_t[:, :, k * 2 * P:(k + 1) * 2 * P].rearrange("p m (t l) -> p t m l", t=2),
                                         ps[:, 4 + k, :].rearrange("p (t m l) -> p t m l", t=2, m=MT), ACT.Copy)
                ins.then_inc(sem("probs_t"), 1)
                for t in range(TT):
                    if h + 1 < XH_:
                        exponentials(h + 1, t)
                    n = h * DC + t
                    act.wait_ge(sem("pv_ready"), n + 1)
                    act.activation(x_high[:, n, 0:SEQ], ps[:, 6 + n % 2, :], ACT.Copy).then_inc(sem("pv_high"), 1)
            act.wait_ge(*after("s_max", 1))
            act.activation(s_probs[0:B * XH_], ps[0:B * XH_, 0, 0:M], ACT.Exp, bias=s_stats[0:B * XH_, 1:2], scale=SCALE,
                           accum_out=s_stats[0:B * XH_, 2:3]).then_inc(sem("s_exp"), 1)
            act.wait_ge(*after("s_valued", B * MT))
            act.activation(os_rows[0:B, :].rearrange("p (h d) -> p h d", h=XH_), ps[0:B, 4:4 + XH_, :], ACT.Copy).then_inc(sem("os_rows"), 1)
            act.wait_ge(*after("os_turned", 1))
            act.activation(x_high[:, :, SEQ:T], ps[:, 2, 0:NC * B].rearrange("p (c b) -> p c b", b=B), ACT.Copy).then_inc(sem("s_o_high"), 1)

            gemm(g_o, take(g_o, ACT.Copy, flat(branch)))
            residual(1)

            act.wait_ge(sem("x_mid"), 32)
            for c0, n, g_up, g_down in ffn:
                def hidden(it, j, g=g_up, c0=c0):
                    b = acc_ready(g, it, j)
                    chunk = it * 2 + j
                    act.activation(sq[:, j].rearrange("p (h t) -> p h t", h=2), ps[:, b:b + 2, 0:HALF], ACT.Silu).then_inc(sem("silu"), 1)
                    act.wait_ge(sem("acc_taken"), g.block(it, j) + 1)
                    act.activation(flat(h_high)[:, bass.ds(chunk * T, T)], xw[:, j], ACT.Copy).then_inc(sem("h_high"), 1)
                gemm(g_up, hidden)
                gemm(g_down, nothing)
            residual(2, last=True)
            for t in range(TT + 1):
                for q in range(4):
                    k = t * 4 + q
                    rows = P if t < TT else B
                    act.wait_ge(*after("y_turned", k + 1))
                    if t >= 2 and q == 0:
                        act.wait_ge(sem(f"y_stored{t % 2}"), 16 * (t // 2))
                    act.activation(y_rows[t % 2][0:rows, q * 512:(q + 1) * 512], ps[0:rows, k % 8, :], ACT.Copy).then_inc(sem("y_copied"), 1)

        @block_.vector
        def _(dve):
            dve.memset(eps_col[:], EPS)
            dve.memset(ssq[:], 1.0).then_inc(sem("ssq_clear"), 1)
            dve.wait_ge(*after("small_turned", 1))
            for k in range(3):
                ins = dve.tensor_copy(par[:, PAR_COLS[k]:PAR_COLS[k] + PAR_ROWS[k]], ps[:, 0, k * P:k * P + PAR_ROWS[k]])
            ins.then_inc(sem("small_copied"), 1)
            NS = B * (TAPS - 1)
            dve.wait_ge(*after("small_turned", 2))
            dve.tensor_copy(conv_state[:, 0:LC, :], ps[:, 1, 0:LC * NS].rearrange("p (c s) -> p c s", s=NS))
            dve.tensor_copy(h0[:], ps[:, 1, LC * NS:LC * NS + LC * B].rearrange("p (c b) -> p c b", b=B)).then_inc(sem("small_copied"), 1)
            for k in range(2):
                dve.wait_ge(*after("small_turned", 3 + k))
                c = LC + k * GC // 2
                dve.tensor_copy(conv_state[:, c:c + GC // 2, :],
                                ps[:, 2 + k, 0:GC // 2 * NS].rearrange("p (c s) -> p c s", s=NS)).then_inc(sem("small_copied"), 1)

            def row_scale(k):
                a, b = row_groups[k]
                dve.wait_ge(sem("row_squares"), b)
                dve.tensor_scalar(ms[:, a:b], ssq[:, a:b], 1.0 / D, EPS, ALU.mult, ALU.add).then_inc(sem("row_means"), 1)
                dve.wait_ge(sem("row_roots"), k + 1)
                dve.reciprocal(rstd_rows[:, a:b], root[:, a:b]).then_inc(sem("row_rstd"), 1)
                dve.wait_ge(sem("row_rstd"), k + 1)
                dve.wait_ge(sem("norm_rows"), 32)
                for t in range(a, b):
                    rows, n, w = row_tiles[t]
                    dve.scalar_tensor_tensor(rows[0:n], rows[0:n], rstd_rows[0:n, t:t + 1], w[0:n],
                                             ALU.mult, ALU.mult).then_inc(sem("rows_scaled"), 1)

            def turn_low(n):
                for k in n:
                    t, c, per, rows, to = turns[k]
                    dve.wait_ge(sem("turn_high"), k + 1)
                    dve.tensor_tensor(to[1], ps[:, k % TURN_BANKS, 0:per * rows].rearrange("p (c t) -> p c t", c=per),
                                      to[0].bitcast(F32), ALU.subtract).then_inc(sem("turn_low"), 1)

            mem_turns = MT * NC // 4
            row_scale(0)
            row_scale(1)
            turn_low(range(0, mem_turns))
            row_scale(2)
            turn_low(range(mem_turns, len(turns)))

            def split_low(g, it, jj):
                slot = (g.slab0 + jj) % SPLIT
                dve.wait_ge(sem("w_high_ready"), g.slab(it, jj) + 1)
                dve.tensor_tensor(w_low[:, slot], w_raw[:, (g.slab0 + jj) % RAW], w_high[:, slot].bitcast(F32),
                                  ALU.subtract).then_inc(sem("w_low_ready"), 1)

            def gemm(g, evacuate, peel=0):
                last = g.name == last_gemm.name

                def body(it, end=False):
                    for j in range(g.blocks):
                        for s in range(SPLIT, g.slabs + SPLIT):
                            if s == g.slabs and end and j == g.blocks - 1:
                                break
                            split_low(g, it, j * g.slabs + s)
                        evacuate(it, j)
                if peel:
                    body(0)
                loop(dve, peel, g.iters - last, body)
                if last:
                    body(g.iters - 1, True)

            def nothing(it, j):
                pass

            def convolve(g, c0, w0, wn, bias):
                def evacuate(it, j):
                    for m in range(2):
                        chunk = it * (2 * g.blocks) + (2 * j + m)
                        done = chunk + c0
                        if m:
                            dve.wait_ge(sem("acc_taken"), g.block(it, j) + 1)
                        else:
                            dve.wait_ge(sem("padded"), it * g.blocks + (c0 // 2 + j + 1))
                        if not (type(it) is int and it == 0 and j == 0 and m == 0 and c0 == 0):
                            dve.wait_ge(sem("conv_taken"), done)
                        x = xpad[:, m]

                        def col(k):
                            return par[:, bass.ds(chunk + k, 1)]
                        if bias is None:
                            ins = dve.tensor_scalar(conved[:], x[:, 0:CONVED], col(w0), None, ALU.mult)
                        else:
                            ins = dve.tensor_scalar(conved[:], x[:, 0:CONVED], col(w0), col(bias), ALU.mult, ALU.add)
                        for tap in range(1, TAPS):
                            ins.then_inc(sem("conv_taps"), 1)
                            dve.wait_ge(sem("conv_taps"), done * (TAPS - 1) + tap)
                            ins = dve.scalar_tensor_tensor(conved[:], x[:, tap:tap + CONVED], col(w0 + tap * wn), conved[:],
                                                           ALU.mult, ALU.add)
                        ins.then_inc(sem("convolved"), 1)
                return evacuate

            split_low(first_gemm, 0, 0)
            split_low(first_gemm, 0, 1)
            gemm(g_wk, nothing)
            gemm(g_wv, nothing)
            gemm(g_lx, convolve(g_lx, 0, CONV0, LC, MISC["lru_conv_b"]), peel=1)
            gemm(g_ly, nothing)
            gemm(g_qkv, convolve(g_qkv, LC, CONV0 + TAPS * LC, GC, None))
            gemm(g_z, nothing)

            gemm(g_bg, nothing)
            chain = [0]

            def link(ins):
                chain[0] += 1
                ins.then_inc(sem("dve_chain"), 1)
                dve.wait_ge(sem("dve_chain"), chain[0])

            dve.wait_ge(sem("slab_used"), g_bg.slab0 + g_bg.slabs)
            dve.tensor_copy(bg_rows[:].rearrange("p (h t) -> p h t", h=2), ps[:, g_bg.acc(0) * 4:g_bg.acc(0) * 4 + 2, 0:HALF]).then_inc(sem("acc_taken"), 1)
            for k in range(CC // 4):
                dve.wait_ge(*after("edge_turned", k + 1))
                dve.tensor_copy(edge_rows[0:EDGE, k * 512:(k + 1) * 512], ps[0:EDGE, 4 + k % 4, :]).then_inc(sem("edge_copied"), 1)
            x, y, d, q, q2, pl = (t[:] for t in sp)
            heads = x[:, LC:SPW].rearrange("p (n h) -> p n h", h=H)
            dve.tensor_scalar(x[:, 0:LC], par[:, MISC["lru_lambda"]:MISC["lru_lambda"] + LC], -1.0, None, ALU.mult)
            link(dve.memset(bg[:], 0.0))
            dve.wait_ge(*after("bg_turned", 1))
            dve.tensor_copy(bg[:, 0:TT, :], ps[:, 1, 0:TT * 40].rearrange("p (n c) -> p n c", c=40))
            link(dve.tensor_copy(bg[0:B, TT, :], ps[0:B, 1, TT * 40:TT * 40 + 40]))
            dve.wait_ge(sem("row_par_loaded"), 32)
            link(dve.tensor_tensor(heads, bg[:, :, 32:32 + H],
                                   row_par[:, 1].rearrange("p (a h) -> p a h", a=1).to_broadcast([P, TT + 1, H]), ALU.add))
            link(dve.tensor_scalar(q, x, -1.0, None, ALU.mult))
            dve.tensor_tensor(y, x, q, ALU.max).then_inc(sem("sp_abs"), 1)
            dve.wait_ge(*after("sp_exp", 1))
            link(dve.tensor_scalar(d, y, 2.0, None, ALU.add))
            link(dve.reciprocal(q, d))
            link(dve.tensor_tensor(q, q, y, ALU.mult))
            link(dve.tensor_tensor(q2, q, q, ALU.mult))
            link(dve.tensor_scalar(pl, q2, 1.0 / 17, None, ALU.mult))
            for k in range(15, 1, -2):
                link(dve.scalar_tensor_tensor(pl, pl, 1.0 / k, q2, ALU.add, ALU.mult))
            link(dve.scalar_tensor_tensor(pl, pl, 1.0, q, ALU.add, ALU.mult))
            link(dve.tensor_scalar(x, x, 0.0, None, ALU.max))
            link(dve.scalar_tensor_tensor(x, pl, 2.0, x, ALU.mult, ALU.add))
            dve.tensor_scalar(x[:, 0:LC], x[:, 0:LC], -8.0, None, ALU.mult).then_inc(sem("lru_rate"), 1)
            dve.wait_ge(*after("sp_exp", 2))
            dve.scalar_tensor_tensor(gate[:].rearrange("p (n h) -> p n h", h=H), heads, -1.0,
                                     row_par[:, 0].rearrange("p (a h) -> p a h", a=1).to_broadcast([P, TT + 1, H]),
                                     ALU.mult, ALU.mult).then_inc(sem("gdn_gate"), 1)
            dve.wait_ge(*after("gates", LC))
            dve.wait_ge(*after("lru_rate", 1))
            for c in range(LC):
                ins = dve.tensor_scalar(gate_a[:, c], gate_a[:, c], x[:, c:c + 1], None, ALU.mult)
            ins.then_inc(sem("log_a"), 1)
            dve.wait_ge(*after("lru_sqrt", 1))
            dve.wait_ge(*after("gated_x", 1))
            link(dve.scalar_tensor_tensor(gate_a[:], lru_a[:], 1.0, gate_a[:], ALU.add, ALU.mult))
            link(dve.tensor_tensor(gate_x[:], gate_x[:], gate_a[:], ALU.mult))
            hs = gate_a[:, :, 0:B]
            link(dve.tensor_tensor(hs, lru_a[:, :, SEQ:T], h0[:], ALU.mult))
            hx = lx[:].rearrange("p (c t) -> p c t", t=T)
            dve.tensor_tensor(hx[:, :, SEQ:T], gate_x[:, :, SEQ:T], hs, ALU.add)
            for c in range(LC):
                ins = dve.tensor_tensor_scan(hx[:, c, 0:SEQ], lru_a[:, c, 0:SEQ], gate_x[:, c, 0:SEQ], 0.0, ALU.mult, ALU.add)
            ins.then_inc(sem("lru_scanned"), 1)
            for c in range(2 * H):
                dve.wait_ge(sem("l2_roots"), c + 1)
                link(dve.reciprocal(l2_root[:, c % 2], l2_root[:, c % 2]))
                v = qkv[:, c * T:(c + 1) * T]
                dve.scalar_tensor_tensor(v, v, P ** -0.5 if c < H else 1.0, l2_root[:, c % 2], ALU.mult, ALU.mult).then_inc(sem("normed"), 1)
            dve.wait_ge(*after("gc_summed", 1))
            link(dve.tensor_copy(gc[:], ps[:, 4, 0:TT * H]))
            dve.tensor_copy(glast[:], ps[:, 4, TT * H:2 * TT * H])
            dve.tensor_tensor(dgc[:], ps[:, 4, TT * H:2 * TT * H], gc[:], ALU.subtract).then_inc(sem("gc_ready"), 1)
            dve.wait_ge(*after("gc_exps", 3))
            dve.wait_ge(*after("beta", 1))
            dve.tensor_tensor(begc[:], beta[:, 0:TT * H], egc[:], ALU.mult).then_inc(sem("gdn_small"), 1)
            for g in range(2):
                ins = dve.memset(S[g][:], 0.0)
            ins.then_inc(sem("S_clear"), 1)
            dve.wait_ge(*after("gdn_small", 1))
            dve.wait_ge(*after("S_clear", 1))
            dve.wait_ge(sem("masks"), 2 + LEVELS)

            def wide(t, n, g):
                return t[:, bass.ds(n * H + g * HG, HG)].rearrange("p (h a) -> p h a", a=1).to_broadcast([P, HG, P])

            def bank(k):
                return ps[:, k, :].rearrange("p (h j) -> p h j", h=HG)

            def chunk(n):
                for g in range(2):
                    dve.wait_ge(*step("grow", g, n))
                    dve.tensor_tensor(inv_t[g][:], bank(4 * g), wide(gc, n, g), ALU.subtract).then_inc(chunk_sem("differ", g), 1)
                    dve.wait_ge(*step("differ", g, n))
                    dve.tensor_scalar(inner[g][:], inv_t[g][:], 0.0, None, ALU.max)
                    dve.tensor_scalar(qk[g][:], inv_t[g][:], 0.0, None, ALU.min).then_inc(chunk_sem("differences", g), 1)
                for g in range(2):
                    dve.wait_ge(*step("k_turned", g, n))
                    dve.tensor_tensor(kbg[g][:], bank(4 * g + 3), wide(begc, n, g), ALU.mult)
                    dve.tensor_tensor(kdec[g][:], bank(4 * g + 3), wide(dgc, n, g), ALU.mult).then_inc(chunk_sem("k_rows", g), 1)
                    dve.wait_ge(*step("v_turned", g, n))
                    dve.tensor_tensor(vb[g][:], bank(4 * g), wide(beta, n, g), ALU.mult).then_inc(chunk_sem("v_rows", g), 1)
                for g in range(2):
                    dve.wait_ge(*step("kk_ready", g, n))
                    dve.wait_ge(*step("inner_beta", g, n))
                    dve.tensor_tensor(inner[g][:], bank(4 * g + 1), inner[g][:], ALU.mult).then_inc(chunk_sem("inner", g), 1)
                    dve.wait_ge(*step("qk_ready", g, n))
                    dve.wait_ge(*step("qk_mask", g, n))
                    dve.tensor_tensor(qk[g][:], bank(4 * g + 2), qk[g][:], ALU.mult).then_inc(chunk_sem("qk", g), 1)
                eye = ident[:].rearrange("p (a j) -> p a j", a=1).to_broadcast([P, HG, P])
                for l in range(LEVELS):
                    mask = blocks_mask[:, l].rearrange("p (a j) -> p a j", a=1).to_broadcast([P, HG, P])
                    for g in range(2):
                        dve.wait_ge(*step(f"half_ready{l}", g, n))
                        dve.tensor_tensor(half_t[g][:], bank(4 * g), mask, ALU.mult).then_inc(chunk_sem(f"half{l}", g), 1)
                    for g in range(2):
                        dve.wait_ge(*step(f"inv_t_ready{l}", g, n))
                        dve.tensor_tensor(inv_t[g][:], bank(4 * g + 1), inv_t[g][:] if l else eye, ALU.add).then_inc(chunk_sem(f"inv_t{l}", g), 1)
                        if l < LEVELS - 1:
                            dve.wait_ge(*step(f"inv_ready{l}", g, n))
                            dve.tensor_tensor(inv[g][:], bank(4 * g + 2), inv[g][:] if l else eye, ALU.add).then_inc(chunk_sem(f"inv{l}", g), 1)
                for g in range(2):
                    dve.wait_ge(*step("S_ready", g, n))
                    for h in range(HG):
                        ins = dve.scalar_tensor_tensor(S[g][:, h], S[g][:, h], glast[:, bass.ds(n * H + (g * HG + h), 1)],
                                                       ps[:, 4 * g + 2, h * P:(h + 1) * P], ALU.mult, ALU.add)
                    ins.then_inc(chunk_sem("S_done", g), 1)
            loop(dve, 0, TT, chunk)

            for k, dst in enumerate((s_q, s_k, s_v)):
                src = qkv[:].rearrange("p (c t) -> p t c", t=T)[:, SEQ:T, k * H:(k + 1) * H]
                dve.tensor_copy(dst[:].rearrange("p (b h) -> p b h", h=H), src).then_inc(sem("s_cols"), 1)
            dve.tensor_copy(s_z[:].rearrange("p (b h) -> p b h", h=H), z[:].rearrange("p (c t) -> p t c", t=T)[:, SEQ:T, :]).then_inc(sem("s_cols"), 1)
            for k, t in enumerate((beta, gate)):
                v = t[0:B, TT * H:(TT + 1) * H].rearrange("p (a h) -> p a h", a=1).to_broadcast([B, B, H])
                e = ident[0:B, 0:B].rearrange("p (b a) -> p b a", a=1).to_broadcast([B, B, H])
                ins = dve.tensor_tensor(s_wide[0:B, k].rearrange("p (b h) -> p b h", h=H), v, e, ALU.mult)
            ins.then_inc(sem("s_wide"), 1)
            dve.wait_ge(*after("o_squares", 1))
            link(dve.tensor_reduce(o_ms[:], o_squares[:], AX_X, ALU.add))
            dve.tensor_scalar(o_ms[:], o_ms[:], 1.0 / P, EPS, ALU.mult, ALU.add).then_inc(sem("o_ms"), 1)
            dve.wait_ge(*after("s_bg_wide", 1))
            dve.wait_ge(*after("s_cols", 4))
            link(dve.tensor_tensor(s_wq[:, :, 0], s_k[:], s_bg[:, 0], ALU.mult))
            link(dve.tensor_copy(s_wq[:, :, 1], s_q[:]))
            link(dve.tensor_tensor(s_v[:], s_v[:], s_bg[:, 0], ALU.mult))
            dve.tensor_tensor(s_t[:], s_q[:], s_k[:], ALU.mult).then_inc(sem("s_products"), 1)
            dve.wait_ge(*after("o_root", 1))
            link(dve.reciprocal(o_root[:], o_root[:]))
            o4 = qkv[:].rearrange("p (c t) -> p c t", t=T)
            for h in range(H):
                ins = dve.tensor_tensor(o4[:, 2 * H + h, 0:SEQ].rearrange("p (n v) -> p n v", v=P),
                                        o4[:, 2 * H + h, 0:SEQ].rearrange("p (n v) -> p n v", v=P),
                                        o_root[:, h * TT:(h + 1) * TT].rearrange("p (n a) -> p n a", a=1).to_broadcast([P, TT, P]), ALU.mult)
                ins.then_inc(sem("o_normed"), 1)
            norm_w = par[:, MISC["gdn_norm_w"]:MISC["gdn_norm_w"] + 1]
            for h in range(H):
                dve.wait_ge(*after("o_turned", h + 1))
                dve.scalar_tensor_tensor(z[:, h * T:h * T + SEQ], ps[:, 2 + h % 2, :], norm_w, z[:, h * T:h * T + SEQ],
                                         ALU.mult, ALU.mult).then_inc(sem("o_done"), 1)
            dve.wait_ge(*after("s_qk_ready", 1))
            link(dve.tensor_copy(s_qk[:], ps[:, 1, 0:BH]))
            dve.wait_ge(*after("s_wS", 1))
            wS = ps[:, 4, 0:2 * BH].rearrange("p (m t) -> p m t", t=2)
            link(dve.tensor_tensor(s_new[:], s_v[:], wS[:, :, 0], ALU.subtract))
            dve.nop().then_inc(sem("s_new"), 1)
            link(dve.tensor_tensor(s_o[:], s_qk[:], s_new[:], ALU.mult))
            link(dve.tensor_tensor(s_o[:], s_o[:], wS[:, :, 1], ALU.add))
            dve.tensor_tensor(s_t[:], s_o[:], s_o[:], ALU.mult).then_inc(sem("s_o_squares"), 1)
            dve.wait_ge(*after("s_rows_ready", 1))
            dve.tensor_copy(s_rows[0:BH], ps[0:BH, 6, 0:2 * P].rearrange("p (k v) -> p k v", k=2)).then_inc(sem("s_rows"), 1)
            dve.wait_ge(*after("s_o_summed", 1))
            dve.tensor_scalar(s_t[:], ps[:, 5, 0:BH], 1.0 / P, EPS, ALU.mult, ALU.add).then_inc(sem("s_var"), 1)
            dve.wait_ge(*after("s_root", 1))
            link(dve.reciprocal(s_t[:], s_t[:]))
            link(dve.scalar_tensor_tensor(s_o[:], s_o[:], norm_w, s_t[:], ALU.mult, ALU.mult))
            dve.tensor_tensor(z[:].rearrange("p (c t) -> p t c", t=T)[:, SEQ:T, :], s_o[:].rearrange("p (b h) -> p b h", h=H),
                              s_z[:].rearrange("p (b h) -> p b h", h=H), ALU.mult).then_inc(sem("s_o_done"), 1)
            dve.wait_ge(*after("s_rows", 1))
            for k in range(BH // SD):
                if k >= 2:
                    dve.wait_ge(*after("s_outer", (k - 1) * SD // 4))
                dve.tensor_tensor(s_diag[k % 2][0:BH], s_rows[0:BH, 0:1].to_broadcast([BH, SD, P]),
                                  ident[0:BH, k * SD:(k + 1) * SD].rearrange("p (m a) -> p m a", a=1).to_broadcast([BH, SD, P]),
                                  ALU.mult).then_inc(sem("s_diag"), 1)
                for m in range(SD // 4):
                    u = k * (SD // 4) + m
                    dve.wait_ge(*after("s_outer", u + 1))
                    dve.tensor_tensor(s_S[:, 4 * u:4 * u + 4], ps[:, u % 4, :].rearrange("p (m v) -> p m v", v=P),
                                      s_S[:, 4 * u:4 * u + 4], ALU.add).then_inc(sem("s_S_new"), 1)
            for k in range(2):
                dve.wait_ge(*after("h_turned", k + 1))
                dve.tensor_copy(h_rows[0:B + 1, k * 512:(k + 1) * 512], ps[0:B + 1, 4 + k, :]).then_inc(sem("h_rows"), 1)
            halves = [(gy, 0), (gy, 1), (z, 0), (z, 1)]
            for k, (src, part) in enumerate(halves):
                dve.wait_ge(*after("mixed_high", k + 1))
                dve.tensor_tensor(x_low[:, 4 * k:4 * k + 4], src[:, part * 4 * T:(part + 1) * 4 * T].rearrange("p (c t) -> p c t", t=T),
                                  x_high[:, 4 * k:4 * k + 4].bitcast(F32), ALU.subtract).then_inc(sem("mixed_low"), 1)

            def two(t):
                return t.rearrange("p (h t) -> p h t", h=2)

            def rstd(r):
                dve.wait_ge(sem("summed"), r + 1)
                dve.tensor_scalar(two(ssum[:]), ps[:, 0:2, 0:HALF], 1.0 / D, EPS, ALU.mult, ALU.add).then_inc(sem("mean"), 1)
                dve.wait_ge(sem("rooted"), r + 1)
                link(dve.reciprocal(ssum[:], ssum[:]))

            def residual(r, post, pre):
                rstd(2 * r)
                if r:
                    dve.wait_ge(sem("x_back"), 16 * r)
                else:
                    dve.wait_ge(*after("x_turns_taken", TT * 4 + 1))
                for c in range(NC):
                    if c >= 2:
                        dve.wait_ge(sem("x_new"), r * NC + c - 1)
                    dve.scalar_tensor_tensor(xw[:, c % 2], branch[:, c], par[:, NORM[post] + c:NORM[post] + c + 1], ssum[:],
                                             ALU.mult, ALU.mult).then_inc(sem("post"), 1)
                    dve.wait_ge(sem("post"), r * NC + c + 1)
                    dve.tensor_tensor(xt[:, c], xt[:, c], xw[:, c % 2], ALU.add).then_inc(sem("x_new"), 1)
                if pre is None:
                    return
                dve.wait_ge(sem("x_new"), r * NC + NC)
                rstd(2 * r + 1)
                for c in range(NC):
                    if c >= 2:
                        dve.wait_ge(sem("norm_low"), r * NC + c - 1)
                    dve.scalar_tensor_tensor(xw[:, c % 2], xt[:, c], par[:, NORM[pre] + c:NORM[pre] + c + 1], ssum[:],
                                             ALU.mult, ALU.mult).then_inc(sem("x_weighed"), 1)
                    if c >= 1:
                        low(r, c - 1)
                low(r, NC - 1)

            def low(r, c):
                dve.wait_ge(sem("norm_high"), r * NC + c + 1)
                dve.tensor_tensor(x_low[:, c], xw[:, c % 2], x_high[:, c].bitcast(F32), ALU.subtract).then_inc(sem("norm_low"), 1)

            gemm(g_out, nothing)
            residual(0, "norm_mix_post", "norm_xa_pre")
            gemm(g_q, nothing)

            def row_max(h, t):
                if t % 2:
                    return
                n = h * TT + t
                dve.wait_ge(sem("scores"), n // 2 + 1)
                link(dve.tensor_reduce(stats[:, 0, n:n + 2], ps[:, h % 2 * 2 + t // 2, :].rearrange("p (t m) -> p t m", t=2), AX_X, ALU.max))
                dve.tensor_scalar(stats[:, 0, n:n + 2], stats[:, 0, n:n + 2], -SCALE, None, ALU.mult).then_inc(sem("row_max"), 1)

            def normalize(h, t):
                n = h * TT + t
                dve.wait_ge(sem("exponentials"), n + 1)
                link(dve.reciprocal(stats[:, 2, n:n + 1], stats[:, 1, n:n + 1]))
                dve.tensor_scalar(probs[:, t], probs[:, t], stats[:, 2, n:n + 1], None, ALU.mult).then_inc(sem("probs"), 1)

            def sample_scores(k):
                b, c = k // MT, k % MT
                dve.wait_ge(sem(f"cache{c}"), 16 * (b + 1))
                dve.wait_ge(sem(f"q_wide{b % 2}"), 16 * (b // 2 + 1))
                hd = D // XH_
                for h in range(XH_):
                    tile = cache[:, c, h * hd:(h + 1) * hd]
                    ins = dve.tensor_tensor_reduce(tile, tile, q_wide[b % 2][:, h * hd:(h + 1) * hd], 1.0, 0.0, ALU.mult, ALU.add,
                                                   s_scores[:, c, b * XH_ + h:b * XH_ + h + 1])
                ins.then_inc(sem("s_scored"), 1)

            dve.wait_ge(sem("x_mid"), 16)
            for t in range(TT):
                row_max(0, t)
                if t:
                    normalize(0, t - 1)
            normalize(0, TT - 1)
            for h in range(XH_):
                for t in range(TT):
                    if h + 1 < XH_:
                        row_max(h + 1, t)
                    sample_scores(h * TT + t)
                    n = h * DC + t
                    dve.wait_ge(sem("pv_high"), n + 1)
                    dve.tensor_tensor(x_low[:, n, 0:SEQ], ps[:, 6 + n % 2, :], x_high[:, n, 0:SEQ].bitcast(F32), ALU.subtract).then_inc(sem("pv_low"), 1)
                    if h + 1 < XH_:
                        normalize(h + 1, t)
            R = B * XH_
            dve.wait_ge(*after("s_turned", 1))
            link(dve.tensor_reduce(s_stats[0:R, 0:1], ps[0:R, 0, 0:M], AX_X, ALU.max))
            dve.tensor_scalar(s_stats[0:R, 1:2], s_stats[0:R, 0:1], -SCALE, None, ALU.mult).then_inc(sem("s_max"), 1)
            dve.wait_ge(*after("s_exp", 1))
            link(dve.reciprocal(s_stats[0:R, 3:4], s_stats[0:R, 2:3]))
            dve.tensor_scalar(s_probs[0:R], s_probs[0:R], s_stats[0:R, 3:4], None, ALU.mult).then_inc(sem("s_probs"), 1)
            dve.wait_ge(*after("s_probs_turned", 1))
            dve.wait_ge(*after("eye_b", 2))
            for c in range(MT):
                for b in range(B):
                    p = ps[:, 1, c * R + b * XH_:c * R + (b + 1) * XH_].rearrange("p (h a) -> p h a", a=1).to_broadcast([P, XH_, B])
                    e = eye_b[:, b:b + 1, :].to_broadcast([P, XH_, B])
                    ins = dve.tensor_tensor(spread[:, c, b], p, e, ALU.mult)
            ins.then_inc(sem("s_spread"), 1)
            dve.wait_ge(*after("s_o_high", 1))
            dve.tensor_tensor(x_low[:, :, SEQ:T], ps[:, 2, 0:NC * B].rearrange("p (c b) -> p c b", b=B),
                              x_high[:, :, SEQ:T].bitcast(F32), ALU.subtract).then_inc(sem("s_o_low"), 1)

            gemm(g_o, nothing)
            residual(1, "norm_xa_post", "norm_ffn_pre")

            for c0, n, g_up, g_down in ffn:
                def hidden(it, j, g=g_up, c0=c0):
                    chunk = it * 2 + j
                    b = g.acc(j) * 4
                    dve.wait_ge(sem("silu"), chunk + (c0 + 1))
                    dve.tensor_tensor(two(xw[:, j]), ps[:, b + 2:b + 4, 0:HALF], two(sq[:, j]), ALU.mult).then_inc(sem("acc_taken"), 1)
                    dve.wait_ge(sem("h_high"), chunk + (c0 + 1))
                    c = bass.ds(chunk * T, T)
                    dve.tensor_tensor(h_low[:].rearrange("p c t -> p (c t)")[:, c], xw[:, j],
                                      h_high[:].rearrange("p c t -> p (c t)")[:, c].bitcast(F32), ALU.subtract).then_inc(sem("h_low"), 1)

                def add_down(it, j, g=g_down, c0=c0):
                    b = g.acc(j) * 4
                    dve.wait_ge(sem("slab_used"), g.slab(it, (j + 1) * g.slabs - 1) + 1)
                    f = branch[:].rearrange("p c t -> p (c t)")
                    for m in range(2):
                        out = f[:, bass.ds((it * g.blocks + j) * (2 * T) + m * T, T)].rearrange("p (h t) -> p h t", h=2)
                        acc = ps[:, b + 2 * m:b + 2 * m + 2, 0:HALF]
                        if c0:
                            ins = dve.tensor_tensor(out, acc, out, ALU.add)
                        else:
                            ins = dve.tensor_copy(out, acc)
                    ins.then_inc(sem("acc_taken"), 1)
                gemm(g_up, hidden)
                gemm(g_down, add_down)
            residual(2, "norm_ffn_post", None)

        @block_.tensor
        def _(pe):
            pe.wait_ge(sem("consts"), 4)
            pe.wait_ge(sem("par_loaded"), 16 * (len(params) + 2 * (TAPS - 1) + 3))
            for k in range(3):
                ins = pe.transpose(ps[:, 0, k * P:k * P + PAR_ROWS[k]], par_rows[0:PAR_ROWS[k], k, :], ident[0:PAR_ROWS[k], 0:PAR_ROWS[k]])
            ins.then_inc(sem("small_turned"), 1)
            NS = B * (TAPS - 1)
            for c in range(LC):
                pe.transpose(ps[:, 1, c * NS:(c + 1) * NS], state_rows[0:NS, c * P:(c + 1) * P], ident[0:NS, 0:NS])
            for c in range(LC):
                ins = pe.transpose(ps[:, 1, LC * NS + c * B:LC * NS + (c + 1) * B], h0_rows[0:B, c * P:(c + 1) * P], ident[0:B, 0:B])
            ins.then_inc(sem("small_turned"), 1)
            for k in range(2):
                for c in range(GC // 2):
                    cc = LC + k * GC // 2 + c
                    ins = pe.transpose(ps[:, 2 + k, c * NS:(c + 1) * NS], state_rows[0:NS, cc * P:(cc + 1) * P], ident[0:NS, 0:NS])
                ins.then_inc(sem("small_turned"), 1)
            pe.wait_ge(sem("small_copied"), 4)
            for k, (t, c, per, n, to) in enumerate(turns):
                pe.wait_ge(sem("rows_scaled"), t + 1)
                if k >= TURN_BANKS:
                    pe.wait_ge(sem("turn_low"), k - TURN_BANKS + 1)
                for q in range(per):
                    ins = pe.transpose(ps[:, k % TURN_BANKS, q * n:(q + 1) * n], row_tiles[t][0][0:n, (c + q) * P:(c + q + 1) * P], ident[0:n, 0:n])
                ins.then_inc(sem("turned"), 1)
            pe.wait_ge(sem("turn_low"), len(turns))

            def gemm(g, m_chunks=2, ready=None):
                def body(it):
                    for j in range(g.blocks):
                        first = type(it) is int and g.block(it, j) < 2
                        if not first:
                            pe.wait_ge(sem("acc_taken"), g.block(it, j) - 1)
                        b = g.acc(j) * 4
                        for s in range(g.slabs):
                            jj = j * g.slabs + s
                            slot = (g.slab0 + jj) % SPLIT
                            pe.wait_ge(sem("w_low_ready"), g.slab(it, jj) + 1)
                            if ready:
                                pe.wait_ge(ready[0], ready[1] + min((s + 1) * ready[2], g.chunks))
                            for k in range(min(KS, g.chunks - s * KS)):
                                c = s * KS + k
                                for m in range(m_chunks):
                                    for n, (w, x) in enumerate(((w_high, g.high), (w_high, g.low), (w_low, g.high))):
                                        flags = dict(start=(c == 0 and n == 0), stop=(c == g.chunks - 1 and n == 2))
                                        wk = w[:, slot, k, m * P:(m + 1) * P]
                                        if g.memory:
                                            ins = pe.matmul(ps[:, b + 2 * m, 0:COLS], x[:, c, m * P:(m + 1) * P], w[:, slot, k, :], **flags)
                                        else:
                                            for h in range(2):
                                                ins = pe.matmul(ps[:, b + 2 * m + h, 0:HALF], wk, x[:, c, h * HALF:(h + 1) * HALF], **flags)
                            ins.then_inc(sem("slab_used"), 1)
                if g.name == first_gemm.name:
                    body(0)
                loop(pe, 1 if g.name == first_gemm.name else 0, g.iters, body)

            for g in (g_wk, g_wv, g_lx, g_ly, g_qkv, g_z, g_bg):
                gemm(g, 1 if g is g_bg else 2)
            for k in range(CC // 4):
                if k == 0:
                    pe.wait_ge(sem("acc_taken"), g_bg.block0)
                if k >= 4:
                    pe.wait_ge(*after("edge_copied", k - 3))
                for q in range(4):
                    ins = pe.transpose(ps[0:EDGE, 4 + k % 4, q * P:(q + 1) * P], edge[:, 4 * k + q, :], ident[:])
                ins.then_inc(sem("edge_turned"), 1)
            pe.wait_ge(sem("acc_taken"), g_bg.block0 + 1)
            for n in range(TT):
                pe.transpose(ps[:, 1, n * 40:(n + 1) * 40], bg_rows[0:40, n * P:(n + 1) * P], ident[0:40, 0:40])
            pe.transpose(ps[0:B, 1, TT * 40:TT * 40 + 40], bg_rows[0:40, SEQ:T], ident[0:40, 0:40]).then_inc(sem("bg_turned"), 1)
            pe.wait_ge(sem("lru_w_loaded"), 32)
            pe.wait_ge(*after("edge_copied", CC // 4))
            pe.wait_ge(*after("sp_abs", 1))
            for c in range(LC):
                if c >= 2:
                    pe.wait_ge(*after("gates", c - 1))
                for k in range(2):
                    for h in range(2):
                        ins = pe.matmul(ps[:, c % 2 * 4 + 2 * k + h, 0:HALF], lru_w[:, k, c, :],
                                        lx[:, c * T + h * HALF:c * T + (h + 1) * HALF], start=True, stop=True)
                ins.then_inc(sem("gates_ready"), 1)
            pe.wait_ge(*after("gates", LC))
            for c in range(2 * H):
                pe.wait_ge(sem("l2_squares"), c + 1)
                if c >= 2:
                    pe.wait_ge(sem("l2_roots"), c - 1)
                for h in range(2):
                    ins = pe.matmul(ps[:, c % 2 * 2 + h, 0:HALF], ones[:], squares[:, c % 2, h * HALF:(h + 1) * HALF], start=True, stop=True)
                ins.then_inc(sem("l2_summed"), 1)
            pe.wait_ge(*after("gdn_gate", 1))
            pe.wait_ge(sem("masks"), 2 + LEVELS)
            pe.matmul(ps[:, 4, 0:TT * H], upper[:], gate[:, 0:TT * H], start=True, stop=True)
            pe.matmul(ps[:, 4, TT * H:2 * TT * H], ones[:], gate[:, 0:TT * H], start=True, stop=True).then_inc(sem("gc_summed"), 1)
            pe.wait_ge(*after("gdn_small", 1))
            pe.wait_ge(*after("S_clear", 1))
            pe.wait_ge(sem("l2_roots"), 2 * H)
            pe.wait_ge(*after("normed", 2 * H))

            def heads(g):
                return ((h, slice(h * P, (h + 1) * P)) for h in range(HG))

            def chunk(n):
                later = type(n) is not int
                for g in range(2):
                    b = 4 * g
                    if later:
                        pe.wait_ge(*step("v_new", g, n - 1))
                    pe.wait_ge(*step("gate_wide", g, n))
                    pe.matmul(ps[:, b, :], ones[:], inv[g][:], start=True, stop=True).then_inc(chunk_sem("grow_ready", g), 1)
                    pe.wait_ge(*step("keys", g, n))
                    if later:
                        pe.wait_ge(*step("wt", g, n - 1))
                    for h, c in heads(g):
                        ins = pe.transpose(ps[:, b + 3, c], keys[g][:, h], ident[:])
                    ins.then_inc(chunk_sem("k_turned", g), 1)
                    if later:
                        pe.wait_ge(*step("o_taken", g, n - 1))
                    for h, c in heads(g):
                        ins = pe.matmul(ps[:, b + 1, c], keys[g][:, h], keys[g][:, h], start=True, stop=True)
                    ins.then_inc(chunk_sem("kk_ready", g), 1)
                    if later:
                        pe.wait_ge(*step("S_done", g, n - 1))
                    for h, c in heads(g):
                        q = qkv[:, bass.ds(n * P + (g * HG + h) * T, P)]
                        ins = pe.matmul(ps[:, b + 2, c], keys[g][:, h], q, start=True, stop=True)
                    ins.then_inc(chunk_sem("qk_ready", g), 1)
                for g in range(2):
                    b = 4 * g
                    pe.wait_ge(*step("values", g, n))
                    pe.wait_ge(*step("differences", g, n))
                    pe.wait_ge(*step("grow", g, n))
                    for h, c in heads(g):
                        ins = pe.transpose(ps[:, b, c], values[g][:, h], ident[:])
                    ins.then_inc(chunk_sem("v_turned", g), 1)
                for l in range(LEVELS):
                    for g in range(2):
                        b = 4 * g
                        if l == 0:
                            pe.wait_ge(*step("v_rows", g, n))
                            pe.wait_ge(*step("inner", g, n))
                        else:
                            pe.wait_ge(*step(f"inv_t{l - 1}", g, n))
                        for h, c in heads(g):
                            ins = pe.matmul(ps[:, b, c], inner[g][:, h], inv_t[g][:, h] if l else ident[:], start=True, stop=True)
                        ins.then_inc(chunk_sem(f"half_ready{l}", g), 1)
                    for g in range(2):
                        b = 4 * g
                        if l:
                            pe.wait_ge(*step(f"inv{l - 1}", g, n))
                        pe.wait_ge(*step(f"half{l}", g, n))
                        for h, c in heads(g):
                            ins = pe.matmul(ps[:, b + 1, c], inv[g][:, h] if l else ident[:], half_t[g][:, h], start=True, stop=True)
                        ins.then_inc(chunk_sem(f"inv_t_ready{l}", g), 1)
                        if l < LEVELS - 1:
                            if l == 0:
                                pe.wait_ge(*step("qk", g, n))
                            for h, c in heads(g):
                                ins = pe.matmul(ps[:, b + 2, c], half_t[g][:, h], inv[g][:, h] if l else ident[:], start=True, stop=True)
                            ins.then_inc(chunk_sem(f"inv_ready{l}", g), 1)
                for g in range(2):
                    b = 4 * g
                    pe.wait_ge(*step(f"inv_t{LEVELS - 1}", g, n))
                    pe.wait_ge(*step("k_rows", g, n))
                    for h, c in heads(g):
                        ins = pe.matmul(ps[:, b + 3, c], kbg[g][:, h], inv_t[g][:, h], start=True, stop=True)
                    ins.then_inc(chunk_sem("wt_ready", g), 1)
                for g in range(2):
                    b = 4 * g
                    pe.wait_ge(*step("wt", g, n))
                    if later:
                        pe.wait_ge(*step("S_done", g, n - 1))
                    for h, c in heads(g):
                        pe.matmul(ps[:, b, c], inv_t[g][:, h], vb[g][:, h], start=True, stop=False)
                        ins = pe.matmul(ps[:, b, c], kbg[g][:, h], S[g][:, h], start=False, stop=True)
                    ins.then_inc(chunk_sem("v_new_ready", g), 1)
                for g in range(2):
                    b = 4 * g
                    pe.wait_ge(*step("v_new", g, n))
                    pe.wait_ge(*step("q_scaled", g, n))
                    for h, c in heads(g):
                        pe.matmul(ps[:, b + 1, c], grow[g][:, h], S[g][:, h], start=True, stop=False)
                        ins = pe.matmul(ps[:, b + 1, c], qk[g][:, h], vb[g][:, h], start=False, stop=True)
                    ins.then_inc(chunk_sem("o_ready", g), 1)
                    for h, c in heads(g):
                        ins = pe.matmul(ps[:, b + 2, c], kdec[g][:, h], vb[g][:, h], start=True, stop=True)
                    ins.then_inc(chunk_sem("S_ready", g), 1)
            chunk(0)
            loop(pe, 1, TT, chunk)

            pe.wait_ge(*after("s_wide", 1))
            pe.wait_ge(*step("v_new", 0, TT - 1))
            pe.matmul(ps[:, 0, 0:2 * BH], ones[0:B, :], s_wide[0:B].rearrange("p k m -> p (k m)"), start=True, stop=True).then_inc(sem("s_wide_ready"), 1)
            pe.wait_ge(*after("s_products", 1))
            pe.wait_ge(*step("o_taken", 0, TT - 1))
            pe.matmul(ps[:, 1, 0:BH], ones[:], s_t[:], start=True, stop=True).then_inc(sem("s_qk_ready"), 1)
            for g in range(2):
                pe.wait_ge(*step("S_done", g, TT - 1))
            for h in range(H):
                pe.wait_ge(*after("o_normed", h + 1))
                if h >= 2:
                    pe.wait_ge(*after("o_done", h - 1))
                for n in range(TT):
                    c = (2 * H + h) * T + n * P
                    ins = pe.transpose(ps[:, 2 + h % 2, n * P:(n + 1) * P], qkv[:, c:c + P], ident[:])
                ins.then_inc(sem("o_turned"), 1)
            pe.wait_ge(*step("v_new", 1, TT - 1))
            pe.wait_ge(*step("o_taken", 1, TT - 1))
            pe.wait_ge(*after("s_decayed", 1))
            for m in range(BH):
                ins = pe.matmul(ps[:, 4, 2 * m:2 * m + 2], s_S[:, m, :], s_wq[:, m, :], start=True, stop=True)
            ins.then_inc(sem("s_wS"), 1)
            pe.wait_ge(*after("s_new", 1))
            pe.transpose(ps[0:BH, 6, 0:P], s_new[:], ident[:])
            pe.transpose(ps[0:BH, 6, P:2 * P], s_k[:], ident[:]).then_inc(sem("s_rows_ready"), 1)
            pe.wait_ge(*after("s_o_squares", 1))
            pe.matmul(ps[:, 5, 0:BH], ones[:], s_t[:], start=True, stop=True).then_inc(sem("s_o_summed"), 1)
            pe.wait_ge(*after("o_done", H))
            pe.wait_ge(*after("s_new", 1))
            for u in range(BH // 4):
                pe.wait_ge(sem("s_diag"), u * 4 // SD + 1)
                if u >= 4:
                    pe.wait_ge(sem("s_S_new"), u - 3)
                d = s_diag[u * 4 // SD % 2]
                m = u * 4 % SD
                pe.matmul(ps[:, u % 4, :], s_rows[0:BH, 1], d[0:BH, m:m + 4], start=True, stop=True).then_inc(sem("s_outer"), 1)
            pe.wait_ge(*after("s_var", 1))
            hx = lx[:].rearrange("p (c t) -> p c t", t=T)
            for k in range(2):
                for q in range(4):
                    ins = pe.transpose(ps[0:B + 1, 4 + k, q * P:(q + 1) * P], hx[:, 4 * k + q, SEQ - 1:T], ident[:])
                ins.then_inc(sem("h_turned"), 1)

            def summed(r):
                for h in range(2):
                    ins = pe.matmul(ps[:, h, 0:HALF], ones[:], ssum[:, h * HALF:(h + 1) * HALF], start=True, stop=True)
                ins.then_inc(sem("summed"), 1)

            def residual_sums(r):
                pe.wait_ge(sem("acc_taken"), (g_out, g_o, ffn[-1][3])[r].block0 + DB)
                pe.wait_ge(sem("sq"), (r + 1) * 3 * DB)
                summed(2 * r)

            gemm(g_out, ready=(*after("mixed_low", 0), 1))
            pe.wait_ge(sem("acc_taken"), g_out.block0 + DB)
            pe.wait_ge(sem("x_rows"), 32)
            for t in range(TT + 1):
                rows, n, per = (x_rows2[:, t], P, 4) if t < TT else (xs_rows2[0:B], B, NC)
                for c in range(0, NC, per):
                    k = t * 4 + c // per
                    if k >= 4:
                        pe.wait_ge(*after("x_turns_taken", k - 3))
                    for q in range(per):
                        ins = pe.transpose(ps[:, 4 + k % 4, q * n:(q + 1) * n], rows[:, (c + q) * P:(c + q + 1) * P], ident[0:n, 0:n])
                    ins.then_inc(sem("x_turned"), 1)
            pe.wait_ge(sem("sq"), 3 * DB)
            summed(0)
            pe.wait_ge(sem("kv_rows"), 16)
            pe.wait_ge(*after("x_turns_taken", TT * 4 + 1))
            for k in range(NC // 2):
                if k >= 4:
                    pe.wait_ge(*after("k_t", k - 3))
                for q in range(2):
                    for m in range(MT):
                        c = 2 * k + q
                        ins = pe.transpose(ps[:, 4 + k % 4, q * M + m * P:q * M + (m + 1) * P], kv_rows[:, m, c * P:(c + 1) * P], ident[:])
                ins.then_inc(sem("k_t_turned"), 1)

            def new_x_squares(r):
                pe.wait_ge(sem("mean"), 2 * r + 1)
                for c in range(NC):
                    pe.wait_ge(sem("x_squares"), r * NC + c + 1)
                    for h in range(2):
                        ins = pe.matmul(ps[:, h, 0:HALF], ones[:], sq[:, c % 2, h * HALF:(h + 1) * HALF], start=c == 0, stop=c == NC - 1)
                        if h and c < NC - 1:
                            ins.then_inc(sem("x_summed"), 1)
                ins.then_inc(sem("summed"), 1)

            new_x_squares(0)
            gemm(g_q, ready=(sem("norm_low"), 0, KS))

            pe.wait_ge(sem("acc_taken"), g_q.block0 + DB)
            for k in range(XH_):
                for q in range(4):
                    ins = pe.transpose(ps[0:B, 4 + k, q * P:(q + 1) * P], q_t[:, 4 * k + q, SEQ:T], ident[:])
                ins.then_inc(sem("qs_turned"), 1)

            def scores(h):
                for pair in range(2):
                    if h >= 2:
                        pe.wait_ge(sem("exponentials"), (h - 2) * TT + 2 * pair + 2)
                    for t in (2 * pair, 2 * pair + 1):
                        for c in range(DC):
                            ins = pe.matmul(ps[:, h % 2 * 2 + pair, t % 2 * M:(t % 2 + 1) * M], q_t[:, h * DC + c, t * P:(t + 1) * P],
                                            k_t[:, h * DC + c, :], start=c == 0, stop=c == DC - 1)
                    ins.then_inc(sem("scores"), 1)

            scores(0)
            scores(1)
            pe.wait_ge(*after("qs_rows", XH_))
            pe.wait_ge(sem("kv_rows"), 32)
            for h in range(XH_):
                pe.wait_ge(sem("probs"), (h + 1) * TT)
                if h:
                    pe.wait_ge(sem("probs_t"), h)
                for t in range(TT):
                    for m in range(MT):
                        ins = pe.transpose(ps[:, 4 + t // 2, (t % 2 * MT + m) * P:(t % 2 * MT + m + 1) * P], probs[:, t, m * P:(m + 1) * P], ident[:])
                ins.then_inc(sem("probs_turned"), 1)
                pe.wait_ge(sem("probs_t"), h + 1)
                for c in range(DC):
                    n = h * DC + c
                    if n >= 2:
                        pe.wait_ge(sem("pv_low"), n - 1)
                    for m in range(MT):
                        ins = pe.matmul(ps[:, 6 + n % 2, :], kv_rows[:, m, n * P:(n + 1) * P], probs_t[:, m, :], start=m == 0, stop=m == MT - 1)
                    ins.then_inc(sem("pv_ready"), 1)
                if h + 2 < XH_:
                    scores(h + 2)
            R = B * XH_
            pe.wait_ge(sem("s_scored"), B * MT)
            pe.wait_ge(sem("exponentials"), XH_ * TT)
            for m in range(MT):
                ins = pe.transpose(ps[0:R, 0, m * P:(m + 1) * P], s_scores[:, m, :], ident[:])
            ins.then_inc(sem("s_turned"), 1)
            pe.wait_ge(*after("s_probs", 1))
            for m in range(MT):
                ins = pe.transpose(ps[:, 1, m * R:(m + 1) * R], s_probs[0:R, m * P:(m + 1) * P], ident[0:R, 0:R])
            ins.then_inc(sem("s_probs_turned"), 1)
            pe.wait_ge(*after("s_spread", 1))
            pe.wait_ge(sem("probs_t"), XH_)
            pe.wait_ge(sem("pv_low"), NC)
            for k in range(B * MT):
                b, m = k // MT, k % MT
                pe.wait_ge(sem(f"values_in{k % 3}"), 16 * (k // 3 + 1))
                for h in range(XH_):
                    ins = pe.matmul(ps[0:B, 4 + h, :], spread[:, m, b, h, :], cache[:, k % 3, h * DC * P:(h + 1) * DC * P],
                                    start=k == 0, stop=k == B * MT - 1)
                ins.then_inc(sem("s_valued"), 1)
            pe.wait_ge(*after("os_rows", 1))
            for c in range(NC):
                ins = pe.transpose(ps[:, 2, c * B:(c + 1) * B], os_rows[0:B, c * P:(c + 1) * P], ident[0:B, 0:B])
            ins.then_inc(sem("os_turned"), 1)
            pe.wait_ge(*after("s_o_low", 1))

            gemm(g_o)
            residual_sums(1)
            new_x_squares(1)
            for c0, n, g_up, g_down in ffn:
                gemm(g_up, ready=(sem("norm_low"), NC, KS) if c0 == 0 else None)
                gemm(g_down, ready=(sem("h_low"), c0, KS))
            residual_sums(2)
            for t in range(TT + 1):
                rows = P if t < TT else B
                for q in range(4):
                    k = t * 4 + q
                    pe.wait_ge(sem("x_new"), 2 * NC + 4 * q + 4)
                    if k >= 8:
                        pe.wait_ge(*after("y_copied", k - 7))
                    for c in range(4):
                        ins = pe.transpose(ps[0:rows, k % 8, c * P:(c + 1) * P], xt[:, 4 * q + c, t * P:t * P + rows], ident[:])
                    ins.then_inc(sem("y_turned"), 1)


def kernel(**inputs):
    import numpy as np
    import concourse.bacc as bacc
    from concourse import mybir as mb
    from concourse.bass_utils import run_bass_kernel_spmd

    x, xs, mem = (inputs[n].shape for n in ("x_prompt", "x_sample", "mem_prompt"))
    k, s = inputs["cache_mem_k"].shape, inputs["state_gdn_S"].shape
    lc, lh, gc = (inputs[n].shape for n in ("state_lru_conv", "state_lru_h", "state_gdn_conv"))
    b = x[0]
    outs = {
        "y_prompt": x, "y_sample": xs,
        "p_lru_conv": (lc[0], b) + lc[2:], "p_lru_h": (lh[0], b) + lh[2:], "p_gdn_conv": (gc[0], b) + gc[2:],
        "p_gdn_S": (s[0], b) + s[2:], "p_mem_k": (k[0], b) + k[2:], "p_mem_v": (k[0], b) + k[2:],
        "s_lru_conv": lc, "s_lru_h": lh, "s_gdn_conv": gc, "s_gdn_S": s,
    }
    nc = bacc.Bacc("TRN2", target_bir_lowering=False, num_devices=1)
    arrays = {f"in_{n}": np.ascontiguousarray(a) for n, a in inputs.items()}
    ins = {n: nc.dram_tensor(f"in_{n}", a.shape, mb.dt.from_np(a.dtype), kind="ExternalInput").ap()
           for n, a in ((n, arrays[f"in_{n}"]) for n in inputs)}
    results = {n: nc.dram_tensor(f"out_{n}", shape, mb.dt.float32, kind="ExternalOutput").ap() for n, shape in outs.items()}
    build(nc, ins, results)
    r = run_bass_kernel_spmd(nc, [arrays], core_ids=[0])
    return tuple(r.results[0][f"out_{n}"] for n in outs)
```

```python
from contextlib import ExitStack

import concourse.bass as bass
from concourse import mybir
from concourse.alu_op_type import AluOpType as ALU

ACT = mybir.ActivationFunctionType
AX_X = mybir.AxisListType.X
F32 = mybir.dt.float32
F32R = mybir.dt.float32r
P = 128
EPS = 1e-6
KS = 4
COLS = 256
RAW = 4
SPLIT = 2


class Gemm:

    def __init__(self, name, sources, iters, blocks, slabs, chunks, high, low, memory=False):
        self.name, self.sources, self.iters, self.blocks, self.slabs = name, sources, iters, blocks, slabs
        self.chunks, self.high, self.low, self.memory = chunks, high, low, memory

    def slab(self, it, jj):
        return it * (self.blocks * self.slabs) + (self.slab0 + jj)

    def block(self, it, j):
        return it * self.blocks + (self.block0 + j)

    def loads(self, it, jj):
        return it * (self.blocks * self.slabs // RAW) + ((self.slab0 + jj) // RAW + 1)

    def acc(self, j):
        return (self.block0 + j) % 2


def loop(engine, first, end, body):
    if end - first == 1:
        body(first)
    elif end > first:
        with engine.Fori(first, end) as i:
            body(i)


def build(nc, i, o):
    D = i["w_out"].shape[2]
    SEQ = i["x_prompt"].shape[1]
    B = i["x_sample"].shape[0]
    T = SEQ + B
    HALF = T // 2
    NC = D // P
    W = i["lru_lambda"].shape[1]
    LC = W // P
    H = i["gdn_A_log"].shape[1]
    QKV = i["gdn_conv_w"].shape[2]
    GC = QKV // P
    CC = LC + GC
    M = i["mem_prompt"].shape[1]
    MT = M // P
    TT = SEQ // P
    FF = i["ffn_w_up"].shape[2] // P
    TAPS = i["lru_conv_w"].shape[1]
    PADDED = TAPS - 1 + SEQ + TAPS * B
    CONVED = PADDED - TAPS + 1
    S0 = TAPS - 1 + SEQ
    EDGE = TAPS - 1 + B
    assert D % 1024 == 0 and T % 4 == 0 and HALF <= 512 and M == COLS and H == LC == TT * 2

    norm_names = ["norm_mix_pre", "norm_mix_post", "norm_xa_pre", "norm_xa_post", "norm_mem", "norm_ffn_pre", "norm_ffn_post"]
    NORM = {n: k * NC for k, n in enumerate(norm_names)}
    CONV0 = len(norm_names) * NC
    MISC0 = CONV0 + TAPS * CC
    misc_names = ["lru_conv_b", "lru_gate_x_b", "lru_gate_a_b", "lru_lambda"]
    MISC = {n: MISC0 + k * LC for k, n in enumerate(misc_names)}
    MISC["gdn_norm_w"] = MISC0 + len(misc_names) * LC
    NPAR = MISC["gdn_norm_w"] + 1

    with ExitStack() as ctx:
        def sb(name, shape, dt=F32):
            return ctx.enter_context(nc.sbuf_tensor(name, shape, dt))

        sems = {}

        NB = B * H // 4
        XT = SEQ // P * 4 + 1
        SEQUENCES = {
            "scalar": [("sp_exp", 2), ("beta", 1), ("gates", LC), 
                       ("l2_squares", 2 * H), ("l2_root", 1), ("lru_tanh", 1), ("lru_sqrt", 1), ("s_bg_wide", 1), ("s_root", 1), ("gc_exps", 3), ("o_root", 1), ("mixed_high", 4), ("x_turns_taken", XT),
                       ("qs_rows", 4), ("k_t", NC // 2), ("s_exp", 1), ("os_rows", 1), ("s_o_high", 1), ("y_copied", XT + 3)],
            "vector": [("edge_copied", CC // 4), ("sp_abs", 1), ("lru_rate", 1), ("gdn_gate", 1), ("log_a", 1),
                       ("head_row", 1), ("l2_inverse", 1), ("normed", 2 * H), ("s_cols", 4), ("s_wide", 1), ("s_products", 1), ("lru_scanned", 1), ("s_new", 1),
                       ("s_o_squares", 1), ("s_rows", 1), ("s_var", 1), ("s_o_done", 1), ("gc_ready", 1), ("gdn_small", 1),
                       ("S_clear", 1), ("h_rows", 2), ("o_ms", 1), ("o_normed", H), ("o_done", H), ("s_max", 1),
                       ("s_probs", 1), ("s_spread", 1), ("s_o_low", 1)],
            "tensor": [("small_turned", 4), ("edge_turned", CC // 4), ("bg_turned", 1), ("gates_ready", LC), ("l2_summed", 2 * H),
                       ("l2_wide", 2 * H), ("s_wide_ready", 1), ("s_qk_ready", 1), ("s_wS", 1), ("s_rows_ready", 1),
                       ("s_o_summed", 1), ("s_outer", NB), ("gc_summed", 1), ("h_turned", 2), ("o_turned", H), ("x_turned", XT), ("qs_turned", 4), ("k_t_turned", NC // 2),
                       ("s_turned", 1), ("s_probs_turned", 1), ("s_valued", B * MT), ("os_turned", 1),
                       ("y_turned", XT + 3)],
            "pool": [("gated_x", 1), ("lru_out", 1), ("eye_b", 2)],
        }
        IN_SEQUENCE = {n: (f"{e}_steps", sum(c for _, c in steps[:k]))
                       for e, steps in SEQUENCES.items() for k, (n, _) in enumerate(steps)}

        def after(name, count):
            return sem(name), IN_SEQUENCE[name][1] + count

        def sem(name):
            name = IN_SEQUENCE.get(name, (name, 0))[0]
            if name not in sems:
                sems[name] = ctx.enter_context(nc.semaphore(name))
            return sems[name]

        ident = sb("ident", [P, P])
        ones = sb("ones", [P, P])
        par = sb("par", [P, NPAR])
        small = sb("small", [P, 4, 8])
        eps_col = sb("eps_col", [P, 1])
        ssq, ms, root, rstd_rows = (small[:, k] for k in range(4))
        row_groups = [(0, MT), (MT, MT + TT + 1)]
        CH = NC * T * 4
        CONV = (nc.sbuf_base + 31) // 32 * 32
        CONVED0 = CONV + (2 * PADDED * 4 + 31) // 32 * 32
        STATE0 = CONVED0 + (CONVED * 4 + 31) // 32 * 32
        HZERO0 = (STATE0 + 4 * CC * B * (TAPS - 1) + 31) // 32 * 32
        EDGE0 = (HZERO0 + 4 * LC * B + 31) // 32 * 32
        arena0 = (EDGE0 + 4 * CC * EDGE + 31) // 32 * 32
        XH, XL, H0, H1, M0, W0 = (arena0 + k * CH for k in range(6))
        SLAB = KS * COLS * 4

        def at(name, shape, dt, offset):
            return nc.alloc_sbuf_tensor_at(name, shape, dt, offset=offset)

        xpad = at("xpad", [P, 2, PADDED], F32, CONV)
        conved = at("conved", [P, CONVED], F32, CONVED0)
        conv_state = at("conv_state", [P, CC, B * (TAPS - 1)], F32, STATE0)
        h0 = at("h0", [P, LC, B], F32, HZERO0)
        edge = at("edge", [P, CC, EDGE], F32, EDGE0)
        w_raw = at("w_raw", [P, RAW, KS, COLS], F32, W0)
        w_high = at("w_high", [P, SPLIT, KS, COLS], F32R, W0 + RAW * SLAB)
        w_low = at("w_low", [P, SPLIT, KS, COLS], F32R, W0 + (RAW + SPLIT) * SLAB)
        x_high = at("x_high", [P, NC, T], F32R, XH)
        x_low = at("x_low", [P, NC, T], F32R, XL)
        mem_high = at("mem_high", [P, NC, M], F32R, H0)
        mem_low = at("mem_low", [P, NC, M], F32R, H0 + NC * M * 4)
        x_rows = at("x_rows", [P, TT, D], F32, H1)
        mem_rows = at("mem_rows", [P, MT, D], F32, M0)
        xs_rows = at("xs_rows", [P, D], F32, M0)
        kv_out = at("kv_out", [P, 2, MT, COLS], F32, M0 + D * 4)
        norm_mem_row = at("norm_mem_row", [P, D], F32, M0 + 2 * D * 4)
        norm_x_row = at("norm_x_row", [P, D], F32, M0 + 3 * D * 4)
        squares_out = at("squares_out", [P, D], F32, XH)
        state_rows = at("state_rows", [P, CC * P], F32, XL)
        h0_rows = at("h0_rows", [P, W], F32, XL + CC * P * 4)
        par_rows = at("par_rows", [P, 3, P], F32, XL + CC * P * 4 + W * 4)
        lx = at("lx", [P, LC * T], F32, M0)
        gy = at("gy", [P, LC * T], F32, M0 + CH // 2)
        qkv = at("qkv", [P, GC * T], F32, H0)
        z = at("z", [P, H * T], F32, H0 + GC * T * 4)
        edge_rows = at("edge_rows", [P, CC * P], F32, XH)
        HT = H * T * 4
        lru_a = at("lru_a", [P, LC, T], F32, XH + CC * P * 4)
        lru_w = at("lru_w", [P, 2, LC, P], F32, XH + CC * P * 4)
        gate_a = at("gate_a", [P, LC, T], F32, XL)
        gate_x = at("gate_x", [P, LC, T], F32, XL + HT)
        HG = H // 2
        GT = HG * P * 4
        top = [XH]

        def more(name, shape, dt=F32):
            t = at(name, shape, dt, top[0])
            size = 4
            for n in shape[1:]:
                size *= n
            top[0] += (size + 31) // 32 * 32
            return t

        half_t = [more(f"half_t{g}", [P, HG, P]) for g in range(2)]
        vb = [more(f"vb{g}", [P, HG, P]) for g in range(2)]
        kdec = [more(f"kdec{g}", [P, HG, P]) for g in range(2)]
        kbg = [more(f"kbg{g}", [P, HG, P]) for g in range(2)]
        grow = [more(f"grow{g}", [P, HG, P]) for g in range(2)]
        inner = [more(f"inner{g}", [P, HG, P]) for g in range(2)]
        qk = [more(f"qk{g}", [P, HG, P]) for g in range(2)]
        inv_t = [more(f"inv_t{g}", [P, HG, P]) for g in range(2)]
        keys = [more(f"keys{g}", [P, HG, P]) for g in range(2)]
        values = [more(f"values{g}", [P, HG, P]) for g in range(2)]
        inv = [more(f"inv{g}", [P, HG, P]) for g in range(2)]
        S = [more(f"S{g}", [P, HG, P]) for g in range(2)]
        LEVELS = 7
        blocks_mask = more("blocks_mask", [P, LEVELS, P])
        upper = more("upper", [P, P])
        lower = more("lower", [P, P])
        pair_mask = more("pair_mask", [P, P])
        o_squares = more("o_squares", [P, 2, HG * P])
        h_rows = more("h_rows", [P, LC * P])
        rest = XL + CH - top[0]
        assert top[0] <= XL + CH
        top[0] = XH
        l2_sq = more("l2_sq", [P, 2, T])
        l2_root = more("l2_root", [P, T])
        head_row = more("head_row", [P, 2 * H, P])
        assert top[0] <= XH + CC * P * 4
        top[0] = CONV
        bg_rows = more("bg_rows", [P, T])
        bg = more("bg", [P, TT + 1, 40])
        SPW = LC + (TT + 1) * H
        sp = [more(f"softplus{k}", [P, SPW]) for k in range(6)]
        row_par = more("row_par", [P, 2, H])
        beta = more("beta", [P, (TT + 1) * H])
        gate = more("gate", [P, (TT + 1) * H])
        gc = more("gc", [P, TT * H])
        egc = more("egc", [P, TT * H])
        begc = more("begc", [P, TT * H])
        dgc = more("dgc", [P, TT * H])
        glast = more("glast", [P, TT * H])
        o_ms = more("o_ms", [P, TT * H])
        o_root = more("o_root", [P, TT * H])
        head_col = more("head_col", [P, 4 * H - 1])
        assert top[0] <= HZERO0
        BH = B * H
        s_S = at("s_S", [P, BH, P], F32, W0)
        assert BH * P * 4 <= (RAW + 2 * SPLIT) * SLAB
        top[0] = XH
        s_q, s_k, s_v, s_z = (more(n, [P, BH]) for n in ("s_q", "s_k", "s_v", "s_z"))
        s_bg = more("s_bg", [P, 2, BH])
        s_wide = more("s_wide", [P, 2, BH])
        s_wq = more("s_wq", [P, BH, 2])
        s_qk = more("s_qk", [P, BH])
        s_new = more("s_new", [P, BH])
        s_o = more("s_o", [P, BH])
        s_t = more("s_t", [P, BH])
        s_rows = more("s_rows", [P, 2, P])
        SD = 8
        s_diag = [more(f"s_diag{k}", [P, SD, P]) for k in range(2)]
        assert top[0] <= XL + CH
        branch = at("branch", [P, NC, T], F32, M0)
        top[0] = CONV
        ssum = more("ssum", [P, T])
        sq = more("sq", [P, 2, T])
        xsum = more("xsum", [P, T])
        xw = more("xw", [P, T])
        assert top[0] <= arena0
        xt = at("xt", [P, NC, T], F32, H0)
        x_rows2 = at("x_rows2", [P, TT, D], F32, H1)
        xs_rows2 = at("xs_rows2", [P, D], F32, XL)
        xt_last = at("xt_last", [P, NC, T], F32, XH)
        y_rows = at("y_rows", [P, TT, D], F32, H1)
        ys_rows = at("ys_rows", [P, D], F32, XL)
        XH_ = i["cache_mem_k"].shape[3]
        DC = D // XH_ // P
        SCALE = float(D // XH_) ** -0.5
        q_t = at("q_t", [P, NC, T], F32, M0)
        k_t = at("k_t", [P, NC, M], F32, H1)
        kv_rows = at("kv_rows", [P, MT, D], F32, H1 + NC * M * 4)
        top[0] = H0
        cache = more("cache", [P, 3, D])
        probs_t = more("probs_t", [P, MT, SEQ])
        probs = more("probs", [P, TT, M])
        s_scores = more("s_scores", [P, MT, B * XH_])
        eye_b = more("eye_b", [P, B, B])
        assert top[0] <= H1
        top[0] = CONV
        q_wide0 = more("q_wide0", [P, D])
        spread = more("spread", [P, MT, B, XH_, B])
        stats = more("stats", [P, 3, TT * XH_])
        s_stats = more("s_stats", [P, 4])
        assert top[0] <= arena0
        q_wide = [q_wide0[:], cache[:, 2, :]]
        s_probs = at("s_probs", [P, M], F32, CONV)
        qs_rows = at("qs_rows", [P, D], F32, CONV)
        os_rows = at("os_rows", [P, D], F32, H0)
        h_high = at("h_high", [P, NC, T], F32R, H0)
        h_low = at("h_low", [P, NC, T], F32R, H1)
        x_mid = nc.dram_tensor("x_mid", (P, NC * T), F32, kind="Internal").ap()
        q_mid = nc.dram_tensor("q_mid", (B, D), F32, kind="Internal").ap()

        ps = ctx.enter_context(nc.psum_tensor("ps", [P, 8, 512], F32))

        def cols(w, it, j, blocks, col0, k0, kn, width=COLS):
            rows = w[0].rearrange("(k p) n -> p k n", p=P)
            return rows[:, k0:k0 + kn, bass.ds(it * (blocks * COLS) + (col0 + j * COLS), width)]

        def plain(w, blocks, col0):
            def sources(it, j, s):
                return [(slice(0, COLS), cols(w, it, j, blocks, col0, s * KS, KS))]
            return sources

        def beta_g(it, j, s):
            c = IN_COLS - 2 * H
            rows = i["w_in"][0].rearrange("(k p) n -> p k n", p=P)[:, s * KS:(s + 1) * KS]
            return [(slice(0, H), rows[:, :, c:c + H]), (slice(32, 32 + H), rows[:, :, c + H:c + 2 * H])]

        IN_COLS = i["w_in"].shape[2]
        SL = NC // KS
        g_wk = Gemm("wk", plain(i["xa_wk"], 2, 0), D // COLS // 2, 2, SL, NC, mem_high, mem_low, memory=True)
        g_wv = Gemm("wv", plain(i["xa_wv"], 2, 0), D // COLS // 2, 2, SL, NC, mem_high, mem_low, memory=True)
        g_lx = Gemm("lx", plain(i["w_in"], 2, 0), W // COLS // 2, 2, SL, NC, x_high, x_low)
        g_ly = Gemm("ly", plain(i["w_in"], 2, W), W // COLS // 2, 2, SL, NC, x_high, x_low)
        g_qkv = Gemm("qkv", plain(i["w_in"], 2, 2 * W), QKV // COLS // 2, 2, SL, NC, x_high, x_low)
        g_z = Gemm("z", plain(i["w_in"], 2, 2 * W + QKV), W // COLS // 2, 2, SL, NC, x_high, x_low)
        g_bg = Gemm("bg", beta_g, 1, 1, SL, NC, x_high, x_low)
        DB = D // COLS
        g_out = Gemm("out", plain(i["w_out"], 2, 0), DB // 2, 2, SL, NC, x_high, x_low)
        g_q = Gemm("q", plain(i["xa_wq"], 2, 0), DB // 2, 2, SL, NC, x_high, x_low)
        g_o = Gemm("o", plain(i["xa_wo"], 2, 0), DB // 2, 2, SL, NC, x_high, x_low)

        def gate_up(c0):
            def sources(it, j, s):
                out = []
                for k, n in enumerate(("ffn_w_gate", "ffn_w_up")):
                    rows = i[n][0].rearrange("(k p) n -> p k n", p=P)[:, s * KS:(s + 1) * KS]
                    out.append((slice(k * P, (k + 1) * P), rows[:, :, bass.ds(it * (2 * P) + (c0 + j) * P, P)]))
                return out
            return sources

        def down(c0, chunks, blocks):
            def sources(it, j, s):
                kn = min(KS, chunks - s * KS)
                return [(slice(0, COLS), cols(i["ffn_w_down"], it, j, blocks, 0, c0 + s * KS, kn))]
            return sources

        ffn = []
        for c0 in range(0, FF, NC):
            n = min(NC, FF - c0)
            slabs = -(-n // KS)
            blocks = 4 if slabs % 2 else 2
            ffn.append((c0, n, Gemm(f"up{c0}", gate_up(c0), n // 2, 2, SL, NC, x_high, x_low),
                        Gemm(f"down{c0}", down(c0, n, blocks), DB // blocks, blocks, slabs, n, h_high, h_low)))
        gemms = [g_wk, g_wv, g_lx, g_ly, g_qkv, g_z, g_bg, g_out, g_q, g_o] + [g for f in ffn for g in f[2:]]
        slab = block = 0
        for g in gemms:
            g.slab0, g.block0 = slab, block
            slab += g.iters * g.blocks * g.slabs
            block += g.iters * g.blocks
            assert g.slab0 % RAW == 0 and (g.blocks * g.slabs % RAW == 0) and (g.iters == 1 or g.blocks % 2 == 0)
        first_gemm, last_gemm = gemms[0], gemms[-1]

        params = ([(0, NORM[n], NC, i[n][0]) for n in norm_names]
                  + [(1, 0, TAPS * LC, i["lru_conv_w"][0]), (1, TAPS * LC, TAPS * GC, i["gdn_conv_w"][0])]
                  + [(2, MISC[n] - MISC0, LC, i[n][0]) for n in misc_names]
                  + [(2, MISC["gdn_norm_w"] - MISC0, 1, i["gdn_norm_w"][0])])
        PAR_ROWS = [len(norm_names) * NC, TAPS * CC, NPAR - MISC0]
        PAR_COLS = [0, CONV0, MISC0]
        row_tiles = ([(mem_rows[:, t, :], P, norm_mem_row) for t in range(MT)]
                     + [(x_rows[:, t, :], P, norm_x_row) for t in range(TT)] + [(xs_rows[:], B, norm_x_row)])
        turns = []
        for t, (rows, n, _) in enumerate(row_tiles):
            per = 4 if n == P else NC
            for c in range(0, NC, per):
                if t < MT:
                    to = [m[:, c:c + per, t * P:t * P + n] for m in (mem_high, mem_low)]
                else:
                    to = [m[:, c:c + per, (t - MT) * P:(t - MT) * P + n] for m in (x_high, x_low)]
                turns.append((t, c, per, n, to))
        mem_turns = MT * NC // 4
        TURN_BANKS = 4

        def turn_bank(k):
            return 1 + 2 * (k % TURN_BANKS)
        SQUARES_AT = {3 * n: MT + n for n in range(TT + 1)}
        ROOT_AT = 3 * TT + 1
        SCALE_AT = {ROOT_AT + 1 + 3 * n: MT + n for n in range(TT + 1)}
        assert max(SCALE_AT) < g_wk.iters * g_wk.blocks * g_wk.slabs

        x_order = [*range(TT // 2, TT), *range(TT // 2), TT]
        assert NC * M * 4 == TT // 2 * D * 4

        levels = range(LEVELS)
        STEPS = {
            "tensor": ["grow_ready", "k_turned", "kk_ready", "qk_ready", "v_turned"]
            + ["half_ready0"] + [f"{n}{l}" for l in levels[1:] for n in ("half_ready", "inv_t_ready", "inv_ready") if (n, l) != ("inv_ready", LEVELS - 1)]
            + ["wt_ready", "v_new_ready", "o_ready", "S_ready"],
            "vector": ["differ", "differences", "k_rows", "v_rows", "inner", "qk"]
            + ["half0", "inv_t0", "pairs", "inv0"]
            + [f"{n}{l}" for l in levels[1:] for n in ("half", "inv_t", "inv") if (n, l) != ("inv", LEVELS - 1)] + ["S_done"],
            "scalar": ["grow", "decays", "wt", "v_new", "o_taken"],
            "pool": ["keys", "values", "gate_wide", "inner_low", "inner_beta", "qk_mask", "q_scaled"],
        }
        ENGINE_OF = {n: e for e, names in STEPS.items() for n in names}

        def chunk_sem(name, g):
            return sem(f"chunk_{ENGINE_OF[name]}{g}")

        def step(name, g, n):
            names = STEPS[ENGINE_OF[name]]
            return chunk_sem(name, g), n * len(names) + (names.index(name) + 1)

        SPLIT_AT = {9: 2, 13: 3}
        assert SPLIT + len(SPLIT_AT) == SL

        O_BANK = g_out.acc(1) * 4

        def gemm_convolved(engine, split, g, after_block, first, second):
            def body(it, start=False, end=False):
                for j in range(g.blocks):
                    for s in range(SPLIT + (not (start and j == 0)), g.slabs + SPLIT):
                        if s == g.slabs + SPLIT - 1:
                            after_block(it, j)
                        split(g, it, j * g.slabs + s)
                    first(it, j)
                    if not (end and j == g.blocks - 1):
                        split(g, it, (j + 1) * g.slabs + SPLIT)
                    second(it, j)
            body(0, start=True)
            loop(engine, 1, g.iters - 1, body)
            body(g.iters - 1, end=True)

        block_ = ctx.enter_context(nc.Block())

        @block_.gpsimd
        def _(pool):
            pool.memset(ones[:], 1.0).then_inc(sem("consts"), 1)
            pool.memset(ident[:], 0.0).then_inc(sem("consts"), 1)
            pool.memset(xpad[:, :, 0:TAPS - 1], 0.0).then_inc(sem("consts"), 1)
            pool.wait_ge(sem("consts"), 2)
            pool.affine_select(out=ident[:], in_=ident[:], compare_op=ALU.not_equal, fill=1.0, base=0,
                               pattern=[[-1, P]], channel_multiplier=1).then_inc(sem("consts"), 1)
            for src, dst in (("state_lru_conv", "s_lru_conv"), ("state_gdn_conv", "s_gdn_conv")):
                pool.dma_start(o[dst][0, :, 0:TAPS - 2, :], i[src][0, :, 1:TAPS - 1, :]).then_inc(sem("stored"), 16)
            for g, name in ((g_wk, "p_mem_k"), (g_wv, "p_mem_v")):
                out = o[name][0, 0].rearrange("(t p) h d -> p t (h d)", p=P)

                def store(it):
                    for j in range(g.blocks):
                        pool.wait_ge(sem("acc_taken"), g.block(it, j) + 1)
                        pool.dma_start(out[:, :, bass.ds((it * g.blocks + j) * COLS, COLS)],
                                       kv_out[:, g.acc(j)]).then_inc(sem(f"kv_stored{g.acc(j)}"), 16)
                loop(pool, 0, g.iters, store)
            pool.wait_ge(sem("conv_taken"), CC)
            for k, n in enumerate(("gdn_A_log", "gdn_dt_bias")):
                pool.dma_start(row_par[:, k, :], i[n].to_broadcast([P, H])).then_inc(sem("row_par_loaded"), 16)
            pool.wait_ge(*after("edge_copied", CC // 4))
            e = edge_rows
            for c0, cn, p_out, s_out in ((0, W, "p_lru_conv", "s_lru_conv"), (W, QKV, "p_gdn_conv", "s_gdn_conv")):
                pool.dma_start(o[p_out][0, 0], e[0:TAPS - 1, c0:c0 + cn]).then_inc(sem("stored"), 16)
                pool.dma_start(o[s_out][0, :, TAPS - 2, :], e[TAPS - 1:EDGE, c0:c0 + cn]).then_inc(sem("stored"), 16)
            pool.wait_ge(*after("gates", LC))
            pool.tensor_tensor(gate_x[:], gate_x[:], lx[:].rearrange("p (c t) -> p c t", t=T), ALU.mult).then_inc(sem("gated_x"), 1)
            pool.wait_ge(*after("lru_scanned", 1))
            pool.wait_ge(sem("stored"), 16 * 6)
            pool.memset(upper[:], 1.0).then_inc(sem("masks0"), 1)
            pool.memset(lower[:], 1.0).then_inc(sem("masks0"), 1)
            pool.memset(blocks_mask[:], 0.0).then_inc(sem("masks0"), 1)
            pool.memset(pair_mask[:], 0.0).then_inc(sem("masks0"), 1)
            pool.wait_ge(sem("masks0"), 4)
            pool.affine_select(out=pair_mask[:], in_=pair_mask[:], compare_op=ALU.not_equal, fill=-1.0, base=-1,
                               pattern=[[-1, P]], channel_multiplier=1).then_inc(sem("masks0"), 1)
            pool.wait_ge(sem("masks0"), 5)
            pool.memset(pair_mask[:, 1:P:2], 0.0).then_inc(sem("masks"), 1)
            pool.affine_select(out=upper[:], in_=upper[:], compare_op=ALU.is_ge, fill=0.0, base=0,
                               pattern=[[1, P]], channel_multiplier=-1).then_inc(sem("masks"), 1)
            pool.affine_select(out=lower[:], in_=lower[:], compare_op=ALU.is_ge, fill=0.0, base=-1,
                               pattern=[[-1, P]], channel_multiplier=1).then_inc(sem("masks"), 1)
            for l in range(LEVELS):
                r = 1 << l
                odd = blocks_mask[:, l].rearrange("p (q o r) -> p q o r", o=2, r=r)[:, :, 1, :]
                n = P // (2 * r)
                pool.memset(odd, -1.0).then_inc(sem("masks0"), 1)
                pool.wait_ge(sem("masks0"), 6 + 2 * l)
                pool.affine_select(out=odd, in_=odd, compare_op=ALU.is_ge, fill=0.0, base=0,
                                   pattern=[[-2 * r, n], [0, r]], channel_multiplier=1).then_inc(sem("masks0"), 1)
                pool.wait_ge(sem("masks0"), 7 + 2 * l)
                pool.affine_select(out=odd, in_=odd, compare_op=ALU.is_ge, fill=0.0, base=r - 1,
                                   pattern=[[2 * r, n], [0, r]], channel_multiplier=-1).then_inc(sem("masks"), 1)
            pool.tensor_tensor(gy[:], gy[:], lx[:], ALU.mult).then_inc(sem("lru_out"), 1)

            pool.wait_ge(sem("masks"), 3 + LEVELS)
            pool.wait_ge(*after("lru_scanned", 1))
            pool.wait_ge(*after("normed", 2 * H))

            def chunk(n):
                later = type(n) is not int
                for g in range(2):
                    for dst, c0, name, used in ((keys, H, "keys", "qk_ready"), (values, 2 * H, "values", "v_turned")):
                        if later:
                            pool.wait_ge(*step(used, g, n - 1))
                        src = qkv[:].rearrange("p (c t) -> p c t", t=T)[:, c0 + g * HG:c0 + (g + 1) * HG, bass.ds(n * P, P)]
                        pool.tensor_copy(dst[g][:], src).then_inc(chunk_sem(name, g), 1)
                for g in range(2):
                    heads = bass.ds(n * H + g * HG, HG)
                    gw = gate[:, heads].rearrange("p (h a) -> p h a", a=1).to_broadcast([P, HG, P])
                    up = upper[:].rearrange("p (a j) -> p a j", a=1).to_broadcast([P, HG, P])
                    if later:
                        pool.wait_ge(*step(f"inv_t_ready{LEVELS - 1}", g, n - 1))
                    pool.tensor_tensor(inv[g][:], gw, up, ALU.mult).then_inc(chunk_sem("gate_wide", g), 1)
                for g in range(2):
                    heads = bass.ds(n * H + g * HG, HG)
                    low = lower[:].rearrange("p (a j) -> p a j", a=1).to_broadcast([P, HG, P])
                    up = upper[:].rearrange("p (a j) -> p a j", a=1).to_broadcast([P, HG, P])
                    bw = beta[:, heads].rearrange("p (h a) -> p h a", a=1).to_broadcast([P, HG, P])
                    pool.wait_ge(*step("decays", g, n))
                    pool.tensor_tensor(inner[g][:], inner[g][:], low, ALU.mult).then_inc(chunk_sem("inner_low", g), 1)
                    pool.wait_ge(*step("inner_low", g, n))
                    pool.tensor_tensor(inner[g][:], inner[g][:], bw, ALU.mult).then_inc(chunk_sem("inner_beta", g), 1)
                    pool.tensor_tensor(qk[g][:], qk[g][:], up, ALU.mult).then_inc(chunk_sem("qk_mask", g), 1)
                    q = qkv[:].rearrange("p (c t) -> p c t", t=T)[:, g * HG:(g + 1) * HG, bass.ds(n * P, P)]
                    pool.tensor_tensor(grow[g][:], grow[g][:], q, ALU.mult).then_inc(chunk_sem("q_scaled", g), 1)
            chunk(0)
            loop(pool, 1, TT, chunk)
            for g in range(2):
                pool.wait_ge(*step("S_done", g, TT - 1))
                pool.dma_start(o["p_gdn_S"][0, 0, g * HG:(g + 1) * HG].rearrange("h k v -> k h v"), S[g][:]).then_inc(sem("stored"), 16)
            pool.wait_ge(*after("h_rows", 2))
            pool.dma_start(o["p_lru_h"][0], h_rows[0:1, :]).then_inc(sem("stored"), 16)
            pool.dma_start(o["s_lru_h"][0], h_rows[1:1 + B, :]).then_inc(sem("stored"), 16)
            pool.wait_ge(sem("mixed_low"), 4)
            pool.dma_start(x_rows2[:], i["x_prompt"][0].rearrange("(t p) d -> p t d", p=P)).then_inc(sem("x_rows"), 16)

            def sum_squares(g, c0):
                def block(it, first=False):
                    for j in range(g.blocks):
                        b = g.block(it, j)
                        v = branch[:].rearrange("p c t -> p (c t)")[:, bass.ds((it * g.blocks + j) * 2 * T, 2 * T)]
                        n = b - c0
                        pool.wait_ge(sem("acc_taken"), b + 1)
                        pool.tensor_tensor(sq[:].rearrange("p a t -> p (a t)"), v, v, ALU.mult).then_inc(sem("sq"), 1)
                        pool.wait_ge(sem("sq"), n * 3 + 1)
                        if first and j == 0:
                            pool.tensor_copy(ssum[:], sq[:, 0]).then_inc(sem("sq"), 1)
                        else:
                            pool.tensor_tensor(ssum[:], ssum[:], sq[:, 0], ALU.add).then_inc(sem("sq"), 1)
                        pool.wait_ge(sem("sq"), n * 3 + 2)
                        pool.tensor_tensor(ssum[:], ssum[:], sq[:, 1], ALU.add).then_inc(sem("sq"), 1)
                        pool.wait_ge(sem("sq"), n * 3 + 3)
                block(0, True)
                loop(pool, 1, g.iters, block)

            sum_squares(g_out, g_out.block0)
            pool.wait_ge(sem("slab_used"), g_q.slab0)
            pool.dma_start(xs_rows2[0:B, :], i["x_sample"][:, 0, :]).then_inc(sem("xs_rows"), 16)
            pool.wait_ge(*after("x_turned", TT // 2 * 4))
            pool.dma_start(kv_rows[:], o["p_mem_k"][0, 0].rearrange("(t p) h d -> p t (h d)", p=P)).then_inc(sem("k_rows"), 16)
            def sum_new_squares(r):
                for c in range(NC):
                    pool.wait_ge(sem("x_squares"), r * NC + c + 1)
                    if c == 0:
                        pool.tensor_copy(xsum[:], sq[:, 0]).then_inc(sem("x_added"), 1)
                    else:
                        pool.wait_ge(sem("x_added"), r * NC + c)
                        pool.tensor_tensor(xsum[:], xsum[:], sq[:, c % 2], ALU.add).then_inc(sem("x_added"), 1)

            sum_new_squares(0)
            pool.wait_ge(sem("x_new"), NC)
            pool.dma_start(x_mid, xt[:].rearrange("p c t -> p (c t)")).then_inc(sem("x_mid"), 16)

            pool.wait_ge(sem("x_mid"), 16)
            pool.wait_ge(sem("norm_low"), NC)
            pool.memset(eye_b[:], 0.0).then_inc(sem("eye_b"), 1)
            pool.wait_ge(*after("eye_b", 1))
            pool.affine_select(out=eye_b[:], in_=eye_b[:], compare_op=ALU.not_equal, fill=1.0, base=0,
                               pattern=[[1, B], [-1, B]], channel_multiplier=0).then_inc(sem("eye_b"), 1)
            pool.wait_ge(*after("eye_b", 2))
            for c in range(2):
                pool.dma_start(cache[:, c, :], i["cache_mem_k"][0, 0, c * P:(c + 1) * P].rearrange("m h d -> m (h d)")).then_inc(sem(f"cache{c}"), 16)
            pool.wait_ge(*after("qs_rows", XH_))
            pool.dma_start(q_mid, qs_rows[0:B, :]).then_inc(sem("q_mid"), 16)
            pool.wait_ge(sem("q_mid"), 16)
            for b in range(B):
                if b >= 2:
                    pool.wait_ge(sem("s_scored"), (b - 1) * MT)
                pool.dma_start(q_wide[b % 2], q_mid[b:b + 1, :].to_broadcast([P, D])).then_inc(sem(f"q_wide{b % 2}"), 16)
                for c in range(MT):
                    if b:
                        pool.wait_ge(sem("s_scored"), (b - 1) * MT + c + 1)
                        pool.dma_start(cache[:, c, :], i["cache_mem_k"][0, b, c * P:(c + 1) * P].rearrange("m h d -> m (h d)")).then_inc(sem(f"cache{c}"), 16)
            for k in range(B * MT):
                if k < 3:
                    pool.wait_ge(sem("s_scored"), B * MT)
                else:
                    pool.wait_ge(*after("s_valued", k - 2))
                pool.dma_start(cache[:, k % 3, :],
                               i["cache_mem_v"][0, k // MT, k % MT * P:(k % MT + 1) * P].rearrange("m h d -> m (h d)")).then_inc(sem(f"values_in{k % 3}"), 16)
            pool.wait_ge(*after("s_o_low", 1))
            pool.wait_ge(sem("slab_used"), g_o.slab0 + 1)
            pool.dma_start(xt[:].rearrange("p c t -> p (c t)"), x_mid).then_inc(sem("x_back"), 16)
            sum_squares(g_o, g_o.block0 - DB)
            sum_new_squares(1)
            pool.wait_ge(sem("x_new"), 2 * NC)
            pool.wait_ge(sem("norm_low"), 2 * NC)
            pool.dma_start(x_mid, xt[:].rearrange("p c t -> p (c t)")).then_inc(sem("x_mid"), 16)
            g_last = ffn[-1][3]
            pool.wait_ge(sem("slab_used"), g_last.slab0)
            pool.wait_ge(sem("x_mid"), 32)
            pool.dma_start(xt_last[:].rearrange("p c t -> p (c t)"), x_mid).then_inc(sem("x_back"), 16)
            sum_squares(g_last, g_last.block0 - 2 * DB)
            pool.wait_ge(sem("x_back"), 32)
            for c in range(1, NC, 2):
                pool.wait_ge(sem("post"), 2 * NC + c + 1)
                pool.tensor_tensor(xt_last[:, c], xt_last[:, c], branch[:, c], ALU.add).then_inc(sem("x_new_odd"), 1)
            pool.wait_ge(sem("stored"), 16 * (6 + 2 + 2))

        @block_.sync
        def _(sp):
            def load(g, it, jj):
                if g.name != first_gemm.name or type(it) is not int or it * g.blocks * g.slabs + jj >= RAW:
                    sp.wait_ge(sem("w_low_ready"), g.slab(it, jj) - (RAW - 1))
                parts = g.sources(it, jj // g.slabs, jj % g.slabs)
                kn = min(KS, g.chunks - jj % g.slabs * KS)
                for where, source in parts:
                    sp.dma_start(w_raw[:, (g.slab0 + jj) % RAW, 0:kn, where],
                                 source).then_inc(sem(f"w_loaded{(g.slab0 + jj) % RAW}"), 32 // len(parts))

            for t in range(MT):
                sp.dma_start(mem_rows[:, t, :], i["mem_prompt"][0, t * P:(t + 1) * P, :]).then_inc(sem(f"rows{t}"), 16)
            sp.dma_start(norm_mem_row[:], i["norm_mem"].to_broadcast([P, D])).then_inc(sem("norm_rows0"), 16)
            for jj in range(RAW):
                load(first_gemm, 0, jj)
            for tile, r, n, v in params:
                v = v.rearrange("(r p) -> r p", p=P) if len(v.shape) == 1 else v.rearrange("j (c p) -> j c p", p=P)
                if len(v.shape) == 3:
                    for j in range(TAPS):
                        m = n // TAPS
                        sp.dma_start(par_rows[r + j * m:r + (j + 1) * m, tile, :], v[j]).then_inc(sem("par_loaded"), 16)
                else:
                    sp.dma_start(par_rows[r:r + n, tile, :], v).then_inc(sem("par_loaded"), 16)
            for c0, cn, src in ((0, W, "state_lru_conv"), (W, QKV, "state_gdn_conv")):
                sp.dma_start(state_rows[0:B * (TAPS - 1), c0:c0 + cn],
                             i[src][0].rearrange("b j n -> (b j) n")).then_inc(sem("par_loaded"), 16)
            sp.dma_start(h0_rows[0:B, :], i["state_lru_h"][0]).then_inc(sem("par_loaded"), 16)
            sp.dma_start(norm_x_row[:], i["norm_mix_pre"].to_broadcast([P, D])).then_inc(sem("norm_rows1"), 16)
            for t in range(TT):
                sp.dma_start(x_rows[:, t, :], i["x_prompt"][0, t * P:(t + 1) * P, :]).then_inc(sem(f"rows{MT + t}"), 16)
            sp.wait_ge(sem("turned"), NC // 4)
            sp.dma_start(xs_rows[0:B, :], i["x_sample"][:, 0, :]).then_inc(sem(f"rows{MT + TT}"), 16)

            for g in gemms:
                if g.name == g_out.name:
                    sp.wait_ge(sem("slab_used"), g_out.slab0)
                    for k, n in enumerate(("lru_gate_a_w", "lru_gate_x_w")):
                        sp.dma_start(lru_w[:, k], i[n][0].rearrange("h i j -> i h j")).then_inc(sem("lru_w_loaded"), 16)
                    for b in range(B):
                        sp.dma_start(s_S[:, b * H:(b + 1) * H, :], i["state_gdn_S"][0, b].rearrange("h k v -> k h v")).then_inc(sem("s_S_loaded"), 16)
                    for b in range(B):
                        sp.wait_ge(sem("s_S_new"), (b + 1) * H // 4)
                        sp.dma_start(o["s_gdn_S"][0, b].rearrange("h k v -> k h v"), s_S[:, b * H:(b + 1) * H, :]).then_inc(sem("s_S_stored"), 16)
                    sp.wait_ge(sem("s_S_stored"), 16 * B)

                def loads(it, g=g):
                    for jj in range(g.blocks * g.slabs):
                        load(g, it, jj)
                if g.name == first_gemm.name:
                    for jj in range(RAW, g.blocks * g.slabs):
                        load(g, 0, jj)
                loop(sp, 1 if g.name == first_gemm.name else 0, g.iters, loads)
            for q in range(4):
                sp.wait_ge(*after("y_copied", (q + 1) * (TT + 1)))
                d = slice(q * 512, (q + 1) * 512)
                sp.dma_start(o["y_prompt"][0, :, d].rearrange("(t p) d -> p t d", p=P), y_rows[:, :, d]).then_inc(sem("y_stored"), 16)
                sp.dma_start(o["y_sample"][:, 0, d], ys_rows[0:B, d]).then_inc(sem("y_stored"), 16)
            sp.wait_ge(sem("y_stored"), 16 * 8)

        @block_.scalar
        def _(act):
            def row_squares(tiles):
                for t in tiles:
                    rows, n, _ = row_tiles[t]
                    act.wait_ge(sem(f"rows{t}"), 16)
                    if t:
                        act.wait_ge(sem("row_squares"), t)
                    act.activation(squares_out[0:n], rows[0:n], ACT.Square, accum_out=ssq[0:n, t:t + 1]).then_inc(sem("row_squares"), 1)

            def row_root(k):
                act.wait_ge(sem("row_means"), k + 1)
                a, b = row_groups[k]
                act.activation(root[:, a:b], ms[:, a:b], ACT.Sqrt).then_inc(sem("row_roots"), 1)

            act.wait_ge(sem("ssq_clear"), 1)
            row_squares(range(0, MT))
            row_root(0)

            def split_high(g, it, jj):
                slot = (g.slab0 + jj) % SPLIT
                act.wait_ge(sem(f"w_loaded{(g.slab0 + jj) % RAW}"), g.loads(it, jj) * 32)
                if not (g.name == first_gemm.name and type(it) is int and it * g.blocks * g.slabs + jj < SPLIT):
                    act.wait_ge(sem("slab_used"), g.slab(it, jj) - (SPLIT - 1))
                act.activation(w_high[:, slot], w_raw[:, (g.slab0 + jj) % RAW], ACT.Copy).then_inc(sem("w_high_ready"), 1)

            def turn_high(n):
                for k in n:
                    t, c, per, rows, to = turns[k]
                    act.wait_ge(sem("turned"), k + 1)
                    act.activation(to[0], ps[:, turn_bank(k), 0:per * rows].rearrange("p (c t) -> p c t", c=per),
                                   ACT.Copy).then_inc(sem("turn_high"), 1)

            turn_high(range(0, mem_turns))
            split_high(first_gemm, 0, 0)
            split_high(first_gemm, 0, 1)

            def gemm(g, evacuate, peel=0):
                last = g.name in (last_gemm.name, g_bg.name)
                taken, rest = evacuate if type(evacuate) is tuple else (None, evacuate)

                def body(it, end=False):
                    for j in range(g.blocks):
                        for s in range(g.slabs if peel and type(it) is int and j == 0 else SPLIT, g.slabs + SPLIT):
                            if s == g.slabs and end and j == g.blocks - 1:
                                break
                            if taken and s == g.slabs + SPLIT - 1:
                                taken(it, j)
                            split_high(g, it, j * g.slabs + s)
                        rest(it, j)
                if peel:
                    body(0)
                loop(act, peel, g.iters - last, body)
                if last:
                    body(g.iters - 1, True)

            def acc_ready(g, it, j):
                act.wait_ge(sem("slab_used"), g.slab(it, (j + 1) * g.slabs - 1) + 1)
                return g.acc(j) * 4

            def take_kv(g):
                def evacuate(it, j):
                    b = acc_ready(g, it, j)
                    if not (g.name == first_gemm.name and type(it) is int and it == 0):
                        act.wait_ge(sem(f"kv_stored{g.acc(j)}"), (it + g.block0 // 2) * 16)
                    for m in range(MT):
                        ins = act.activation(kv_out[:, g.acc(j), m], ps[:, b + 2 * m, 0:COLS], ACT.Copy)
                    ins.then_inc(sem("acc_taken"), 1)
                return evacuate

            def gemm_kv(g):
                def body(it):
                    for j in range(g.blocks):
                        for s in range(SPLIT, g.slabs + SPLIT):
                            split_high(g, it, j * g.slabs + s)
                            if g.name == first_gemm.name:
                                n = (it * g.blocks + j) * g.slabs + s - SPLIT
                                if n in SQUARES_AT:
                                    row_squares([SQUARES_AT[n]])
                                if n == ROOT_AT:
                                    row_root(1)
                        take_kv(g)(it, j)
                if g.name == first_gemm.name:
                    for it in range(g.iters):
                        body(it)
                else:
                    loop(act, 0, g.iters, body)

            gemm_kv(g_wk)
            act.wait_ge(sem("row_squares"), len(row_tiles))
            turn_high(range(mem_turns, len(turns)))
            gemm_kv(g_wv)

            for p in range(2):
                act.wait_ge(sem(f"kv_stored{p}"), 16 * (g_wk.iters + g_wv.iters))

            def take_convolved(g, func, out, c0):
                def pad(m):
                    def evacuate(it, j):
                        b = acc_ready(g, it, j)
                        chunk = it * (2 * g.blocks) + (2 * j + m)
                        done = chunk + c0
                        first = type(it) is int and c0 == 0 and it == 0 and j == 0
                        if not first:
                            act.wait_ge(sem("convolved"), done - 1)
                        acc = ps[:, b + 2 * m:b + 2 * m + 2, 0:HALF]
                        x = xpad[:, m]
                        windows = x[:, S0:PADDED].rearrange("p (b j) -> p b j", j=TAPS)
                        act.activation(x[:, TAPS - 1:TAPS - 1 + HALF], acc[:, 0], ACT.Copy)
                        act.activation(x[:, TAPS - 1 + HALF:S0], acc[:, 1, 0:SEQ - HALF], ACT.Copy)
                        act.activation(windows[:, :, TAPS - 1], acc[:, 1, SEQ - HALF:HALF], ACT.Copy)
                        act.activation(windows[:, :, 0:TAPS - 1],
                                       conv_state[:, bass.ds(done, 1), :].rearrange("p a (b j) -> p (a b) j", b=B), ACT.Copy)
                        ins = act.activation(edge[:, bass.ds(done, 1), :].rearrange("p a e -> p (a e)"),
                                             acc[:, 1, HALF - EDGE:HALF], ACT.Copy)
                        ins.then_inc(sem("acc_taken" if m else "padded"), 1)
                    return evacuate

                def activate(m):
                    def evacuate(it, j):
                        chunk = it * (2 * g.blocks) + (2 * j + m)
                        done = chunk + c0
                        act.wait_ge(sem("convolved"), done + 1)
                        act.activation(out[:, bass.ds(chunk * T, SEQ)], conved[:, 0:SEQ], func)
                        act.activation(out[:, bass.ds(chunk * T + SEQ, B)], conved[:, S0:CONVED:TAPS],
                                       func).then_inc(sem("conv_taken"), 1)
                    return evacuate

                def activate_both(it, j):
                    activate(0)(it, j)
                    activate(1)(it, j)
                return pad(0), pad(1), activate_both

            def take(g, func, out):
                def evacuate(it, j):
                    b = acc_ready(g, it, j)
                    for m in range(2):
                        chunk = it * (2 * g.blocks) + (2 * j + m)
                        ins = act.activation(out[:, bass.ds(chunk * T, T)].rearrange("p (h t) -> p h t", h=2),
                                             ps[:, b + 2 * m:b + 2 * m + 2, 0:HALF], func)
                    ins.then_inc(sem("acc_taken"), 1)
                return evacuate

            gemm_convolved(act, split_high, g_lx, *take_convolved(g_lx, ACT.Identity, lx, 0))
            gemm(g_ly, take(g_ly, ACT.Gelu_apprx_tanh, gy))
            gemm_convolved(act, split_high, g_qkv, *take_convolved(g_qkv, ACT.Silu, qkv, LC))
            gemm(g_z, take(g_z, ACT.Silu, z))

            def nothing(it, j):
                pass

            gemm(g_bg, nothing)

            act.wait_ge(*after("sp_abs", 1))
            act.activation(sp[1][:], sp[1][:], ACT.Exp, scale=-1.0).then_inc(sem("sp_exp"), 1)
            act.wait_ge(sem("row_par_loaded"), 32)
            act.activation(row_par[:, 0], row_par[:, 0], ACT.Exp).then_inc(sem("sp_exp"), 1)
            act.activation(beta[:].rearrange("p (n h) -> p n h", h=H), bg[:, :, 0:H], ACT.Sigmoid).then_inc(sem("beta"), 1)
            for c in range(LC):
                act.wait_ge(*after("gates_ready", c + 1))
                b = c % 2 * 4
                for k, (dst, name) in enumerate(((gate_a, "lru_gate_a_b"), (gate_x, "lru_gate_x_b"))):
                    ins = act.activation(dst[:, c].rearrange("p (h t) -> p h t", h=2), ps[:, b + 2 * k:b + 2 * k + 2, 0:HALF],
                                         ACT.Sigmoid, bias=par[:, MISC[name] + c:MISC[name] + c + 1])
                ins.then_inc(sem("gates"), 1)
            act.wait_ge(sem("stored"), 16 * 6)
            for c in range(2 * H):
                if c >= 2:
                    act.wait_ge(*after("l2_summed", c - 1))
                act.activation(l2_sq[:, c % 2], qkv[:, c * T:(c + 1) * T], ACT.Square).then_inc(sem("l2_squares"), 1)
            act.wait_ge(*after("l2_summed", 2 * H))
            act.wait_ge(sem("l2_clear"), 1)
            act.activation(l2_root[0:2 * H].rearrange("p (h t) -> p h t", h=2), ps[0:2 * H, 0:2, 0:HALF],
                           ACT.Sqrt, bias=eps_col[0:2 * H]).then_inc(sem("l2_root"), 1)
            act.wait_ge(*after("log_a", 1))
            act.activation(lru_a[:], gate_a[:], ACT.Exp)
            act.activation(gate_a[:], gate_a[:], ACT.Tanh, scale=-0.5).then_inc(sem("lru_tanh"), 1)
            act.wait_ge(*after("lru_tanh", 1))
            act.activation(gate_a[:], gate_a[:], ACT.Sqrt).then_inc(sem("lru_sqrt"), 1)

            act.wait_ge(*after("s_wide_ready", 1))
            act.activation(s_bg[:, 0], ps[:, 0, 0:BH], ACT.Copy)
            act.activation(s_bg[:, 1], ps[:, 0, BH:2 * BH], ACT.Exp).then_inc(sem("s_bg_wide"), 1)
            act.wait_ge(*after("s_bg_wide", 1))
            act.wait_ge(sem("s_S_loaded"), 16 * B)
            for m in range(BH):
                ins = act.activation(s_S[:, m], s_S[:, m], ACT.Copy, scale=s_bg[:, 1, m:m + 1])
                if m % H == H - 1:
                    ins.then_inc(sem("s_decayed"), 1)
            act.wait_ge(*after("s_var", 1))
            act.activation(s_t[:], s_t[:], ACT.Sqrt).then_inc(sem("s_root"), 1)
            act.wait_ge(*after("gc_ready", 1))
            act.activation(egc[:], gc[:], ACT.Exp).then_inc(sem("gc_exps"), 1)
            act.activation(glast[:], glast[:], ACT.Exp).then_inc(sem("gc_exps"), 1)
            act.activation(dgc[:], dgc[:], ACT.Exp).then_inc(sem("gc_exps"), 1)

            def chunk(n):
                for g in range(2):
                    act.wait_ge(*step("grow_ready", g, n))
                    act.activation(grow[g][:], ps[:, 4 * g, :].rearrange("p (h j) -> p h j", h=HG), ACT.Exp).then_inc(chunk_sem("grow", g), 1)
                    act.wait_ge(*step("differences", g, n))
                    act.activation(inner[g][:], inner[g][:], ACT.Exp, scale=-1.0)
                    act.activation(qk[g][:], qk[g][:], ACT.Exp).then_inc(chunk_sem("decays", g), 1)
                for g in range(2):
                    act.wait_ge(*step("wt_ready", g, n))
                    act.activation(kbg[g][:], ps[:, 4 * g + 3, :].rearrange("p (h j) -> p h j", h=HG), ACT.Copy, scale=-1.0).then_inc(chunk_sem("wt", g), 1)
                for g in range(2):
                    act.wait_ge(*step("v_new_ready", g, n))
                    act.activation(vb[g][:], ps[:, 4 * g, :].rearrange("p (h j) -> p h j", h=HG), ACT.Copy).then_inc(chunk_sem("v_new", g), 1)
                for g in range(2):
                    act.wait_ge(*step("o_ready", g, n))
                    dst = qkv[:].rearrange("p (c t) -> p c t", t=T)[:, 2 * H + g * HG:2 * H + (g + 1) * HG, bass.ds(n * P, P)]
                    if type(n) is not int:
                        act.wait_ge(*step("o_taken", g, n - 1))
                    for h in range(HG):
                        act.activation(o_squares[:, g, h * P:(h + 1) * P], ps[:, 4 * g + 1, h * P:(h + 1) * P], ACT.Square,
                                       accum_out=o_ms[:, bass.ds((g * HG + h) * TT + n, 1)])
                    act.activation(dst, ps[:, 4 * g + 1, :].rearrange("p (h j) -> p h j", h=HG), ACT.Copy).then_inc(chunk_sem("o_taken", g), 1)
            chunk(0)
            loop(act, 1, TT, chunk)
            for s in range(SPLIT):
                split_high(g_out, 0, s)
            act.wait_ge(*after("o_ms", 1))
            act.activation(o_root[:], o_ms[:], ACT.Sqrt).then_inc(sem("o_root"), 1)

            act.wait_ge(*after("lru_out", 1))
            halves = [(gy, 0), (gy, 1), (z, 0), (z, 1)]
            for g in range(2):
                act.wait_ge(*step("S_done", g, TT - 1))
            for k, (src, part) in enumerate(halves):
                if k >= 2:
                    act.wait_ge(*after("o_done", (k - 1) * H // 2))
                act.activation(x_high[:, 4 * k:4 * k + 4], src[:, part * 4 * T:(part + 1) * 4 * T].rearrange("p (c t) -> p c t", t=T),
                               ACT.Copy).then_inc(sem("mixed_high"), 1)
            act.wait_ge(sem("mixed_low"), 4)

            def flat(t):
                return t[:].rearrange("p c t -> p (c t)")

            def root_of_mean(r):
                s = xsum if r % 2 else ssum
                act.wait_ge(sem("mean"), r + 1)
                act.activation(s[:], s[:], ACT.Sqrt).then_inc(sem("rooted"), 1)

            def residual(r, pre=None, g_next=None):
                root_of_mean(2 * r)
                if pre is None:
                    return
                for c in range(NC):
                    if c in SPLIT_AT:
                        split_high(g_next, 0, SPLIT_AT[c])
                    act.wait_ge(sem("x_new"), r * NC + c + 1)
                    act.activation(x_high[:, c], xt[:, c], ACT.Copy, scale=par[:, NORM[pre] + c:NORM[pre] + c + 1]).then_inc(sem("norm_high"), 1)
                    if c >= 2:
                        act.wait_ge(sem("x_added"), r * NC + c - 1)
                    act.activation(sq[:, c % 2], xt[:, c], ACT.Square).then_inc(sem("x_squares"), 1)

            gemm(g_out, take(g_out, ACT.Copy, flat(branch)))
            for n, t in enumerate(x_order):
                for b in range(4 if t < TT else 1):
                    k = n * 4 + b
                    act.wait_ge(*after("x_turned", k + 1))
                    if t < TT:
                        act.activation(xt[:, 4 * b:4 * b + 4, t * P:(t + 1) * P],
                                       ps[:, 4 + k % 4, :].rearrange("p (c t) -> p c t", c=4), ACT.Copy).then_inc(sem("x_turns_taken"), 1)
                    else:
                        act.activation(xt[:, :, SEQ:T], ps[:, 4 + k % 4, 0:NC * B].rearrange("p (c t) -> p c t", c=NC),
                                       ACT.Copy).then_inc(sem("x_turns_taken"), 1)
            residual(0, "norm_xa_pre", g_q)

            def root_at_first(it, j):
                if type(it) is int and it == 0 and j == 0:
                    root_of_mean(1)
            gemm(g_q, root_at_first, peel=1)
            for k in range(XH_):
                act.wait_ge(*after("qs_turned", k + 1))
                act.activation(qs_rows[0:B, k * 512:(k + 1) * 512], ps[0:B, 4 + k, :], ACT.Copy).then_inc(sem("qs_rows"), 1)
            for k in range(NC // 2):
                act.wait_ge(*after("k_t_turned", k + 1))
                act.activation(k_t[:, 2 * k:2 * k + 2, :], ps[:, 4 + k % 4, :].rearrange("p (c m) -> p c m", c=2), ACT.Copy).then_inc(sem("k_t"), 1)
            act.dma_start(kv_rows[:], o["p_mem_v"][0, 0].rearrange("(t p) h d -> p t (h d)", p=P)).then_inc(sem("v_rows"), 16)

            def exponentials(h, t):
                n = h * TT + t
                act.wait_ge(sem("row_max"), n // 2 + 1)
                if h:
                    act.wait_ge(sem("probs_turned"), h)
                act.activation(probs[:, t], ps[:, h % 2 * 2 + t // 2, t % 2 * M:(t % 2 + 1) * M], ACT.Exp, bias=stats[:, 0, n:n + 1],
                               scale=SCALE, accum_out=stats[:, 1, n:n + 1]).then_inc(sem("exponentials"), 1)

            act.wait_ge(sem("x_mid"), 16)
            for t in range(TT):
                exponentials(0, t)
            for h in range(XH_):
                act.wait_ge(sem("probs_turned"), h + 1)
                if h:
                    act.wait_ge(sem("pv_ready"), h * DC)
                for k in range(2):
                    ins = act.activation(probs_t[:, :, k * 2 * P:(k + 1) * 2 * P].rearrange("p m (t l) -> p t m l", t=2),
                                         ps[:, 4 + k, :].rearrange("p (t m l) -> p t m l", t=2, m=MT), ACT.Copy)
                ins.then_inc(sem("probs_t"), 1)
                for t in range(TT):
                    if h + 1 < XH_:
                        exponentials(h + 1, t)
                    n = h * DC + t
                    act.wait_ge(sem("pv_ready"), n + 1)
                    act.activation(x_high[:, n, 0:SEQ], ps[:, 6 + n % 2, :], ACT.Copy).then_inc(sem("pv_high"), 1)
            act.wait_ge(*after("s_max", 1))
            act.activation(s_probs[0:B * XH_], ps[0:B * XH_, 0, 0:M], ACT.Exp, bias=s_stats[0:B * XH_, 1:2], scale=SCALE,
                           accum_out=s_stats[0:B * XH_, 2:3]).then_inc(sem("s_exp"), 1)
            act.wait_ge(*after("s_valued", B * MT))
            act.activation(os_rows[0:B, :].rearrange("p (h d) -> p h d", h=XH_), ps[0:B, 4:4 + XH_, :], ACT.Copy).then_inc(sem("os_rows"), 1)
            act.wait_ge(*after("os_turned", 1))
            act.activation(x_high[:, :, SEQ:T], ps[:, 2, 0:NC * B].rearrange("p (c b) -> p c b", b=B), ACT.Copy).then_inc(sem("s_o_high"), 1)

            gemm(g_o, take(g_o, ACT.Copy, flat(branch)))
            residual(1, "norm_ffn_pre", ffn[0][2])

            for c0, n, g_up, g_down in ffn:
                def hidden(it, j, g=g_up, c0=c0):
                    chunk = it * 2 + j
                    if c0 == 0 and type(it) is int and j == 0:
                        root_of_mean(3)
                    act.wait_ge(sem("gate_scaled"), chunk + (c0 + 1))
                    act.activation(sq[:, j], sq[:, j], ACT.Silu).then_inc(sem("silu"), 1)
                    act.wait_ge(sem("hidden"), chunk + (c0 + 1))
                    if c0 == 0 and type(it) is int and j == 0:
                        act.wait_ge(sem("x_mid"), 32)
                    act.activation(flat(h_high)[:, bass.ds(chunk * T, T)], xw[:], ACT.Copy).then_inc(sem("h_high"), 1)
                gemm(g_up, hidden, peel=c0 == 0)
                gemm(g_down, nothing)
            residual(2)
            for k in range(4 * (TT + 1)):
                q, t = k // (TT + 1), k % (TT + 1)
                rows, y = (P, y_rows[:, t]) if t < TT else (B, ys_rows[0:B])
                act.wait_ge(*after("y_turned", k + 1))
                act.activation(y[:, q * 512:(q + 1) * 512], ps[0:rows, k % 8, :], ACT.Copy).then_inc(sem("y_copied"), 1)

        @block_.vector
        def _(dve):
            dve.memset(eps_col[:], EPS)
            dve.memset(ssq[:], 1.0).then_inc(sem("ssq_clear"), 1)


            def small_copies():
                dve.wait_ge(*after("small_turned", 1))
                for k in range(3):
                    ins = dve.tensor_copy(par[:, PAR_COLS[k]:PAR_COLS[k] + PAR_ROWS[k]], ps[:, 1, k * P:k * P + PAR_ROWS[k]])
                ins.then_inc(sem("small_copied"), 1)
                NS = B * (TAPS - 1)
                dve.wait_ge(*after("small_turned", 2))
                dve.tensor_copy(conv_state[:, 0:LC, :], ps[:, 3, 0:LC * NS].rearrange("p (c s) -> p c s", s=NS))
                dve.tensor_copy(h0[:], ps[:, 3, LC * NS:LC * NS + LC * B].rearrange("p (c b) -> p c b", b=B)).then_inc(sem("small_copied"), 1)
                for k in range(2):
                    dve.wait_ge(*after("small_turned", 3 + k))
                    c = LC + k * GC // 2
                    dve.tensor_copy(conv_state[:, c:c + GC // 2, :],
                                    ps[:, 5 + 2 * k, 0:GC // 2 * NS].rearrange("p (c s) -> p c s", s=NS)).then_inc(sem("small_copied"), 1)

            def row_rstd(k):
                a, b = row_groups[k]
                dve.wait_ge(sem("row_squares"), b)
                dve.tensor_scalar(ms[:, a:b], ssq[:, a:b], 1.0 / D, EPS, ALU.mult, ALU.add).then_inc(sem("row_means"), 1)
                dve.wait_ge(sem("row_roots"), k + 1)
                dve.reciprocal(rstd_rows[:, a:b], root[:, a:b]).then_inc(sem("row_rstd"), 1)
                dve.wait_ge(sem("row_rstd"), k + 1)

            def row_scale(tiles):
                for t in tiles:
                    rows, n, w = row_tiles[t]
                    dve.wait_ge(sem("norm_rows0" if t < MT else "norm_rows1"), 16)
                    dve.scalar_tensor_tensor(rows[0:n], rows[0:n], rstd_rows[0:n, t:t + 1], w[0:n],
                                             ALU.mult, ALU.mult).then_inc(sem("rows_scaled"), 1)

            def turn_low(n):
                for k in n:
                    t, c, per, rows, to = turns[k]
                    dve.wait_ge(sem("turn_high"), k + 1)
                    dve.tensor_tensor(to[1], ps[:, turn_bank(k), 0:per * rows].rearrange("p (c t) -> p c t", c=per),
                                      to[0].bitcast(F32), ALU.subtract).then_inc(sem("turn_low"), 1)

            row_rstd(0)
            row_scale(range(MT))
            turn_low(range(0, mem_turns))

            def split_low(g, it, jj):
                slot = (g.slab0 + jj) % SPLIT
                dve.wait_ge(sem("w_high_ready"), g.slab(it, jj) + 1)
                dve.tensor_tensor(w_low[:, slot], w_raw[:, (g.slab0 + jj) % RAW], w_high[:, slot].bitcast(F32),
                                  ALU.subtract).then_inc(sem("w_low_ready"), 1)

            def gemm(g, evacuate, peel=0):
                last = g.name in (last_gemm.name, g_bg.name)
                taken, rest = evacuate if type(evacuate) is tuple else (None, evacuate)

                def body(it, end=False):
                    for j in range(g.blocks):
                        for s in range(g.slabs if peel and type(it) is int and j == 0 else SPLIT, g.slabs + SPLIT):
                            if s == g.slabs and end and j == g.blocks - 1:
                                break
                            if taken and s == g.slabs + SPLIT - 1:
                                taken(it, j)
                            split_low(g, it, j * g.slabs + s)
                        rest(it, j)
                if peel:
                    body(0)
                loop(dve, peel, g.iters - last, body)
                if last:
                    body(g.iters - 1, True)

            def nothing(it, j):
                pass

            def convolve(g, c0, w0, wn, bias):
                def half(m):
                    def evacuate(it, j):
                        chunk = it * (2 * g.blocks) + (2 * j + m)
                        done = chunk + c0
                        if m:
                            dve.wait_ge(sem("acc_taken"), g.block(it, j) + 1)
                        else:
                            dve.wait_ge(sem("padded"), it * g.blocks + (c0 // 2 + j + 1))
                        if not (type(it) is int and it == 0 and j == 0 and m == 0 and c0 == 0):
                            dve.wait_ge(sem("conv_taken"), done)
                        x = xpad[:, m]

                        def col(k):
                            return par[:, bass.ds(chunk + k, 1)]
                        if bias is None:
                            ins = dve.tensor_scalar(conved[:], x[:, 0:CONVED], col(w0), None, ALU.mult)
                        else:
                            ins = dve.tensor_scalar(conved[:], x[:, 0:CONVED], col(w0), col(bias), ALU.mult, ALU.add)
                        for tap in range(1, TAPS):
                            ins.then_inc(sem("conv_taps"), 1)
                            dve.wait_ge(sem("conv_taps"), done * (TAPS - 1) + tap)
                            ins = dve.scalar_tensor_tensor(conved[:], x[:, tap:tap + CONVED], col(w0 + tap * wn), conved[:],
                                                           ALU.mult, ALU.add)
                        ins.then_inc(sem("convolved"), 1)
                    return evacuate
                return nothing, half(0), half(1)

            split_low(first_gemm, 0, 0)
            split_low(first_gemm, 0, 1)
            for n in range(g_wk.iters * g_wk.blocks):
                for s in range(SPLIT, g_wk.slabs + SPLIT):
                    split_low(g_wk, 0, n * g_wk.slabs + s)
                    k = n * g_wk.slabs + s - SPLIT
                    if k == ROOT_AT:
                        row_rstd(1)
                    if k in SCALE_AT:
                        row_scale([SCALE_AT[k]])
            small_copies()
            turn_low(range(mem_turns, len(turns)))
            gemm(g_wv, nothing)
            gemm_convolved(dve, split_low, g_lx, *convolve(g_lx, 0, CONV0, LC, MISC["lru_conv_b"]))
            gemm(g_ly, nothing)
            gemm_convolved(dve, split_low, g_qkv, *convolve(g_qkv, LC, CONV0 + TAPS * LC, GC, None))
            gemm(g_z, nothing)

            gemm(g_bg, nothing)
            chain = [0]

            def link(ins):
                chain[0] += 1
                ins.then_inc(sem("dve_chain"), 1)
                dve.wait_ge(sem("dve_chain"), chain[0])

            dve.wait_ge(sem("slab_used"), g_bg.slab0 + g_bg.slabs)
            dve.tensor_copy(bg_rows[:].rearrange("p (h t) -> p h t", h=2), ps[:, g_bg.acc(0) * 4:g_bg.acc(0) * 4 + 2, 0:HALF]).then_inc(sem("acc_taken"), 1)
            for k in range(CC // 4):
                dve.wait_ge(*after("edge_turned", k + 1))
                dve.tensor_copy(edge_rows[0:EDGE, k * 512:(k + 1) * 512], ps[0:EDGE, 4 + k % 4, :]).then_inc(sem("edge_copied"), 1)
            x, y, d, q, q2, pl = (t[:] for t in sp)
            heads = x[:, LC:SPW].rearrange("p (n h) -> p n h", h=H)
            dve.tensor_scalar(x[:, 0:LC], par[:, MISC["lru_lambda"]:MISC["lru_lambda"] + LC], -1.0, None, ALU.mult)
            dve.memset(head_col[:], 0.0)
            link(dve.memset(bg[:], 0.0))
            dve.memset(head_col[:, 2 * H - 1:2 * H], 1.0).then_inc(sem("head_col"), 1)
            dve.wait_ge(*after("bg_turned", 1))
            dve.tensor_copy(bg[:, 0:TT, :], ps[:, 1, 0:TT * 40].rearrange("p (n c) -> p n c", c=40))
            link(dve.tensor_copy(bg[0:B, TT, :], ps[0:B, 1, TT * 40:TT * 40 + 40]))
            dve.wait_ge(sem("row_par_loaded"), 32)
            link(dve.tensor_tensor(heads, bg[:, :, 32:32 + H],
                                   row_par[:, 1].rearrange("p (a h) -> p a h", a=1).to_broadcast([P, TT + 1, H]), ALU.add))
            link(dve.tensor_scalar(q, x, -1.0, None, ALU.mult))
            dve.tensor_tensor(y, x, q, ALU.max).then_inc(sem("sp_abs"), 1)
            dve.wait_ge(*after("sp_exp", 1))
            link(dve.tensor_scalar(d, y, 2.0, None, ALU.add))
            link(dve.reciprocal(q, d))
            link(dve.tensor_tensor(q, q, y, ALU.mult))
            link(dve.tensor_tensor(q2, q, q, ALU.mult))
            link(dve.tensor_scalar(pl, q2, 1.0 / 17, None, ALU.mult))
            for k in range(15, 1, -2):
                link(dve.scalar_tensor_tensor(pl, pl, 1.0 / k, q2, ALU.add, ALU.mult))
            link(dve.scalar_tensor_tensor(pl, pl, 1.0, q, ALU.add, ALU.mult))
            link(dve.tensor_scalar(x, x, 0.0, None, ALU.max))
            link(dve.scalar_tensor_tensor(x, pl, 2.0, x, ALU.mult, ALU.add))
            dve.tensor_scalar(x[:, 0:LC], x[:, 0:LC], -8.0, None, ALU.mult).then_inc(sem("lru_rate"), 1)
            dve.wait_ge(*after("sp_exp", 2))
            dve.scalar_tensor_tensor(gate[:].rearrange("p (n h) -> p n h", h=H), heads, -1.0,
                                     row_par[:, 0].rearrange("p (a h) -> p a h", a=1).to_broadcast([P, TT + 1, H]),
                                     ALU.mult, ALU.mult).then_inc(sem("gdn_gate"), 1)
            dve.wait_ge(sem("stored"), 16 * 6)
            dve.memset(l2_root[:], 0.0).then_inc(sem("l2_clear"), 1)
            dve.wait_ge(*after("gates", LC))
            dve.wait_ge(*after("lru_rate", 1))
            for c in range(LC):
                ins = dve.tensor_scalar(gate_a[:, c], gate_a[:, c], x[:, c:c + 1], None, ALU.mult)
            ins.then_inc(sem("log_a"), 1)

            def scan_lru():
                dve.wait_ge(*after("lru_sqrt", 1))
                dve.wait_ge(*after("gated_x", 1))
                link(dve.scalar_tensor_tensor(gate_a[:], lru_a[:], 1.0, gate_a[:], ALU.add, ALU.mult))
                link(dve.tensor_tensor(gate_x[:], gate_x[:], gate_a[:], ALU.mult))
                hs = gate_a[:, :, 0:B]
                link(dve.tensor_tensor(hs, lru_a[:, :, SEQ:T], h0[:], ALU.mult))
                hx = lx[:].rearrange("p (c t) -> p c t", t=T)
                dve.tensor_tensor(hx[:, :, SEQ:T], gate_x[:, :, SEQ:T], hs, ALU.add)
                for c in range(LC):
                    ins = dve.tensor_tensor_scan(hx[:, c, 0:SEQ], lru_a[:, c, 0:SEQ], gate_x[:, c, 0:SEQ], 0.0, ALU.mult, ALU.add)
                ins.then_inc(sem("lru_scanned"), 1)

            norm_w = par[:, MISC["gdn_norm_w"]:MISC["gdn_norm_w"] + 1]

            def samples_start():
                for k, dst in enumerate((s_q, s_k, s_v)):
                    src = qkv[:].rearrange("p (c t) -> p t c", t=T)[:, SEQ:T, k * H:(k + 1) * H]
                    dve.tensor_copy(dst[:].rearrange("p (b h) -> p b h", h=H), src).then_inc(sem("s_cols"), 1)
                dve.tensor_copy(s_z[:].rearrange("p (b h) -> p b h", h=H), z[:].rearrange("p (c t) -> p t c", t=T)[:, SEQ:T, :]).then_inc(sem("s_cols"), 1)
                for k, t in enumerate((beta, gate)):
                    v = t[0:B, TT * H:(TT + 1) * H].rearrange("p (a h) -> p a h", a=1).to_broadcast([B, B, H])
                    e = ident[0:B, 0:B].rearrange("p (b a) -> p b a", a=1).to_broadcast([B, B, H])
                    ins = dve.tensor_tensor(s_wide[0:B, k].rearrange("p (b h) -> p b h", h=H), v, e, ALU.mult)
                ins.then_inc(sem("s_wide"), 1)
                dve.wait_ge(*after("s_bg_wide", 1))
                dve.wait_ge(*after("s_cols", 4))
                link(dve.tensor_tensor(s_wq[:, :, 0], s_k[:], s_bg[:, 0], ALU.mult))
                dve.memset(s_rows[:], 0.0)
                link(dve.tensor_copy(s_wq[:, :, 1], s_q[:]))
                link(dve.tensor_tensor(s_v[:], s_v[:], s_bg[:, 0], ALU.mult))
                dve.tensor_tensor(s_t[:], s_q[:], s_k[:], ALU.mult).then_inc(sem("s_products"), 1)

            def samples_step():
                dve.wait_ge(*after("s_qk_ready", 1))
                link(dve.tensor_copy(s_qk[:], ps[:, 1, 0:BH]))
                dve.wait_ge(*after("s_wS", 1))
                wS = ps[:, 4, 0:2 * BH].rearrange("p (m t) -> p m t", t=2)
                dve.tensor_tensor(s_new[:], s_v[:], wS[:, :, 0], ALU.subtract).then_inc(sem("s_new"), 1)
                dve.wait_ge(*after("s_new", 1))
                link(dve.tensor_tensor(s_o[:], s_qk[:], s_new[:], ALU.mult))
                link(dve.tensor_tensor(s_o[:], s_o[:], wS[:, :, 1], ALU.add))
                dve.tensor_tensor(s_t[:], s_o[:], s_o[:], ALU.mult).then_inc(sem("s_o_squares"), 1)
                dve.wait_ge(*after("s_rows_ready", 1))
                dve.tensor_copy(s_rows[0:BH], ps[0:BH, 6, 0:2 * P].rearrange("p (k v) -> p k v", k=2)).then_inc(sem("s_rows"), 1)
                dve.wait_ge(*after("s_o_summed", 1))
                dve.tensor_scalar(s_t[:], ps[:, 5, 0:BH], 1.0 / P, EPS, ALU.mult, ALU.add).then_inc(sem("s_var"), 1)
                dve.wait_ge(*after("s_root", 1))
                link(dve.reciprocal(s_t[:], s_t[:]))
                link(dve.scalar_tensor_tensor(s_o[:], s_o[:], norm_w, s_t[:], ALU.mult, ALU.mult))
                dve.tensor_tensor(z[:].rearrange("p (c t) -> p t c", t=T)[:, SEQ:T, :], s_o[:].rearrange("p (b h) -> p b h", h=H),
                                  s_z[:].rearrange("p (b h) -> p b h", h=H), ALU.mult).then_inc(sem("s_o_done"), 1)
                def diagonal(k):
                    if k >= 2:
                        dve.wait_ge(*after("s_outer", (k - 1) * SD // 4))
                    dve.tensor_tensor(s_diag[k % 2][:], s_rows[:, 0:1].to_broadcast([P, SD, P]),
                                      ident[:, k * SD:(k + 1) * SD].rearrange("p (m a) -> p m a", a=1).to_broadcast([P, SD, P]),
                                      ALU.mult).then_inc(sem("s_diag"), 1)
                diagonal(0)
                for k in range(BH // SD):
                    if k + 1 < BH // SD:
                        diagonal(k + 1)
                    for m in range(SD // 4):
                        u = k * (SD // 4) + m
                        dve.wait_ge(*after("s_outer", u + 1))
                        dve.tensor_tensor(s_S[:, 4 * u:4 * u + 4], ps[:, u % 4, :].rearrange("p (m v) -> p m v", v=P),
                                          s_S[:, 4 * u:4 * u + 4], ALU.add).then_inc(sem("s_S_new"), 1)

            dve.wait_ge(sem("stored"), 16 * 6)
            dve.tensor_copy(head_row[:], ident[:, 0:2 * H].rearrange("p (c a) -> p c a", a=1).to_broadcast([P, 2 * H, P])).then_inc(sem("head_row"), 1)
            dve.wait_ge(*after("l2_root", 1))
            dve.reciprocal(l2_root[0:2 * H], l2_root[0:2 * H]).then_inc(sem("l2_inverse"), 1)
            for c in range(2 * H):
                dve.wait_ge(*after("l2_wide", c + 1))
                b = 4 + c % 2 * 2
                v = qkv[:, c * T:(c + 1) * T].rearrange("p (h t) -> p h t", h=2)
                dve.scalar_tensor_tensor(v, v, P ** -0.5 if c < H else 1.0, ps[:, b:b + 2, 0:HALF], ALU.mult, ALU.mult).then_inc(sem("normed"), 1)
            dve.wait_ge(*after("normed", 2 * H))
            dve.wait_ge(*after("beta", 1))
            dve.wait_ge(*after("gdn_gate", 1))
            samples_start()
            scan_lru()
            samples_step()
            dve.wait_ge(*after("gc_summed", 1))
            link(dve.tensor_copy(gc[:], ps[:, 4, 0:TT * H]))
            dve.tensor_copy(glast[:], ps[:, 4, TT * H:2 * TT * H])
            dve.tensor_tensor(dgc[:], ps[:, 4, TT * H:2 * TT * H], gc[:], ALU.subtract).then_inc(sem("gc_ready"), 1)
            dve.wait_ge(*after("gc_exps", 3))
            dve.wait_ge(*after("beta", 1))
            dve.tensor_tensor(begc[:], beta[:, 0:TT * H], egc[:], ALU.mult).then_inc(sem("gdn_small"), 1)
            for g in range(2):
                ins = dve.memset(S[g][:], 0.0)
            ins.then_inc(sem("S_clear"), 1)
            for k in range(2):
                dve.wait_ge(*after("h_turned", k + 1))
                dve.tensor_copy(h_rows[0:B + 1, k * 512:(k + 1) * 512], ps[0:B + 1, 6 + k, :]).then_inc(sem("h_rows"), 1)
            dve.wait_ge(*after("gdn_small", 1))
            dve.wait_ge(*after("S_clear", 1))
            dve.wait_ge(sem("masks"), 3 + LEVELS)

            def wide(t, n, g):
                return t[:, bass.ds(n * H + g * HG, HG)].rearrange("p (h a) -> p h a", a=1).to_broadcast([P, HG, P])

            def bank(k):
                return ps[:, k, :].rearrange("p (h j) -> p h j", h=HG)

            def chunk(n):
                for g in range(2):
                    dve.wait_ge(*step("grow", g, n))
                    dve.tensor_tensor(inv_t[g][:], bank(4 * g), wide(gc, n, g), ALU.subtract).then_inc(chunk_sem("differ", g), 1)
                    dve.wait_ge(*step("differ", g, n))
                    dve.tensor_scalar(inner[g][:], inv_t[g][:], 0.0, None, ALU.max)
                    dve.tensor_scalar(qk[g][:], inv_t[g][:], 0.0, None, ALU.min).then_inc(chunk_sem("differences", g), 1)
                for g in range(2):
                    dve.wait_ge(*step("k_turned", g, n))
                    dve.tensor_tensor(kbg[g][:], bank(4 * g + 3), wide(begc, n, g), ALU.mult)
                    dve.tensor_tensor(kdec[g][:], bank(4 * g + 3), wide(dgc, n, g), ALU.mult).then_inc(chunk_sem("k_rows", g), 1)
                    dve.wait_ge(*step("v_turned", g, n))
                    dve.tensor_tensor(vb[g][:], bank(4 * g), wide(beta, n, g), ALU.mult).then_inc(chunk_sem("v_rows", g), 1)
                for g in range(2):
                    dve.wait_ge(*step("kk_ready", g, n))
                    dve.wait_ge(*step("inner_beta", g, n))
                    dve.tensor_tensor(inner[g][:], bank(4 * g + 1), inner[g][:], ALU.mult).then_inc(chunk_sem("inner", g), 1)
                    dve.wait_ge(*step("qk_ready", g, n))
                    dve.wait_ge(*step("qk_mask", g, n))
                    dve.tensor_tensor(qk[g][:], bank(4 * g + 2), qk[g][:], ALU.mult).then_inc(chunk_sem("qk", g), 1)
                eye = ident[:].rearrange("p (a j) -> p a j", a=1).to_broadcast([P, HG, P])
                for l in range(LEVELS):
                    mask = blocks_mask[:, l].rearrange("p (a j) -> p a j", a=1).to_broadcast([P, HG, P])
                    for g in range(2):
                        dve.wait_ge(*step(f"half_ready{l}", g, n))
                        dve.tensor_tensor(half_t[g][:], bank(4 * g), mask, ALU.mult).then_inc(chunk_sem(f"half{l}", g), 1)
                    for g in range(2):
                        if l == 0:
                            dve.wait_ge(*step("half0", g, n))
                            dve.tensor_tensor(inv_t[g][:], half_t[g][:], eye, ALU.add).then_inc(chunk_sem("inv_t0", g), 1)
                            pairs = pair_mask[:].rearrange("p (a j) -> p a j", a=1).to_broadcast([P, HG, P])
                            dve.tensor_tensor(inv[g][:], inner[g][:], pairs, ALU.mult).then_inc(chunk_sem("pairs", g), 1)
                            dve.wait_ge(*step("pairs", g, n))
                            dve.tensor_tensor(inv[g][:], inv[g][:], eye, ALU.add).then_inc(chunk_sem("inv0", g), 1)
                            continue
                        dve.wait_ge(*step(f"inv_t_ready{l}", g, n))
                        dve.tensor_tensor(inv_t[g][:], bank(4 * g + 1), inv_t[g][:], ALU.add).then_inc(chunk_sem(f"inv_t{l}", g), 1)
                        if l < LEVELS - 1:
                            dve.wait_ge(*step(f"inv_ready{l}", g, n))
                            dve.tensor_tensor(inv[g][:], bank(4 * g + 2), inv[g][:], ALU.add).then_inc(chunk_sem(f"inv{l}", g), 1)
                for g in range(2):
                    dve.wait_ge(*step("S_ready", g, n))
                    for h in range(HG):
                        ins = dve.scalar_tensor_tensor(S[g][:, h], S[g][:, h], glast[:, bass.ds(n * H + (g * HG + h), 1)],
                                                       ps[:, 4 * g + 2, h * P:(h + 1) * P], ALU.mult, ALU.add)
                    ins.then_inc(chunk_sem("S_done", g), 1)
            loop(dve, 0, TT, chunk)

            halves = [(gy, 0), (gy, 1), (z, 0), (z, 1)]

            def mixed_low(k):
                src, part = halves[k]
                dve.wait_ge(*after("mixed_high", k + 1))
                if k == 1:
                    dve.wait_ge(sem("stored"), 16 * (6 + 2 + 2))
                dve.tensor_tensor(x_low[:, 4 * k:4 * k + 4], src[:, part * 4 * T:(part + 1) * 4 * T].rearrange("p (c t) -> p c t", t=T),
                                  x_high[:, 4 * k:4 * k + 4].bitcast(F32), ALU.subtract).then_inc(sem("mixed_low"), 1)

            for s in range(SPLIT):
                split_low(g_out, 0, s)
            for g in range(2):
                dve.wait_ge(*step("o_taken", g, TT - 1))
            dve.tensor_scalar(o_ms[:], o_ms[:], 1.0 / P, EPS, ALU.mult, ALU.add).then_inc(sem("o_ms"), 1)
            dve.wait_ge(*after("o_root", 1))
            link(dve.reciprocal(o_root[:], o_root[:]))
            o4 = qkv[:].rearrange("p (c t) -> p c t", t=T)
            for h in range(H):
                ins = dve.tensor_tensor(o4[:, 2 * H + h, 0:SEQ].rearrange("p (n v) -> p n v", v=P),
                                        o4[:, 2 * H + h, 0:SEQ].rearrange("p (n v) -> p n v", v=P),
                                        o_root[:, h * TT:(h + 1) * TT].rearrange("p (n a) -> p n a", a=1).to_broadcast([P, TT, P]), ALU.mult)
                ins.then_inc(sem("o_normed"), 1)
            for h in range(H):
                dve.wait_ge(*after("o_turned", h + 1))
                dve.scalar_tensor_tensor(z[:, h * T:h * T + SEQ], ps[:, O_BANK + h % 4, :], norm_w, z[:, h * T:h * T + SEQ],
                                         ALU.mult, ALU.mult).then_inc(sem("o_done"), 1)
                if h == 3:
                    mixed_low(0)
            for k in range(1, 4):
                mixed_low(k)

            def two(t):
                return t.rearrange("p (h t) -> p h t", h=2)

            def rstd(r, bank):
                s = xsum if r % 2 else ssum
                dve.wait_ge(sem("summed"), r + 1)
                dve.tensor_scalar(two(s[:]), ps[:, bank:bank + 2, 0:HALF], 1.0 / D, EPS, ALU.mult, ALU.add).then_inc(sem("mean"), 1)
                dve.wait_ge(sem("rooted"), r + 1)
                link(dve.reciprocal(s[:], s[:]))

            def residual(r, post, pre, g_next=None):
                rstd(2 * r, 0)
                x = xt if r < 2 else xt_last
                if r:
                    dve.wait_ge(sem("x_back"), 16 * r)
                else:
                    dve.wait_ge(*after("x_turns_taken", TT * 4 + 1))

                def weigh(c):
                    dve.scalar_tensor_tensor(branch[:, c], branch[:, c], par[:, NORM[post] + c:NORM[post] + c + 1], ssum[:],
                                             ALU.mult, ALU.mult).then_inc(sem("post"), 1)

                def low(c):
                    dve.wait_ge(sem("norm_high"), r * NC + c + 1)
                    dve.scalar_tensor_tensor(x_low[:, c], xt[:, c], par[:, NORM[pre] + c:NORM[pre] + c + 1], x_high[:, c].bitcast(F32),
                                             ALU.mult, ALU.subtract).then_inc(sem("norm_low"), 1)
                weigh(0)
                for c in range(NC):
                    if r == 2 and c % 2:
                        continue
                    if pre and c in SPLIT_AT:
                        split_low(g_next, 0, SPLIT_AT[c])
                    for m in ((c + 1, c + 2) if r == 2 else (c + 1,)):
                        if m < NC:
                            weigh(m)
                    dve.wait_ge(sem("post"), r * NC + c + 1)
                    dve.tensor_tensor(x[:, c], x[:, c], branch[:, c], ALU.add).then_inc(sem("x_new"), 1)
                    if pre and c:
                        low(c - 1)
                if pre:
                    low(NC - 1)

            gemm(g_out, nothing)
            residual(0, "norm_mix_post", "norm_xa_pre", g_q)

            def scale_q(it, j):
                b = g_q.acc(j) * 4
                if type(it) is int and j == 0:
                    rstd(1, g_q.acc(1) * 4)
                dve.wait_ge(sem("slab_used"), g_q.slab(it, (j + 1) * g_q.slabs - 1) + 1)
                f = q_t[:].rearrange("p c t -> p (c t)")
                for m in range(2):
                    out = f[:, bass.ds((it * g_q.blocks + j) * (2 * T) + m * T, T)]
                    ins = dve.tensor_tensor(two(out), ps[:, b + 2 * m:b + 2 * m + 2, 0:HALF], two(xsum[:]), ALU.mult)
                ins.then_inc(sem("acc_taken"), 1)
            gemm(g_q, scale_q, peel=1)

            def row_max(h, t):
                if t % 2:
                    return
                n = h * TT + t
                dve.wait_ge(sem("scores"), n // 2 + 1)
                link(dve.tensor_reduce(stats[:, 0, n:n + 2], ps[:, h % 2 * 2 + t // 2, :].rearrange("p (t m) -> p t m", t=2), AX_X, ALU.max))
                dve.tensor_scalar(stats[:, 0, n:n + 2], stats[:, 0, n:n + 2], -SCALE, None, ALU.mult).then_inc(sem("row_max"), 1)

            def normalize(h, t):
                n = h * TT + t
                dve.wait_ge(sem("exponentials"), n + 1)
                link(dve.reciprocal(stats[:, 2, n:n + 1], stats[:, 1, n:n + 1]))
                dve.tensor_scalar(probs[:, t], probs[:, t], stats[:, 2, n:n + 1], None, ALU.mult).then_inc(sem("probs"), 1)

            def sample_scores(k):
                b, c = k // MT, k % MT
                dve.wait_ge(sem(f"cache{c}"), 16 * (b + 1))
                dve.wait_ge(sem(f"q_wide{b % 2}"), 16 * (b // 2 + 1))
                hd = D // XH_
                for h in range(XH_):
                    tile = cache[:, c, h * hd:(h + 1) * hd]
                    ins = dve.tensor_tensor_reduce(tile, tile, q_wide[b % 2][:, h * hd:(h + 1) * hd], 1.0, 0.0, ALU.mult, ALU.add,
                                                   s_scores[:, c, b * XH_ + h:b * XH_ + h + 1])
                ins.then_inc(sem("s_scored"), 1)

            dve.wait_ge(sem("x_mid"), 16)
            EARLY = 2
            for t in range(TT):
                row_max(0, t)
                if t:
                    normalize(0, t - 1)
            normalize(0, TT - 1)
            for k in range(EARLY):
                sample_scores(k)
            for h in range(XH_):
                for t in range(TT):
                    if h + 1 < XH_:
                        row_max(h + 1, t)
                    if h * TT + t + EARLY < B * MT:
                        sample_scores(h * TT + t + EARLY)
                    n = h * DC + t
                    dve.wait_ge(sem("pv_high"), n + 1)
                    dve.tensor_tensor(x_low[:, n, 0:SEQ], ps[:, 6 + n % 2, :], x_high[:, n, 0:SEQ].bitcast(F32), ALU.subtract).then_inc(sem("pv_low"), 1)
                    if h + 1 < XH_:
                        normalize(h + 1, t)
            R = B * XH_
            dve.wait_ge(*after("s_turned", 1))
            link(dve.tensor_reduce(s_stats[0:R, 0:1], ps[0:R, 0, 0:M], AX_X, ALU.max))
            dve.tensor_scalar(s_stats[0:R, 1:2], s_stats[0:R, 0:1], -SCALE, None, ALU.mult).then_inc(sem("s_max"), 1)
            dve.wait_ge(*after("s_exp", 1))
            link(dve.reciprocal(s_stats[0:R, 3:4], s_stats[0:R, 2:3]))
            dve.tensor_scalar(s_probs[0:R], s_probs[0:R], s_stats[0:R, 3:4], None, ALU.mult).then_inc(sem("s_probs"), 1)
            dve.wait_ge(*after("s_probs_turned", 1))
            dve.wait_ge(*after("eye_b", 2))
            for c in range(MT):
                for b in range(B):
                    p = ps[:, 1, c * R + b * XH_:c * R + (b + 1) * XH_].rearrange("p (h a) -> p h a", a=1).to_broadcast([P, XH_, B])
                    e = eye_b[:, b:b + 1, :].to_broadcast([P, XH_, B])
                    ins = dve.tensor_tensor(spread[:, c, b], p, e, ALU.mult)
            ins.then_inc(sem("s_spread"), 1)
            dve.wait_ge(*after("s_o_high", 1))
            dve.tensor_tensor(x_low[:, :, SEQ:T], ps[:, 2, 0:NC * B].rearrange("p (c b) -> p c b", b=B),
                              x_high[:, :, SEQ:T].bitcast(F32), ALU.subtract).then_inc(sem("s_o_low"), 1)

            gemm(g_o, nothing)
            residual(1, "norm_xa_post", "norm_ffn_pre", ffn[0][2])

            for c0, n, g_up, g_down in ffn:
                def hidden(it, j, g=g_up, c0=c0):
                    chunk = it * 2 + j
                    b = g.acc(j) * 4
                    if c0 == 0 and type(it) is int and j == 0:
                        rstd(3, g.acc(1) * 4)
                    dve.wait_ge(sem("slab_used"), g.slab(it, (j + 1) * g.slabs - 1) + 1)
                    dve.tensor_tensor(two(sq[:, j]), ps[:, b:b + 2, 0:HALF], two(xsum[:]), ALU.mult).then_inc(sem("gate_scaled"), 1)
                    dve.tensor_tensor(two(xw[:]), ps[:, b + 2:b + 4, 0:HALF], two(xsum[:]), ALU.mult).then_inc(sem("acc_taken"), 1)
                    dve.wait_ge(sem("silu"), chunk + (c0 + 1))
                    dve.wait_ge(sem("acc_taken"), g.block(it, j) + 1)
                    dve.tensor_tensor(xw[:], xw[:], sq[:, j], ALU.mult).then_inc(sem("hidden"), 1)
                    dve.wait_ge(sem("h_high"), chunk + (c0 + 1))
                    c = bass.ds(chunk * T, T)
                    dve.tensor_tensor(h_low[:].rearrange("p c t -> p (c t)")[:, c], xw[:],
                                      h_high[:].rearrange("p c t -> p (c t)")[:, c].bitcast(F32), ALU.subtract).then_inc(sem("h_low"), 1)

                def add_down(it, j, g=g_down, c0=c0):
                    b = g.acc(j) * 4
                    dve.wait_ge(sem("slab_used"), g.slab(it, (j + 1) * g.slabs - 1) + 1)
                    f = branch[:].rearrange("p c t -> p (c t)")
                    for m in range(2):
                        out = f[:, bass.ds((it * g.blocks + j) * (2 * T) + m * T, T)].rearrange("p (h t) -> p h t", h=2)
                        acc = ps[:, b + 2 * m:b + 2 * m + 2, 0:HALF]
                        if c0:
                            ins = dve.tensor_tensor(out, acc, out, ALU.add)
                        else:
                            ins = dve.tensor_copy(out, acc)
                    ins.then_inc(sem("acc_taken"), 1)
                gemm(g_up, hidden, peel=c0 == 0)
                gemm(g_down, add_down)
            residual(2, "norm_ffn_post", None)

        @block_.tensor
        def _(pe):
            pe.wait_ge(sem("consts"), 4)
            def turn(tiles):
                for k in tiles:
                    t, c, per, n, to = turns[k]
                    pe.wait_ge(sem("rows_scaled"), t + 1)
                    if k >= TURN_BANKS:
                        pe.wait_ge(sem("turn_low"), k - TURN_BANKS + 1)
                    for q in range(per):
                        ins = pe.transpose(ps[:, turn_bank(k), q * n:(q + 1) * n], row_tiles[t][0][0:n, (c + q) * P:(c + q + 1) * P], ident[0:n, 0:n])
                    ins.then_inc(sem("turned"), 1)

            def turn_small():
                pe.wait_ge(sem("par_loaded"), 16 * (len(params) + 2 * (TAPS - 1) + 3))
                for k in range(3):
                    ins = pe.transpose(ps[:, 1, k * P:k * P + PAR_ROWS[k]], par_rows[0:PAR_ROWS[k], k, :], ident[0:PAR_ROWS[k], 0:PAR_ROWS[k]])
                ins.then_inc(sem("small_turned"), 1)
                NS = B * (TAPS - 1)
                for c in range(LC):
                    pe.transpose(ps[:, 3, c * NS:(c + 1) * NS], state_rows[0:NS, c * P:(c + 1) * P], ident[0:NS, 0:NS])
                for c in range(LC):
                    ins = pe.transpose(ps[:, 3, LC * NS + c * B:LC * NS + (c + 1) * B], h0_rows[0:B, c * P:(c + 1) * P], ident[0:B, 0:B])
                ins.then_inc(sem("small_turned"), 1)
                for k in range(2):
                    for c in range(GC // 2):
                        cc = LC + k * GC // 2 + c
                        ins = pe.transpose(ps[:, 5 + 2 * k, c * NS:(c + 1) * NS], state_rows[0:NS, cc * P:(cc + 1) * P], ident[0:NS, 0:NS])
                    ins.then_inc(sem("small_turned"), 1)
                pe.wait_ge(sem("small_copied"), 4)

            turn(range(mem_turns))
            pe.wait_ge(sem("turn_low"), mem_turns)

            def gemm(g, m_chunks=2, ready=None, after_first=None):
                def body(it):
                    for j in range(g.blocks):
                        first = type(it) is int and g.block(it, j) < 2
                        if not first:
                            pe.wait_ge(sem("acc_taken"), g.block(it, j) - 1)
                        if after_first and type(it) is int and j == 1:
                            pe.wait_ge(sem("mean"), after_first[1])
                        b = g.acc(j) * 4
                        for s in range(g.slabs):
                            jj = j * g.slabs + s
                            slot = (g.slab0 + jj) % SPLIT
                            pe.wait_ge(sem("w_low_ready"), g.slab(it, jj) + 1)
                            by_chunk = ready and ready[2] == KS and type(it) is int and j == 0
                            if ready and not by_chunk:
                                pe.wait_ge(ready[0], ready[1] + min((s + 1) * ready[2], g.chunks))
                            for k in range(min(KS, g.chunks - s * KS)):
                                c = s * KS + k
                                if by_chunk:
                                    pe.wait_ge(ready[0], ready[1] + c + 1)
                                for m in range(m_chunks):
                                    for n, (w, x) in enumerate(((w_high, g.high), (w_high, g.low), (w_low, g.high))):
                                        flags = dict(start=(c == 0 and n == 0), stop=(c == g.chunks - 1 and n == 2))
                                        wk = w[:, slot, k, m * P:(m + 1) * P]
                                        if g.memory:
                                            ins = pe.matmul(ps[:, b + 2 * m, 0:COLS], x[:, c, m * P:(m + 1) * P], w[:, slot, k, :], **flags)
                                        else:
                                            for h in range(2):
                                                ins = pe.matmul(ps[:, b + 2 * m + h, 0:HALF], wk, x[:, c, h * HALF:(h + 1) * HALF], **flags)
                            ins.then_inc(sem("slab_used"), 1)
                        if after_first and type(it) is int and j == 0:
                            after_first[0]()
                peel = g.name == first_gemm.name or after_first is not None
                if peel:
                    body(0)
                loop(pe, int(peel), g.iters, body)

            gemm(g_wk)
            turn_small()
            turn(range(mem_turns, len(turns)))
            for g in (g_wv, g_lx, g_ly, g_qkv, g_z, g_bg):
                gemm(g, 1 if g is g_bg else 2)
            for k in range(CC // 4):
                if k == 0:
                    pe.wait_ge(sem("acc_taken"), g_bg.block0)
                if k >= 4:
                    pe.wait_ge(*after("edge_copied", k - 3))
                for q in range(4):
                    ins = pe.transpose(ps[0:EDGE, 4 + k % 4, q * P:(q + 1) * P], edge[:, 4 * k + q, :], ident[:])
                ins.then_inc(sem("edge_turned"), 1)
            pe.wait_ge(sem("acc_taken"), g_bg.block0 + 1)
            for n in range(TT):
                pe.transpose(ps[:, 1, n * 40:(n + 1) * 40], bg_rows[0:40, n * P:(n + 1) * P], ident[0:40, 0:40])
            pe.transpose(ps[0:B, 1, TT * 40:TT * 40 + 40], bg_rows[0:40, SEQ:T], ident[0:40, 0:40]).then_inc(sem("bg_turned"), 1)
            pe.wait_ge(sem("lru_w_loaded"), 32)
            pe.wait_ge(*after("edge_copied", CC // 4))
            pe.wait_ge(*after("sp_abs", 1))
            for c in range(LC):
                if c >= 2:
                    pe.wait_ge(*after("gates", c - 1))
                for k in range(2):
                    for h in range(2):
                        ins = pe.matmul(ps[:, c % 2 * 4 + 2 * k + h, 0:HALF], lru_w[:, k, c, :],
                                        lx[:, c * T + h * HALF:c * T + (h + 1) * HALF], start=True, stop=True)
                ins.then_inc(sem("gates_ready"), 1)
            pe.wait_ge(*after("gates", LC))
            pe.wait_ge(sem("head_col"), 1)
            for c in range(2 * H):
                pe.wait_ge(*after("l2_squares", c + 1))
                for h in range(2):
                    ins = pe.matmul(ps[0:2 * H, h, 0:HALF], head_col[:, 2 * H - 1 - c:4 * H - 1 - c], l2_sq[:, c % 2, h * HALF:(h + 1) * HALF],
                                    start=c == 0, stop=c == 2 * H - 1)
                ins.then_inc(sem("l2_summed"), 1)
            pe.wait_ge(*after("head_row", 1))
            pe.wait_ge(*after("l2_inverse", 1))
            for c in range(2 * H):
                if c >= 2:
                    pe.wait_ge(*after("normed", c - 1))
                for h in range(2):
                    ins = pe.matmul(ps[:, 4 + c % 2 * 2 + h, 0:HALF], head_row[:, c], l2_root[:, h * HALF:(h + 1) * HALF], start=True, stop=True)
                ins.then_inc(sem("l2_wide"), 1)
            pe.wait_ge(*after("s_wide", 1))
            pe.matmul(ps[:, 0, 0:2 * BH], ones[0:B, :], s_wide[0:B].rearrange("p k m -> p (k m)"), start=True, stop=True).then_inc(sem("s_wide_ready"), 1)
            pe.wait_ge(*after("s_products", 1))
            pe.matmul(ps[:, 1, 0:BH], ones[:], s_t[:], start=True, stop=True).then_inc(sem("s_qk_ready"), 1)
            for m in range(BH):
                if m % H == 0:
                    pe.wait_ge(sem("s_decayed"), m // H + 1)
                ins = pe.matmul(ps[:, 4, 2 * m:2 * m + 2], s_S[:, m, :], s_wq[:, m, :], start=True, stop=True)
            ins.then_inc(sem("s_wS"), 1)
            pe.wait_ge(*after("s_new", 1))
            pe.transpose(ps[0:BH, 6, 0:P], s_new[:], ident[:])
            pe.transpose(ps[0:BH, 6, P:2 * P], s_k[:], ident[:]).then_inc(sem("s_rows_ready"), 1)
            pe.wait_ge(*after("s_o_squares", 1))
            pe.matmul(ps[:, 5, 0:BH], ones[:], s_t[:], start=True, stop=True).then_inc(sem("s_o_summed"), 1)
            for u in range(BH // 4):
                pe.wait_ge(sem("s_diag"), u * 4 // SD + 1)
                if u >= 4:
                    pe.wait_ge(sem("s_S_new"), u - 3)
                d = s_diag[u * 4 // SD % 2]
                m = u * 4 % SD
                pe.matmul(ps[:, u % 4, :], s_rows[:, 1], d[:, m:m + 4], start=True, stop=True).then_inc(sem("s_outer"), 1)
            pe.wait_ge(*after("gdn_gate", 1))
            pe.wait_ge(sem("masks"), 3 + LEVELS)
            pe.matmul(ps[:, 4, 0:TT * H], upper[:], gate[:, 0:TT * H], start=True, stop=True)
            pe.matmul(ps[:, 4, TT * H:2 * TT * H], ones[:], gate[:, 0:TT * H], start=True, stop=True).then_inc(sem("gc_summed"), 1)
            hx = lx[:].rearrange("p (c t) -> p c t", t=T)
            for k in range(2):
                for q in range(4):
                    ins = pe.transpose(ps[0:B + 1, 6 + k, q * P:(q + 1) * P], hx[:, 4 * k + q, SEQ - 1:T], ident[:])
                ins.then_inc(sem("h_turned"), 1)
            pe.wait_ge(*after("gdn_small", 1))
            pe.wait_ge(*after("S_clear", 1))
            pe.wait_ge(sem("s_S_new"), BH // 4)
            pe.wait_ge(*after("h_rows", 2))

            def heads(g):
                return ((h, slice(h * P, (h + 1) * P)) for h in range(HG))

            def chunk(n):
                later = type(n) is not int
                for g in range(2):
                    b = 4 * g
                    if later:
                        pe.wait_ge(*step("v_new", g, n - 1))
                    pe.wait_ge(*step("gate_wide", g, n))
                    pe.matmul(ps[:, b, :], ones[:], inv[g][:], start=True, stop=True).then_inc(chunk_sem("grow_ready", g), 1)
                    pe.wait_ge(*step("keys", g, n))
                    if later:
                        pe.wait_ge(*step("wt", g, n - 1))
                    for h, c in heads(g):
                        ins = pe.transpose(ps[:, b + 3, c], keys[g][:, h], ident[:])
                    ins.then_inc(chunk_sem("k_turned", g), 1)
                    if later:
                        pe.wait_ge(*step("o_taken", g, n - 1))
                    for h, c in heads(g):
                        ins = pe.matmul(ps[:, b + 1, c], keys[g][:, h], keys[g][:, h], start=True, stop=True)
                    ins.then_inc(chunk_sem("kk_ready", g), 1)
                    if later:
                        pe.wait_ge(*step("S_done", g, n - 1))
                    for h, c in heads(g):
                        q = qkv[:, bass.ds(n * P + (g * HG + h) * T, P)]
                        ins = pe.matmul(ps[:, b + 2, c], keys[g][:, h], q, start=True, stop=True)
                    ins.then_inc(chunk_sem("qk_ready", g), 1)
                for g in range(2):
                    b = 4 * g
                    pe.wait_ge(*step("values", g, n))
                    pe.wait_ge(*step("differences", g, n))
                    pe.wait_ge(*step("grow", g, n))
                    for h, c in heads(g):
                        ins = pe.transpose(ps[:, b, c], values[g][:, h], ident[:])
                    ins.then_inc(chunk_sem("v_turned", g), 1)
                for l in range(LEVELS):
                    for g in range(2):
                        b = 4 * g
                        if l == 0:
                            pe.wait_ge(*step("v_rows", g, n))
                            pe.wait_ge(*step("inner", g, n))
                        else:
                            pe.wait_ge(*step(f"inv_t{l - 1}", g, n))
                        for h, c in heads(g):
                            ins = pe.matmul(ps[:, b, c], inner[g][:, h], inv_t[g][:, h] if l else ident[:], start=True, stop=True)
                        ins.then_inc(chunk_sem(f"half_ready{l}", g), 1)
                    for g in range(2):
                        if l == 0:
                            continue
                        b = 4 * g
                        pe.wait_ge(*step(f"inv{l - 1}", g, n))
                        pe.wait_ge(*step(f"half{l}", g, n))
                        for h, c in heads(g):
                            ins = pe.matmul(ps[:, b + 1, c], inv[g][:, h], half_t[g][:, h], start=True, stop=True)
                        ins.then_inc(chunk_sem(f"inv_t_ready{l}", g), 1)
                        if l < LEVELS - 1:
                            if l == 1:
                                pe.wait_ge(*step("qk", g, n))
                            for h, c in heads(g):
                                ins = pe.matmul(ps[:, b + 2, c], half_t[g][:, h], inv[g][:, h], start=True, stop=True)
                            ins.then_inc(chunk_sem(f"inv_ready{l}", g), 1)
                for g in range(2):
                    b = 4 * g
                    pe.wait_ge(*step(f"inv_t{LEVELS - 1}", g, n))
                    pe.wait_ge(*step("k_rows", g, n))
                    for h, c in heads(g):
                        ins = pe.matmul(ps[:, b + 3, c], kbg[g][:, h], inv_t[g][:, h], start=True, stop=True)
                    ins.then_inc(chunk_sem("wt_ready", g), 1)
                for g in range(2):
                    b = 4 * g
                    pe.wait_ge(*step("wt", g, n))
                    if later:
                        pe.wait_ge(*step("S_done", g, n - 1))
                    for h, c in heads(g):
                        pe.matmul(ps[:, b, c], inv_t[g][:, h], vb[g][:, h], start=True, stop=False)
                        ins = pe.matmul(ps[:, b, c], kbg[g][:, h], S[g][:, h], start=False, stop=True)
                    ins.then_inc(chunk_sem("v_new_ready", g), 1)
                for g in range(2):
                    b = 4 * g
                    pe.wait_ge(*step("v_new", g, n))
                    pe.wait_ge(*step("q_scaled", g, n))
                    for h, c in heads(g):
                        pe.matmul(ps[:, b + 1, c], grow[g][:, h], S[g][:, h], start=True, stop=False)
                        ins = pe.matmul(ps[:, b + 1, c], qk[g][:, h], vb[g][:, h], start=False, stop=True)
                    ins.then_inc(chunk_sem("o_ready", g), 1)
                    for h, c in heads(g):
                        ins = pe.matmul(ps[:, b + 2, c], kdec[g][:, h], vb[g][:, h], start=True, stop=True)
                    ins.then_inc(chunk_sem("S_ready", g), 1)
            chunk(0)
            loop(pe, 1, TT, chunk)

            for g in range(2):
                pe.wait_ge(*step("S_done", g, TT - 1))
                pe.wait_ge(*step("o_taken", g, TT - 1))
            for h in range(H):
                pe.wait_ge(*after("o_normed", h + 1))
                if h >= 4:
                    pe.wait_ge(*after("o_done", h - 3))
                for n in range(TT):
                    c = (2 * H + h) * T + n * P
                    ins = pe.transpose(ps[:, O_BANK + h % 4, n * P:(n + 1) * P], qkv[:, c:c + P], ident[:])
                ins.then_inc(sem("o_turned"), 1)
            def summed(s, bank=0):
                for h in range(2):
                    ins = pe.matmul(ps[:, bank + h, 0:HALF], ones[:], s[:, h * HALF:(h + 1) * HALF], start=True, stop=True)
                ins.then_inc(sem("summed"), 1)

            def new_squares_summed(r, g):
                def sums():
                    pe.wait_ge(sem("acc_taken"), g.block0)
                    pe.wait_ge(sem("x_added"), (r + 1) * NC)
                    summed(xsum, g.acc(1) * 4)
                return sums

            def residual_sums(r):
                pe.wait_ge(sem("acc_taken"), (g_out, g_o, ffn[-1][3])[r].block0 + DB)
                pe.wait_ge(sem("sq"), (r + 1) * 3 * DB)
                summed(ssum)

            gemm(g_out, ready=(sem("mixed_low"), 0, 1))
            pe.wait_ge(sem("acc_taken"), g_out.block0 + DB)
            pe.wait_ge(sem("x_rows"), 16)
            for turn, t in enumerate(x_order):
                rows, n, per = (x_rows2[:, t], P, 4) if t < TT else (xs_rows2[0:B], B, NC)
                if t == TT:
                    pe.wait_ge(sem("xs_rows"), 16)
                for c in range(0, NC, per):
                    k = turn * 4 + c // per
                    if k >= 4:
                        pe.wait_ge(*after("x_turns_taken", k - 3))
                    for q in range(per):
                        ins = pe.transpose(ps[:, 4 + k % 4, q * n:(q + 1) * n], rows[:, (c + q) * P:(c + q + 1) * P], ident[0:n, 0:n])
                    ins.then_inc(sem("x_turned"), 1)
            pe.wait_ge(sem("sq"), 3 * DB)
            summed(ssum)
            pe.wait_ge(sem("mean"), 1)
            gemm(g_q, ready=(sem("norm_low"), 0, KS), after_first=(new_squares_summed(0, g_q), 2))

            pe.wait_ge(sem("acc_taken"), g_q.block0 + DB)
            for k in range(XH_):
                for q in range(4):
                    ins = pe.transpose(ps[0:B, 4 + k, q * P:(q + 1) * P], q_t[:, 4 * k + q, SEQ:T], ident[:])
                ins.then_inc(sem("qs_turned"), 1)
            pe.wait_ge(*after("qs_rows", XH_))
            pe.wait_ge(sem("k_rows"), 16)
            for k in range(NC // 2):
                if k >= 4:
                    pe.wait_ge(*after("k_t", k - 3))
                for q in range(2):
                    for m in range(MT):
                        c = 2 * k + q
                        ins = pe.transpose(ps[:, 4 + k % 4, q * M + m * P:q * M + (m + 1) * P], kv_rows[:, m, c * P:(c + 1) * P], ident[:])
                ins.then_inc(sem("k_t_turned"), 1)

            pe.wait_ge(*after("k_t", NC // 2))

            def scores(h):
                for pair in range(2):
                    if h >= 2:
                        pe.wait_ge(sem("exponentials"), (h - 2) * TT + 2 * pair + 2)
                    for t in (2 * pair, 2 * pair + 1):
                        for c in range(DC):
                            ins = pe.matmul(ps[:, h % 2 * 2 + pair, t % 2 * M:(t % 2 + 1) * M], q_t[:, h * DC + c, t * P:(t + 1) * P],
                                            k_t[:, h * DC + c, :], start=c == 0, stop=c == DC - 1)
                    ins.then_inc(sem("scores"), 1)

            scores(0)
            scores(1)
            pe.wait_ge(*after("qs_rows", XH_))
            pe.wait_ge(sem("v_rows"), 16)
            for h in range(XH_):
                pe.wait_ge(sem("probs"), (h + 1) * TT)
                if h:
                    pe.wait_ge(sem("probs_t"), h)
                for t in range(TT):
                    for m in range(MT):
                        ins = pe.transpose(ps[:, 4 + t // 2, (t % 2 * MT + m) * P:(t % 2 * MT + m + 1) * P], probs[:, t, m * P:(m + 1) * P], ident[:])
                ins.then_inc(sem("probs_turned"), 1)
                pe.wait_ge(sem("probs_t"), h + 1)
                for c in range(DC):
                    n = h * DC + c
                    if n >= 2:
                        pe.wait_ge(sem("pv_low"), n - 1)
                    for m in range(MT):
                        ins = pe.matmul(ps[:, 6 + n % 2, :], kv_rows[:, m, n * P:(n + 1) * P], probs_t[:, m, :], start=m == 0, stop=m == MT - 1)
                    ins.then_inc(sem("pv_ready"), 1)
                if h + 2 < XH_:
                    scores(h + 2)
            R = B * XH_
            pe.wait_ge(sem("s_scored"), B * MT)
            pe.wait_ge(sem("exponentials"), XH_ * TT)
            for m in range(MT):
                ins = pe.transpose(ps[0:R, 0, m * P:(m + 1) * P], s_scores[:, m, :], ident[:])
            ins.then_inc(sem("s_turned"), 1)
            pe.wait_ge(*after("s_probs", 1))
            for m in range(MT):
                ins = pe.transpose(ps[:, 1, m * R:(m + 1) * R], s_probs[0:R, m * P:(m + 1) * P], ident[0:R, 0:R])
            ins.then_inc(sem("s_probs_turned"), 1)
            pe.wait_ge(*after("s_spread", 1))
            pe.wait_ge(sem("probs_t"), XH_)
            pe.wait_ge(sem("pv_low"), NC)
            for k in range(B * MT):
                b, m = k // MT, k % MT
                pe.wait_ge(sem(f"values_in{k % 3}"), 16 * (k // 3 + 1))
                for h in range(XH_):
                    ins = pe.matmul(ps[0:B, 4 + h, :], spread[:, m, b, h, :], cache[:, k % 3, h * DC * P:(h + 1) * DC * P],
                                    start=k == 0, stop=k == B * MT - 1)
                ins.then_inc(sem("s_valued"), 1)
            pe.wait_ge(*after("os_rows", 1))
            for c in range(NC):
                ins = pe.transpose(ps[:, 2, c * B:(c + 1) * B], os_rows[0:B, c * P:(c + 1) * P], ident[0:B, 0:B])
            ins.then_inc(sem("os_turned"), 1)
            pe.wait_ge(*after("s_o_low", 1))

            gemm(g_o)
            residual_sums(1)
            pe.wait_ge(sem("mean"), 3)
            for c0, n, g_up, g_down in ffn:
                gemm(g_up, ready=(sem("norm_low"), NC, KS) if c0 == 0 else None,
                     after_first=(new_squares_summed(1, g_up), 4) if c0 == 0 else None)
                gemm(g_down, ready=(sem("h_low"), c0, KS))
            residual_sums(2)
            for k in range(4 * (TT + 1)):
                q, t = k // (TT + 1), k % (TT + 1)
                rows = P if t < TT else B
                pe.wait_ge(sem("x_new"), 2 * NC + 2 * q + 2)
                pe.wait_ge(sem("x_new_odd"), 2 * q + 2)
                if k >= 8:
                    pe.wait_ge(*after("y_copied", k - 7))
                for c in range(4):
                    ins = pe.transpose(ps[0:rows, k % 8, c * P:(c + 1) * P], xt_last[:, 4 * q + c, t * P:t * P + rows], ident[:])
                ins.then_inc(sem("y_turned"), 1)


def kernel(**inputs):
    import numpy as np
    import concourse.bacc as bacc
    from concourse import mybir as mb
    from concourse.bass_utils import run_bass_kernel_spmd

    x, xs, mem = (inputs[n].shape for n in ("x_prompt", "x_sample", "mem_prompt"))
    k, s = inputs["cache_mem_k"].shape, inputs["state_gdn_S"].shape
    lc, lh, gc = (inputs[n].shape for n in ("state_lru_conv", "state_lru_h", "state_gdn_conv"))
    b = x[0]
    outs = {
        "y_prompt": x, "y_sample": xs,
        "p_lru_conv": (lc[0], b) + lc[2:], "p_lru_h": (lh[0], b) + lh[2:], "p_gdn_conv": (gc[0], b) + gc[2:],
        "p_gdn_S": (s[0], b) + s[2:], "p_mem_k": (k[0], b) + k[2:], "p_mem_v": (k[0], b) + k[2:],
        "s_lru_conv": lc, "s_lru_h": lh, "s_gdn_conv": gc, "s_gdn_S": s,
    }
    nc = bacc.Bacc("TRN2", target_bir_lowering=False, num_devices=1)
    arrays = {f"in_{n}": np.ascontiguousarray(a) for n, a in inputs.items()}
    ins = {n: nc.dram_tensor(f"in_{n}", a.shape, mb.dt.from_np(a.dtype), kind="ExternalInput").ap()
           for n, a in ((n, arrays[f"in_{n}"]) for n in inputs)}
    results = {n: nc.dram_tensor(f"out_{n}", shape, mb.dt.float32, kind="ExternalOutput").ap() for n, shape in outs.items()}
    build(nc, ins, results)
    r = run_bass_kernel_spmd(nc, [arrays], core_ids=[0])
    return tuple(r.results[0][f"out_{n}"] for n in outs)
```
